# Optimizing a Trainium2 kernel written in Bass

```python
import jax, jax.numpy as jnp
from jax import lax
import numpy as np

D_MODEL = 1024
BATCH = 1
SEQ = 256
DEPTH = 2
DEC_BATCH = 1
DEC_SEQ = 32
PAST_LEN = 256

CHUNK = 64
Q_BLOCK = 128
MIX_WIDTH = D_MODEL
HG_HEADS = 4
HG_DIM = 128
HG_WIDTH = HG_HEADS * HG_DIM
MLA_HEADS = 4
NOPE_DIM = 128
ROPE_DIM = 64
V_DIM = 128
MLA_WIDTH = MLA_HEADS * V_DIM
Q_LORA = 384
KV_LORA = 256
ROPE_BASE = 10000.0
MLA_SCALE = (NOPE_DIM + ROPE_DIM) ** -0.5
D_FF = 2816
N_EXPERTS = 8
TOP_K = 2
D_EXPERT = 3584
N_DENSE = (DEPTH + 1) // 2
N_MOE = DEPTH // 2
EPS = 1e-6
IN_COLS = 4 * HG_WIDTH + Q_LORA + KV_LORA + ROPE_DIM
IN_SPLITS = (HG_WIDTH, 2 * HG_WIDTH, 3 * HG_WIDTH, 4 * HG_WIDTH,
             4 * HG_WIDTH + Q_LORA, 4 * HG_WIDTH + Q_LORA + KV_LORA)

kernel_name = "hgrn2_mla_hybrid_stream_step"

def _rms(x, w):
    xf = x.astype(jnp.float32)
    y = xf * lax.rsqrt(jnp.mean(xf * xf, axis=-1, keepdims=True) + EPS)
    return (y * w.astype(jnp.float32)).astype(x.dtype)

def _rope(x, pos):
    half = ROPE_DIM // 2
    inv_freq = ROPE_BASE ** (-jnp.arange(half, dtype=jnp.float32) / half)
    ang = pos.astype(jnp.float32)[:, None] * inv_freq[None, :]
    cos = jnp.cos(ang)[None, :, None, :]
    sin = jnp.sin(ang)[None, :, None, :]
    xf = x.astype(jnp.float32)
    x1, x2 = xf[..., :half], xf[..., half:]
    return jnp.concatenate([x1 * cos - x2 * sin, x2 * cos + x1 * sin], axis=-1).astype(x.dtype)

def _hgrn_chunk(q, k, v, logf, s0):
    L = q.shape[1]
    b = jnp.cumsum(logf, axis=1)
    o_inter = jnp.einsum('blhk,bhkv->blhv', q * jnp.exp(b), s0)
    causal = jnp.tril(jnp.ones((L, L), dtype=bool))[None, :, :, None, None]
    diff = b[:, :, None] - b[:, None, :]
    decay = jnp.where(causal, jnp.exp(jnp.minimum(diff, 0.0)), 0.0)
    scores = jnp.einsum('btshk,bshk->bhts', q[:, :, None] * decay, k)
    o_intra = jnp.einsum('bhts,bshv->bthv', scores, v)
    b_last = b[:, -1]
    k_dec = k * jnp.exp(b_last[:, None] - b)
    s_new = jnp.exp(b_last)[..., None] * s0 + jnp.einsum('blhk,blhv->bhkv', k_dec, v)
    return o_inter + o_intra, s_new

def _hgrn_scan(q, k, v, logf, s0):
    B, S = q.shape[:2]
    n = S // CHUNK

    def blocks(a):
        return jnp.swapaxes(a.reshape(B, n, CHUNK, *a.shape[2:]), 0, 1)

    def step(s, xs):
        o, s = _hgrn_chunk(xs[0], xs[1], xs[2], xs[3], s)
        return s, o

    s_final, o = lax.scan(step, s0, (blocks(q), blocks(k), blocks(v), blocks(logf)))
    return jnp.swapaxes(o, 0, 1).reshape(B, S, *o.shape[3:]), s_final

def _mla_attend(q_nope, q_pe, k_nope, k_pe, v, mask):
    s = (jnp.einsum('bqhd,bkhd->bhqk', q_nope, k_nope).astype(jnp.float32)
         + jnp.einsum('bqhr,bkr->bhqk', q_pe, k_pe).astype(jnp.float32)) * MLA_SCALE
    if mask is not None:
        s = jnp.where(mask[None, None], s, -1e30)
    p = jax.nn.softmax(s, axis=-1)
    return jnp.einsum('bhqk,bkhv->bqhv', p.astype(v.dtype), v)

def _mla_prompt(q_nope, q_pe, k_nope, k_pe, v):
    B, S = q_nope.shape[:2]
    kchunk = jnp.arange(S) // CHUNK

    def block(i):
        start = i * Q_BLOCK
        qn = lax.dynamic_slice_in_dim(q_nope, start, Q_BLOCK, axis=1)
        qp = lax.dynamic_slice_in_dim(q_pe, start, Q_BLOCK, axis=1)
        qchunk = (start + jnp.arange(Q_BLOCK)) // CHUNK
        mask = kchunk[None, :] <= qchunk[:, None]
        return _mla_attend(qn, qp, k_nope, k_pe, v, mask)

    o = lax.map(block, jnp.arange(S // Q_BLOCK))
    return jnp.swapaxes(o, 0, 1).reshape(B, S, MLA_HEADS, V_DIM)

def _token_mixers(h, pos, lb, hg_state, ckv_past, kpe_past, p, l):
    B, L, _ = h.shape
    f32 = jnp.float32
    proj = jnp.einsum('bld,dn->bln', h, p['w_in'][l])
    hq, hf, hi, hg, cq, ckv, kpe = jnp.split(proj, IN_SPLITS, axis=-1)
    heads = (B, L, HG_HEADS, HG_DIM)
    fl = hf.astype(f32)
    one_minus_f = (1.0 - lb) * jax.nn.sigmoid(-fl)
    logf = jnp.log1p(-one_minus_f).reshape(heads)
    k = one_minus_f.reshape(heads)
    q = jax.nn.silu(hq.astype(f32)).reshape(heads)
    v = hi.astype(f32).reshape(heads)
    if ckv_past is None:
        s0 = jnp.zeros((B, HG_HEADS, HG_DIM, HG_DIM), f32)
        o, s_new = _hgrn_scan(q, k, v, logf, s0)
    else:
        o, s_new = _hgrn_chunk(q, k, v, logf, hg_state.astype(f32))
    o = _rms(o, p['hg_onorm_w'][l]) * jax.nn.silu(hg.astype(f32)).reshape(heads)
    o_hg = o.reshape(B, L, HG_WIDTH).astype(h.dtype)
    cq = _rms(cq, p['mla_qa_norm_w'][l])
    qh = jnp.einsum('blr,rn->bln', cq, p['mla_wqb'][l]).reshape(B, L, MLA_HEADS, NOPE_DIM + ROPE_DIM)
    q_nope = _rms(qh[..., :NOPE_DIM], p['mla_qn_nope_w'][l])
    q_pe = _rope(_rms(qh[..., NOPE_DIM:], p['mla_qn_rope_w'][l]), pos)
    ckv = _rms(ckv, p['mla_kva_norm_w'][l])
    kpe = _rope(_rms(kpe[:, :, None, :], p['mla_kn_rope_w'][l]), pos)[:, :, 0, :]
    if ckv_past is None:
        ckv_all, kpe_all = ckv, kpe
    else:
        ckv_all = jnp.concatenate([ckv_past.astype(ckv.dtype), ckv], axis=1)
        kpe_all = jnp.concatenate([kpe_past.astype(kpe.dtype), kpe], axis=1)
    kv = jnp.einsum('bsr,rn->bsn', ckv_all, p['mla_wkvb'][l]).reshape(B, -1, MLA_HEADS, NOPE_DIM + V_DIM)
    k_nope = _rms(kv[..., :NOPE_DIM], p['mla_kn_nope_w'][l])
    v_mla = kv[..., NOPE_DIM:]
    if ckv_past is None:
        o_mla = _mla_prompt(q_nope, q_pe, k_nope, kpe_all, v_mla)
    else:
        o_mla = _mla_attend(q_nope, q_pe, k_nope, kpe_all, v_mla, None)
    o_mla = _rms(o_mla.reshape(B, L, MLA_WIDTH), p['mla_onorm_w'][l])
    mix = jnp.concatenate([o_hg, o_mla], axis=-1)
    y = jnp.einsum('bln,nd->bld', mix, p['w_o'][l])
    return y, s_new, ckv, kpe

def _swiglu(h, wg, wu, wd):
    a = jax.nn.silu(jnp.einsum('bld,df->blf', h, wg)) * jnp.einsum('bld,df->blf', h, wu)
    return jnp.einsum('blf,fd->bld', a, wd)

def _moe(h, router, wg, wu, wd):
    logits = jnp.einsum('bld,de->ble', h, router).astype(jnp.float32)
    top_v, top_i = lax.top_k(logits, TOP_K)
    gates = jax.nn.softmax(top_v, axis=-1)
    dense_gate = jnp.sum(jax.nn.one_hot(top_i, N_EXPERTS, dtype=jnp.float32) * gates[..., None], axis=-2)
    out = jnp.zeros_like(h)
    for e in range(N_EXPERTS):
        out = out + dense_gate[..., e:e + 1].astype(h.dtype) * _swiglu(h, wg[e], wu[e], wd[e])
    return out

def _trunk(x, c, pos, hg_state, ckv_past, kpe_past, p, lower):
    sc = jax.nn.silu(c)
    new_s, new_ckv, new_kpe = [], [], []
    for l in range(DEPTH):
        mod = jnp.einsum('bd,dn->bn', sc, p['ada_w'][l]) + p['ada_b'][l]
        sh1, sc1, g1, sh2, sc2, g2 = [m[:, None, :] for m in jnp.split(mod, 6, axis=-1)]
        h = _rms(x, p['norm1_w'][l]) * (1 + sc1) + sh1
        y, s_l, ckv_l, kpe_l = _token_mixers(
            h, pos, lower[l],
            None if hg_state is None else hg_state[l],
            None if ckv_past is None else ckv_past[l],
            None if kpe_past is None else kpe_past[l], p, l)
        x = x + g1 * y
        h = _rms(x, p['norm2_w'][l]) * (1 + sc2) + sh2
        j = l // 2
        if l % 2 == 0:
            f = _swiglu(h, p['ffn_w_gate'][j], p['ffn_w_up'][j], p['ffn_w_down'][j])
        else:
            f = _moe(h, p['moe_router'][j], p['moe_w_gate'][j], p['moe_w_up'][j], p['moe_w_down'][j])
        x = x + g2 * f
        new_s.append(s_l.astype(x.dtype))
        new_ckv.append(ckv_l)
        new_kpe.append(kpe_l)
    return x, jnp.stack(new_s), jnp.stack(new_ckv), jnp.stack(new_kpe)

def setup_inputs(seed: int = 0) -> dict:
    key = jax.random.key(seed)
    ks = iter(list(jax.random.split(key, 48)))
    D = D_MODEL

    def nrm(shape, scale):
        return scale * jax.random.normal(next(ks), shape, jnp.float32)

    def gain(shape):
        return 1.0 + 0.05 * jax.random.normal(next(ks), shape, jnp.float32)

    return {
        'x_prompt': nrm((BATCH, SEQ, D), 1.0),
        'x_sample': nrm((DEC_BATCH, DEC_SEQ, D), 1.0),
        'c_prompt': nrm((BATCH, D), 1.0),
        'c_sample': nrm((DEC_BATCH, D), 1.0),
        'state_hgrn': nrm((DEPTH, DEC_BATCH, HG_HEADS, HG_DIM, HG_DIM), 0.5),
        'cache_ckv': nrm((DEPTH, DEC_BATCH, PAST_LEN, KV_LORA), 1.0),
        'cache_kpe': nrm((DEPTH, DEC_BATCH, PAST_LEN, ROPE_DIM), 1.0),
        'ada_w': nrm((DEPTH, D, 6 * D), 0.5 * D ** -0.5),
        'ada_b': nrm((DEPTH, 6 * D), 0.02),
        'norm1_w': gain((DEPTH, D)),
        'norm2_w': gain((DEPTH, D)),
        'w_in': nrm((DEPTH, D, IN_COLS), D ** -0.5),
        'hg_lower_bounds': nrm((DEPTH, HG_WIDTH), 0.5),
        'hg_onorm_w': gain((DEPTH, HG_DIM)),
        'mla_qa_norm_w': gain((DEPTH, Q_LORA)),
        'mla_wqb': nrm((DEPTH, Q_LORA, MLA_HEADS * (NOPE_DIM + ROPE_DIM)), Q_LORA ** -0.5),
        'mla_kva_norm_w': gain((DEPTH, KV_LORA)),
        'mla_wkvb': nrm((DEPTH, KV_LORA, MLA_HEADS * (NOPE_DIM + V_DIM)), KV_LORA ** -0.5),
        'mla_qn_nope_w': gain((DEPTH, NOPE_DIM)),
        'mla_qn_rope_w': gain((DEPTH, ROPE_DIM)),
        'mla_kn_nope_w': gain((DEPTH, NOPE_DIM)),
        'mla_kn_rope_w': gain((DEPTH, ROPE_DIM)),
        'mla_onorm_w': gain((DEPTH, MLA_WIDTH)),
        'w_o': nrm((DEPTH, MIX_WIDTH, D), MIX_WIDTH ** -0.5),
        'ffn_w_gate': nrm((N_DENSE, D, D_FF), D ** -0.5),
        'ffn_w_up': nrm((N_DENSE, D, D_FF), D ** -0.5),
        'ffn_w_down': nrm((N_DENSE, D_FF, D), D_FF ** -0.5),
        'moe_router': nrm((N_MOE, D, N_EXPERTS), D ** -0.5),
        'moe_w_gate': nrm((N_MOE, N_EXPERTS, D, D_EXPERT), D ** -0.5),
        'moe_w_up': nrm((N_MOE, N_EXPERTS, D, D_EXPERT), D ** -0.5),
        'moe_w_down': nrm((N_MOE, N_EXPERTS, D_EXPERT, D), D_EXPERT ** -0.5),
    }

def reference(x_prompt, x_sample, c_prompt, c_sample, state_hgrn, cache_ckv, cache_kpe,
              ada_w, ada_b, norm1_w, norm2_w, w_in, hg_lower_bounds, hg_onorm_w,
              mla_qa_norm_w, mla_wqb, mla_kva_norm_w, mla_wkvb, mla_qn_nope_w, mla_qn_rope_w,
              mla_kn_nope_w, mla_kn_rope_w, mla_onorm_w, w_o,
              ffn_w_gate, ffn_w_up, ffn_w_down,
              moe_router, moe_w_gate, moe_w_up, moe_w_down):
    p = dict(ada_w=ada_w, ada_b=ada_b, norm1_w=norm1_w, norm2_w=norm2_w, w_in=w_in,
             hg_onorm_w=hg_onorm_w, mla_qa_norm_w=mla_qa_norm_w, mla_wqb=mla_wqb,
             mla_kva_norm_w=mla_kva_norm_w, mla_wkvb=mla_wkvb, mla_qn_nope_w=mla_qn_nope_w,
             mla_qn_rope_w=mla_qn_rope_w, mla_kn_nope_w=mla_kn_nope_w, mla_kn_rope_w=mla_kn_rope_w,
             mla_onorm_w=mla_onorm_w, w_o=w_o, ffn_w_gate=ffn_w_gate, ffn_w_up=ffn_w_up,
             ffn_w_down=ffn_w_down, moe_router=moe_router, moe_w_gate=moe_w_gate,
             moe_w_up=moe_w_up, moe_w_down=moe_w_down)
    lw = jax.nn.softmax(hg_lower_bounds.astype(jnp.float32), axis=0)
    lower = jnp.clip(jnp.cumsum(lw, axis=0) - lw[0], 0.0, 1.0)
    pos_p = jnp.arange(x_prompt.shape[1])
    pos_s = cache_ckv.shape[2] + jnp.arange(x_sample.shape[1])
    y_prompt, s_p, ckv_p, kpe_p = _trunk(x_prompt, c_prompt, pos_p, None, None, None, p, lower)
    y_sample, s_s, ckv_s, kpe_s = _trunk(x_sample, c_sample, pos_s, state_hgrn, cache_ckv, cache_kpe, p, lower)
    return (y_prompt, y_sample, s_p, ckv_p, kpe_p, s_s, ckv_s, kpe_s)


_drawn_inputs = setup_inputs


def setup_inputs(seed=0):
    import zlib

    import numpy as np

    out = dict(_drawn_inputs(seed))
    spreads = {}
    factors = {'state_hgrn': 5.189,
     'hg_onorm_w': 3.975,
     'mla_qa_norm_w': 4.241,
     'mla_qn_nope_w': 3.54,
     'mla_qn_rope_w': 21.911,
     'mla_kn_nope_w': 5.203,
     'mla_onorm_w': 3.186}
    for name, (base, spread) in spreads.items():
        noise = np.random.default_rng([zlib.crc32(name.encode()), seed]).standard_normal(out[name].shape)
        drawn = base * np.exp(spread * noise) if base else spread * noise
        out[name] = __import__('jax').numpy.asarray(drawn.astype(out[name].dtype))
    for name, factor in factors.items():
        out[name] = (out[name] * factor).astype(out[name].dtype)
    return out
```

```python
import numpy as np
import concourse.bass as bass
from concourse import mybir
from contextlib import ExitStack

F32 = mybir.dt.float32
I32 = mybir.dt.int32
ALU = mybir.AluOpType
ACT = mybir.ActivationFunctionType
AX = mybir.AxisListType

D, SEQ, DEC, PAST, DEPTH = 1024, 256, 32, 256, 2
T = SEQ + DEC
KD = D // 128
HEADS = 4
QL, KVL, ROPE = 384, 256, 64
SCALE = (128 + ROPE) ** -0.5
FF, FX, NX = 2816, 3584, 8
NF, NFX = FF // 128, FX // 128
EPS = 1e-6
KEYS = T + PAST
CH, SUB = 32, 4
NC_, NB_ = T // CH, CH // SUB
SLOTS_X = 128
ITEMS = 12
GRP = ((0, 0, SEQ), (1, SEQ, DEC))
TB = ((0, 128), (128, 128), (256, 32))
NSLOT, SLOTW = 7, 3072
ARENA = 16224
PF, PQ, PI, PC, PK, PCQ, PG, NP = 0, 4, 8, 12, 14, 15, 18, 22
VB, VN1, VN2, VON, VQA, VKV, VQN, VQR, VKN, VKR, VMO, VLB, NV = 0, 48, 56, 64, 65, 68, 70, 71, 72, 73, 74, 78, 82
CI, CO, CO64, CROT, CCOS, CSIN, CCM, CRS, CU, CIO, CLT, CMQ, CMK, CIT, CEX, NCST = np.cumsum(
    [0, 128, 128, 128, 128, T, T, 128, HEADS * T, 128, 128, 64, 128, 128, ITEMS, NX]).tolist()


def constants():
    c = np.zeros((128, NCST), np.float32)
    p = np.arange(128)
    c[:, CI:CI + 128] = np.eye(128)
    c[:, CO:CO + 128] = 1.0
    c[:, CO64:CO64 + 128] = p[:, None] // 64 == p[None, :] // 64
    for h in (0, 64):
        for m in range(32):
            c[h + 32 + m, CROT + h + m] = -1.0
            c[h + m, CROT + h + 32 + m] = 1.0
    inv = (10000.0 ** (-np.arange(32, dtype=np.float32) / 32)).astype(np.float32)
    pos = np.concatenate([np.arange(SEQ), PAST + np.arange(DEC)]).astype(np.float32)
    ang = (pos[None, :] * inv[p % 32][:, None]).astype(np.float32)
    c[:, CCOS:CCOS + T] = np.cos(ang.astype(np.float64))
    c[:, CSIN:CSIN + T] = np.sin(ang.astype(np.float64))
    s, t = p[:, None], p[None, :]
    c[:, CCM:CCM + 128] = (s // CH == t // CH) & (s <= t)
    c[:, CRS:CRS + HEADS * T] = np.arange(HEADS * T)[None, :] % CH != 0
    c[:, CU:CU + 128] = s < t
    c[:, CIO:CIO + 128] = t
    e = np.arange(NX)
    c[:, CLT:CLT + 64] = (e[None, :] < e[:, None]).reshape(1, 64)
    c[0, CMQ:CMQ + 128] = p < 64
    c[0, CMK:CMK + 128] = np.where(p < 64, 0.0, -1e30)
    c[:, CIT:CIT + ITEMS] = np.arange(ITEMS)
    c[:, CEX:CEX + NX] = e
    return c


STREAM = [(n, l, k, w) for l in range(DEPTH) for n, k, w in
          [("ada", 16, 3072), ("win", 11, 2048), ("wqb", 1, 2304), ("wkvb", 1, 2048), ("wo", 4, 2048)]
          + [("up", NF, 2048), ("down", KD, FF)] * (l == 0)]
START = {}
_at = 0
for _n, _l, _k, _w in STREAM:
    START[_n, _l] = _at
    _at += _k
START["moe", 1] = _at


def slot_of(at):
    return at % NSLOT


def fills(at):
    return 16 * (at // NSLOT + 1)


def psum_plan():
    plan, count, at = {}, [0] * 8, [0]

    def use(name, bank=None):
        if bank is None:
            bank = at[0] % 8
            at[0] += 1
        plan[name] = (bank, count[bank])
        count[bank] += 1

    for k in range(KD):
        use(("x", k))
    for l in range(DEPTH):
        for j in range(16):
            use(("mod", l, j))
            if j:
                use(("modT", l, j - 1))
        use(("modT", l, 15))
        use(("ss", l, "n1"))
        for j in range(NP):
            use(("p", l, j))
        for s in ("ckv", "kpe", "cq"):
            use(("ss", l, s))
        use(("rotk", l))
        for h in range(HEADS):
            use(("vt", l, h))
        for j in range(3):
            use(("cache", l, j))
        for h in range(HEADS):
            use(("kd", l, h))
        for h in range(HEADS):
            use(("sc", l, h))
        for h in range(HEADS):
            use(("o", l, h), h)
        for c in range(NC_):
            use(("u", l, c), 4 + c % 4)
        for h in range(HEADS):
            use(("ss", l, "o%d" % h), 4 + h)
        for j in range(6):
            use(("q", l, j))
            if j:
                use(("ss", l, "q%d" % (j - 1)))
        use(("ss", l, "q5"))
        for j in range(2):
            use(("rotq", l, j))
        for j in range(8):
            use(("k", l, j))
            if j:
                use(("ss", l, "k%d" % (j - 1)))
        use(("ss", l, "k7"))
        for b in range(5):
            use(("v", l, b))
        for g in range(3):
            use(("ckvo", l, g))
        for h in range(HEADS):
            use(("oT", l, h), h % 2)
            for b in range(3):
                use(("s", l, h, b), 2 + (3 * h + b) % 3)
                use(("pT", l, h, b), 5 + (3 * h + b) % 3)
        use(("ss", l, "om"))
        for k in range(KD):
            use(("wo", l, k))
        use(("ss", l, "n2"))
        if l == 0:
            for k in range(KD):
                use(("down", k))
        else:
            for g in range(3):
                for f in range(2):
                    use(("ht", g, f))
            use(("logits",))
            use(("rank",))
    for g in range(3):
        for f in range(2):
            use(("y", g, f))
    return plan, count


def build(nc, consts, vecs, cond, x_in, state_in, cache_in, w_ada, w_win, w_wqb, w_wkvb, w_wo,
          w_up, w_down, w_router, w_moe, y_out, s_out, kv_out):
    PLAN, _ = psum_plan()
    ctx = ExitStack()
    with ctx:
        def sb(name, cols, dt=F32):
            return ctx.enter_context(nc.sbuf_tensor(name, [128, cols], dt))

        sems = {}

        def sem(name):
            if name not in sems:
                sems[name] = ctx.enter_context(nc.semaphore(name))
            return sems[name]

        ring = sb("ring", NSLOT * SLOTW)
        cst = sb("cst", NCST)
        vec = sb("vec", DEPTH * NV)
        xT = sb("xT", KD * T)
        hT = sb("hT", KD * T)
        arena = sb("arena", ARENA)
        misc = sb("misc", 580)

        arena_at = [0]

        def cut(cols, at=None):
            if at is None:
                at = arena_at[0]
                arena_at[0] += cols
            assert at + cols <= ARENA, at + cols
            return arena[:, at:at + cols]

        def tiles(ap, n):
            return ap.rearrange("p (n t) -> p n t", n=n)

        proj_f = cut(NP * T)
        proj = tiles(proj_f, NP)
        kf, qf = proj_f[:, PF * T:(PF + 4) * T], proj_f[:, PQ * T:(PQ + 4) * T]
        ckv_all = tiles(cut(2 * KEYS), 2)
        kpe_all = cut(KEYS)
        qpe = tiles(cut(2 * T), 2)
        bcum = cut(HEADS * T)
        tmp = cut(HEADS * T)
        qt_f = cut(HEADS * T)
        tok0 = arena_at[0]
        kd_tok = tiles(cut(3 * 512), 3)
        v_tok = tiles(cut(3 * 512), 3)
        sq4 = tiles(cut(4 * T), 4)
        kn = tiles(cut(HEADS * KEYS, 0), HEADS)
        vals = tiles(cut(5 * 512, tok0), 5)
        qn = tiles(qt_f, HEADS)
        sT = tiles(tmp, HEADS)
        qt = tiles(qt_f, HEADS)
        sq8_f = cut(KD * T, 0)
        x_tok = tiles(cut(3 * D, 0), 3)
        aT = tiles(cut(NF * T, 0), NF)
        sig_up = tiles(cut(2 * T, NF * T), 2)
        h_tok = tiles(cut(3 * D, KD * T), 3)
        hgT = tiles(cut(D, KD * T + 3 * D), KD)
        ysb = cut(D, KD * T + 4 * D)
        acc = tiles(cut(KD * T, KD * T + 5 * D), KD)
        m0 = 2 * KD * T + 5 * D
        aX = tiles(cut(7 * 128, m0), 7)
        sgX = tiles(cut(4 * 128, m0 + 896), 4)
        pick = tiles(cut(3 * 128, m0 + 1408), 3)
        pickg = tiles(cut(3 * 128, m0 + 1792), 3)
        gT = cut(T, m0 + 2176)
        cmp8 = cut(3 * 64, m0 + 2500)
        cmp8b = cut(3 * 64, m0 + 2700)
        cmpi = cut(ITEMS * NX, m0 + 2900)
        cmpi2 = cut(ITEMS * NX, m0 + 3000)
        router = tiles(cut(KD * NX, m0 + 3100), KD)
        rt = cut(400, m0 + 3200)
        y_tok = tiles(cut(3 * D, KD * T), 3)

        rot_tmp = sb("rot_tmp", T)
        sq1 = tiles(sb("sq1", 2 * T)[:, :], 2)
        rstd = tiles(sb("rstd", 2 * T)[:, :], 2)
        sg1 = tiles(sb("sg1", 2 * T)[:, :], 2)
        states = tiles(sb("states", 2 * 512)[:, :], 2)
        s_smp = sb("s_smp", 512)
        s_new = sb("s_new", 512)
        cache_tok = tiles(sb("cache_tok", 2 * 384)[:, :], 2)
        probs = tiles(sb("probs", 2 * T)[:, :], 2)
        pT = tiles(sb("pT", 2 * T)[:, :], 2)
        kv_tok = tiles(sb("kv_tok", 2 * 384)[:, :], 2)
        ref = misc[:, 288:288 + HEADS * T // SUB]

        mods = misc[:, 0:96].rearrange("p (f g) -> p f g", g=2)
        gain = misc[:, 96:128].rearrange("p (n k g) -> p n k g", n=2, g=2)
        condT = misc[:, 128:144].rearrange("p (k g) -> p k g", g=2)
        scond = sb("scond", KD * 32)[:, :].rearrange("p (k g) -> p k g", g=32)
        eps = misc[:, 160:161]
        lbw = misc[:, 164:184]
        oml = misc[:, 184:192].rearrange("p (l h) -> p l h", l=2)
        rowmax = misc[:, 192:216]
        negmax = misc[:, 216:240]
        rowsum = misc[:, 240:264]
        rinv = misc[:, 264:288]
        ids = ctx.enter_context(nc.sbuf_tensor("ids", [128, 16], I32))

        banks = [ctx.enter_context(nc.psum_tensor("bank%d" % b, [128, 512], F32)) for b in range(8)]
        bank_full = [sem("bank_full%d" % b) for b in range(8)]
        bank_free = [sem("bank_free%d" % b) for b in range(8)]
        slot_full = [sem("slot_full%d" % s) for s in range(NSLOT)]

        ident, ones, ones64 = cst[:, CI:CI + 128], cst[:, CO:CO + 128], cst[:, CO64:CO64 + 128]
        rot, cos, sin = cst[:, CROT:CROT + 128], cst[:, CCOS:CCOS + T], cst[:, CSIN:CSIN + T]

        def V(l, col, n=1):
            return vec[:, l * NV + col:l * NV + col + n]

        def ps(name):
            return banks[PLAN[name][0]]

        def take(eng, name):
            b, n = PLAN[name]
            eng.wait_ge(bank_full[b], n + 1)

        def done(ins, name):
            ins.then_inc(bank_free[PLAN[name][0]], 1)

        def await_done(eng, name):
            b, n = PLAN[name]
            eng.wait_ge(bank_free[b], n + 1)

        rms_order = []
        for l in range(DEPTH):
            rms_order += [(l, s) for s in ["n1", "ckv", "kpe", "cq"] + ["o%d" % h for h in range(4)]
                          + ["q%d" % j for j in range(6)] + ["k%d" % j for j in range(8)] + ["om", "n2"]]
        RMS = {n: i for i, n in enumerate(rms_order)}
        squares_ready, rstd_ready, normed = sem("squares_ready"), sem("rstd_ready"), sem("normed")
        def used_up(at):
            name, l, first = max(((n, l, f) for (n, l), f in START.items() if f <= at), key=lambda x: x[2])
            j = at - first
            if name == "up":
                return sem("gu_full"), j + 1
            last = {"ada": ("mod", l, j), "win": ("p", l, 2 * j + 1), "wqb": ("q", l, 5), "wkvb": ("v", l, 4),
                    "wo": ("wo", l, 2 * j + 1), "down": ("down", j)}[name]
            b, n = PLAN[last]
            return bank_full[b], n + 1

        QB = ((0, 128, 0, 128), (0, 256, 128, 128), (SEQ, T, SEQ, DEC))
        VBLK = ((0, 128), (128, 128), (256, 32), (288, 128), (416, 128))
        BLK_OF = ((0,), (0, 1), (2, 3, 4))
        block = ctx.enter_context(nc.Block())

        @block.sync
        def _(sp):
            sp.dma_start(cst[:, :], consts).then_inc(sem("consts_loaded"), 16)
            sp.dma_start(misc[:, 128:144], cond).then_inc(sem("cond_loaded"), 16)
            sp.dma_start(vec[:, :], vecs).then_inc(sem("vecs_loaded"), 16)
            for g, (t0, n) in enumerate(TB):
                sp.dma_start(x_tok[0:n, g, :], x_in[t0:t0 + n, :]).then_inc(sem("x_loaded"), 16)

            def slab(at, src, width):
                if at >= NSLOT:
                    sp.wait_ge(*used_up(at - NSLOT))
                sp.dma_start(ring[:, slot_of(at) * SLOTW:slot_of(at) * SLOTW + width], src
                             ).then_inc(slot_full[slot_of(at)], 16)

            src = {"ada": w_ada, "win": w_win, "wqb": w_wqb, "wkvb": w_wkvb, "wo": w_wo,
                   "up": w_up, "down": w_down}
            for name, l, k, w in STREAM:
                first = START[name, l]
                for j in range(k):
                    a = src[name][l, j] if name not in ("up", "down") else src[name][j]
                    slab(first + j, a, w)
            sp.wait_ge(*used_up(START["moe", 1] - 1))
            sp.sem_inc(sem("slots_free"), NSLOT)
            sp.wait_ge(sem("ids_ready"), 1)
            n_items = sp.value_load(ids[0:1, ITEMS:ITEMS + 1], min_val=NX, max_val=ITEMS)
            first = START["moe", 1]
            with sp.Fori(0, n_items) as i:
                e = sp.value_load(ids[0:1, bass.ds(i, 1)], min_val=0, max_val=NX - 1)
                with sp.Fori(0, NFX // 7) as q:
                    for j in range(7):
                        sp.wait_ge(sem("slots_free"), i * NFX + q * 7 + (j + 1))
                        s = slot_of(first + j)
                        sp.dma_start(ring[:, s * SLOTW:(s + 1) * SLOTW],
                                     w_moe[bass.ds(e * NFX + q * 7 + j, 1)].rearrange("a p n -> (a p) n")
                                     ).then_inc(slot_full[s], 16)

        @block.tensor
        def _(pe):
            mm = nc.tensor.matmul

            def use(name):
                b, n = PLAN[name]
                if n:
                    pe.wait_ge(bank_free[b], n)
                return banks[b]

            def full(ins, name):
                ins.then_inc(bank_full[PLAN[name][0]], 1)

            def slab(at, width):
                pe.wait_ge(slot_full[slot_of(at)], fills(at))
                return ring[:, slot_of(at) * SLOTW:slot_of(at) * SLOTW + width]

            def sum_squares(l, name, src, mat=ones):
                o = use(("ss", l, name))
                pe.wait_ge(squares_ready, RMS[l, name] + 1)
                for k, a in enumerate(src):
                    last = mm(o[:, 0:a.shape[1]], mat, a, start=k == 0, stop=k == len(src) - 1)
                full(last, ("ss", l, name))

            pe.wait_ge(sem("consts_loaded"), 16)
            pe.wait_ge(sem("x_loaded"), 48)
            for k in range(KD):
                o = use(("x", k))
                for g, (t0, n) in enumerate(TB):
                    last = nc.tensor.transpose(o[:, t0:t0 + n], x_tok[0:n, g, 128 * k:128 * k + 128], ident[0:n, 0:n])
                full(last, ("x", k))
            pe.wait_ge(sem("cond_silu"), 1)
            for l in range(DEPTH):
                def turn_mod(j):
                    o = use(("modT", l, j))
                    pe.wait_ge(sem("modrow_ready"), 16 * l + j + 1)
                    for f in range(3):
                        last = nc.tensor.transpose(o[:, 128 * f:128 * f + 128], kv_tok[:, j % 2, 128 * f:128 * f + 128], ident)
                    full(last, ("modT", l, j))

                for j in range(16):
                    o = use(("mod", l, j))
                    w = slab(START["ada", l] + j, 3072).rearrange("p (k n) -> p k n", k=KD)
                    for k in range(KD):
                        r = 32 * (k % 4)
                        last = mm(o[r:r + 32, 0:384], scond[:, k, :], w[:, k], start=k < 4, stop=k >= 4)
                    full(last, ("mod", l, j))
                    if j:
                        turn_mod(j - 1)
                turn_mod(15)
                sum_squares(l, "n1", [sq8_f[:, k * T:(k + 1) * T] for k in range(KD)])
                pe.wait_ge(sem("h1_ready"), l + 1)
                for j in range(NP):
                    o = use(("p", l, j))
                    w = slab(START["win", l] + j // 2, 2048).rearrange("p (f k n) -> p f k n", f=2, k=KD)
                    for k in range(KD):
                        last = mm(o[:, 0:T], w[:, j % 2, k], hT[:, k * T:(k + 1) * T], start=k == 0, stop=k == KD - 1)
                    full(last, ("p", l, j))
                sum_squares(l, "ckv", [sq4[:, k] for k in range(2)])
                sum_squares(l, "kpe", [sq1[:, 0]], ones64)
                sum_squares(l, "cq", [sq4[:, k] for k in range(3)])
                o = use(("rotk", l))
                pe.wait_ge(normed, RMS[l, "kpe"] + 1)
                full(mm(o[:, 0:T], rot, kpe_all[:, 0:T], start=True, stop=True), ("rotk", l))
                for h in range(HEADS):
                    o = use(("vt", l, h))
                    await_done(pe, ("p", l, PI + h))
                    for g, (t0, n) in enumerate(TB):
                        last = nc.tensor.transpose(o[0:n, 128 * g:128 * g + 128], proj[:, PI + h, t0:t0 + n], ident)
                    full(last, ("vt", l, h))
                pe.wait_ge(sem("cache_loaded"), 48 * (l + 1))
                for j in range(3):
                    o = use(("cache", l, j))
                    for b in range(2):
                        last = nc.tensor.transpose(o[:, 128 * b:128 * b + 128], cache_tok[:, b, 128 * j:128 * j + 128], ident)
                    full(last, ("cache", l, j))
                pe.wait_ge(sem("kd_ready"), l + 1)
                for h in range(HEADS):
                    o = use(("kd", l, h))
                    for g, (t0, n) in enumerate(TB):
                        last = nc.tensor.transpose(o[0:n, 128 * g:128 * g + 128],
                                                   tmp[:, h * T + t0:h * T + t0 + n], ident)
                    full(last, ("kd", l, h))
                for h in range(HEADS):
                    o = use(("sc", l, h))
                    pe.wait_ge(sem("kt_ready"), 4 * l + h + 1)
                    for g, (t0, n) in enumerate(TB):
                        for b in range(NB_):
                            dst = o[0:n, t0:t0 + n].rearrange("p (c b s) -> p c b s", b=NB_, s=SUB)[:, :, b, :]
                            q = qt[:, h, t0:t0 + n].rearrange("p (c b s) -> p c b s", b=NB_, s=SUB)[:, :, b, :]
                            last = mm(dst, hT[:, b * T + t0:b * T + t0 + n], q, start=True, stop=True)
                    full(last, ("sc", l, h))
                for h in range(HEADS):
                    o = use(("o", l, h))
                    await_done(pe, ("sc", l, h))
                    if h == 0:
                        pe.wait_ge(sem("v_tok_ready"), 8 * (l + 1))
                    for g, (t0, n) in enumerate(TB):
                        mm(o[:, t0:t0 + n], v_tok[0:n, g, 128 * h:128 * h + 128], sT[0:n, h, t0:t0 + n],
                           start=g == 0, stop=False, skip_group_check=True)
                pe.wait_ge(sem("kd_tok_ready"), 8 * (l + 1))
                pe.wait_ge(sem("qe_ready"), l + 1)

                def inter(c):
                    if c < NC_ - 1:
                        pe.wait_ge(sem("state_ready"), 8 * l + c)
                        s = states[:, c % 2]
                    else:
                        pe.wait_ge(sem("state_loaded"), 16 * (l + 1))
                        s = s_smp
                    for h in range(HEADS):
                        last = mm(banks[h][:, CH * c:CH * c + CH], s[:, 128 * h:128 * h + 128],
                                  qf[:, h * T + CH * c:h * T + CH * c + CH],
                                  start=False, stop=True, skip_group_check=True)
                        if c == NC_ - 1:
                            full(last, ("o", l, h))
                    if c < NC_ - 1:
                        last.then_inc(sem("state_used"), 1)

                for c in range(NC_):
                    o = use(("u", l, c))
                    g, r = divmod(CH * c, 128)
                    for h in range(HEADS):
                        last = mm(o[:, 128 * h:128 * h + 128], kd_tok[r:r + CH, g, 128 * h:128 * h + 128],
                                  v_tok[r:r + CH, g, 128 * h:128 * h + 128], start=True, stop=True)
                    full(last, ("u", l, c))
                    if c >= 2:
                        inter(c - 1)
                inter(NC_ - 1)
                for h in range(HEADS):
                    sum_squares(l, "o%d" % h, [sq1[:, RMS[l, "o%d" % h] % 2]])
                wq = slab(START["wqb", l], 2304).rearrange("p (k n) -> p k n", k=3)
                pe.wait_ge(normed, RMS[l, "cq"] + 1)
                for j in range(6):
                    o = use(("q", l, j))
                    for k in range(3):
                        last = mm(o[:, 0:T], wq[:, k, 128 * j:128 * j + 128], proj[:, PCQ + k, :],
                                  start=k == 0, stop=k == 2)
                    full(last, ("q", l, j))
                    if j:
                        sum_squares(l, "q%d" % (j - 1), [sq1[:, RMS[l, "q%d" % (j - 1)] % 2]],
                                    ones64 if j - 1 >= 4 else ones)
                sum_squares(l, "q5", [sq1[:, RMS[l, "q5"] % 2]], ones64)
                for j in range(2):
                    o = use(("rotq", l, j))
                    pe.wait_ge(normed, RMS[l, "q%d" % (4 + j)] + 1)
                    full(mm(o[:, 0:T], rot, qpe[:, j, :], start=True, stop=True), ("rotq", l, j))
                wk = slab(START["wkvb", l], 2048).rearrange("p (k n) -> p k n", k=2)
                pe.wait_ge(sem("ckv_all_ready"), 2 * (l + 1))
                for j in range(8):
                    h, (t0, n) = j // 2, ((0, T), (T, PAST))[j % 2]
                    o = use(("k", l, j))
                    for k in range(2):
                        last = mm(o[:, 0:n], wk[:, k, 128 * h:128 * h + 128], ckv_all[:, k, t0:t0 + n],
                                  start=k == 0, stop=k == 1)
                    full(last, ("k", l, j))
                    if j:
                        sum_squares(l, "k%d" % (j - 1), [sq1[:, RMS[l, "k%d" % (j - 1)] % 2, 0:(T, PAST)[(j - 1) % 2]]])
                sum_squares(l, "k7", [sq1[:, RMS[l, "k7"] % 2, 0:PAST]])
                for b, (t0, n) in enumerate(VBLK):
                    o = use(("v", l, b))
                    for k in range(2):
                        last = mm(o[0:n, :], ckv_all[:, k, t0:t0 + n], wk[:, k, 512:1024], start=k == 0, stop=k == 1)
                    full(last, ("v", l, b))
                pe.wait_ge(sem("kpe_ready"), l + 1)
                for g, (t0, n) in enumerate(TB):
                    o = use(("ckvo", l, g))
                    for k in range(2):
                        nc.tensor.transpose(o[0:n, 128 * k:128 * k + 128], ckv_all[:, k, t0:t0 + n], ident)
                    full(nc.tensor.transpose(o[0:n, 256:384], kpe_all[:, t0:t0 + n], ident), ("ckvo", l, g))
                pe.wait_ge(sem("qpe_ready"), 2 * (l + 1))
                pe.wait_ge(normed, RMS[l, "k7"] + 1)
                pe.wait_ge(sem("vals_ready"), 5 * (l + 1))

                def scores(h, b):
                    k0, nk, q0, nq = QB[b]
                    o = use(("s", l, h, b))
                    r = 64 * (h % 2)
                    mm(o[0:nq, 0:nk], qn[:, h, q0:q0 + nq], kn[:, h, k0:k0 + nk], start=True, stop=False)
                    if b < 2:
                        mm(o[0:nq, nk - 128:nk], cst[0:1, CMQ:CMQ + 128], cst[0:1, CMK:CMK + 128],
                           start=False, stop=False, skip_group_check=True)
                    last = mm(o[0:nq, 0:nk], qpe[r:r + 64, h // 2, q0:q0 + nq], kpe_all[r:r + 64, k0:k0 + nk],
                              start=False, stop=True)
                    full(last, ("s", l, h, b))

                def mix(h, b):
                    k0, nk, q0, nq = QB[b]
                    i = 3 * h + b
                    o = use(("pT", l, h, b))
                    pe.wait_ge(sem("probs_ready"), 12 * l + i + 1)
                    for n_, kb in enumerate(BLK_OF[b]):
                        t0, n = VBLK[kb]
                        last = nc.tensor.transpose(o[0:n, nq * n_:nq * n_ + nq], probs[0:nq, i % 2, t0 - k0:t0 - k0 + n],
                                                   ident[0:nq, 0:nq])
                    full(last, ("pT", l, h, b))

                def weigh(h, b):
                    k0, nk, q0, nq = QB[b]
                    i = 3 * h + b
                    o = use(("oT", l, h)) if b == 0 else ps(("oT", l, h))
                    pe.wait_ge(sem("pT_ready"), 12 * l + i + 1)
                    for n_, kb in enumerate(BLK_OF[b]):
                        t0, n = VBLK[kb]
                        last = mm(o[:, q0:q0 + nq], vals[0:n, kb, 128 * h:128 * h + 128],
                                  pT[0:n, i % 2, nq * n_:nq * n_ + nq],
                                  start=n_ == 0, stop=n_ == len(BLK_OF[b]) - 1)
                    if b == 2:
                        full(last, ("oT", l, h))

                todo = [(h, b) for h in range(HEADS) for b in range(3)]
                for i in range(14):
                    if i < 12:
                        scores(*todo[i])
                    if 1 <= i < 13:
                        mix(*todo[i - 1])
                    if i >= 2:
                        weigh(*todo[i - 2])
                sum_squares(l, "om", [sq4[:, k] for k in range(4)])
                pe.wait_ge(sem("mix_ready"), 5 * (l + 1))
                for k in range(KD):
                    o = use(("wo", l, k))
                    w = slab(START["wo", l] + k // 2, 2048).rearrange("p (f k n) -> p f k n", f=2, k=KD)
                    for j in range(8):
                        m = proj[:, (PG + j) if j < 4 else (PI + j - 4), :]
                        last = mm(o[:, 0:T], w[:, k % 2, j], m, start=j == 0, stop=j == 7)
                    full(last, ("wo", l, k))
                sum_squares(l, "n2", [sq8_f[:, k * T:(k + 1) * T] for k in range(KD)])
                pe.wait_ge(sem("h2_ready"), l + 1)
                if l == 0:
                    for b in range(8):
                        n = min(n for nm, (bb, n) in PLAN.items() if bb == b and (nm[0] == "down" or nm[1:2] == (1,)))
                        pe.wait_ge(bank_free[b], n)

                    def up(at, q, j):
                        s = slot_of(at + j)
                        pe.wait_ge(sem("gu_read"), q * 7 + (j + 1 if j < 3 else j))
                        pe.wait_ge(slot_full[s], q * 16 + fills(at + j))
                        w = ring[:, s * SLOTW:s * SLOTW + 2048].rearrange("p (h k n) -> p h k n", h=2, k=KD)
                        for u in range(2):
                            for k in range(KD):
                                last = mm(banks[2 * (j % 4) + u][:, 0:T], w[:, u, k], hT[:, k * T:(k + 1) * T],
                                          start=k == 0, stop=k == KD - 1)
                        last.then_inc(sem("gu_full"), 1)

                    with pe.Fori(0, 3) as q:
                        for j in range(7):
                            up(START["up", 0], q, j)
                    up(START["up", 0], 3, 0)
                    pe.wait_ge(sem("gu_read"), NF + 3)
                    for k in range(KD):
                        o = use(("down", k))
                        w = slab(START["down", 0] + k, FF).rearrange("p (f n) -> p f n", f=NF)
                        for f in range(NF):
                            last = mm(o[:, 0:T], w[:, f], aT[:, f], start=f == 0, stop=f == NF - 1)
                        full(last, ("down", k))
            for g, (t0, n) in enumerate(TB):
                for f in range(2):
                    o = use(("ht", g, f))
                    for k in range(4):
                        last = nc.tensor.transpose(o[0:n, 128 * k:128 * k + 128],
                                                   hT[:, (4 * f + k) * T + t0:(4 * f + k) * T + t0 + n], ident)
                    full(last, ("ht", g, f))
            o = use(("logits",))
            pe.wait_ge(sem("router_loaded"), 16)
            for g, (t0, n) in enumerate(TB):
                for k in range(KD):
                    last = mm(o[0:n, NX * g:NX * g + NX], hT[:, k * T + t0:k * T + t0 + n], router[:, k],
                              start=k == 0, stop=k == KD - 1)
            full(last, ("logits",))
            o = use(("rank",))
            pe.wait_ge(sem("chosen_ready"), 1)
            chosen = rt[:, 24:48].rearrange("p (g e) -> p g e", g=3)
            for g in range(3):
                for b in range(g + 1):
                    mm(o[:, NX * g:NX * g + NX], cst[:, CU:CU + 128] if b == g else ones, chosen[:, b],
                       start=b == 0, stop=b == g)
            for b in range(3):
                last = mm(o[:, 24:32], ones, chosen[:, b], start=b == 0, stop=b == 2)
            full(last, ("rank",))
            for b in range(8):
                n = max(n for nm, (bb, n) in PLAN.items() if bb == b and nm[0] != "y")
                pe.wait_ge(bank_free[b], n + 1)
            pe.wait_ge(sem("ids_ready"), 1)
            n_items = pe.value_load(ids[0:1, ITEMS:ITEMS + 1], min_val=NX, max_val=ITEMS)
            at = START["moe", 1]
            with pe.Fori(0, n_items) as i:
                pe.wait_ge(sem("pick_ready"), i + 1)
                pe.wait_ge(sem("scatter_read"), i * KD + KD)
                for k in range(KD):
                    for g, (t0, n) in enumerate(TB):
                        last = mm(banks[6 + k // 4][:, 128 * (k % 4):128 * (k % 4) + 128],
                                  h_tok[0:n, g, 128 * k:128 * k + 128], pick[0:n, g, :], start=g == 0, stop=g == 2)
                    if k % 4 == 3:
                        last.then_inc(sem("gathered"), 1)
                pe.wait_ge(sem("hg_lo_ready"), i + 1)
                pe.wait_ge(sem("hg_hi_ready"), i + 1)
                for g, (t0, n) in enumerate(TB):
                    last = nc.tensor.transpose(banks[6][:, t0:t0 + n], pickg[0:n, g, :], ident[0:n, 0:n])
                last.then_inc(sem("gates_turned"), 1)

                def up(j, q):
                    s = slot_of(at + j)
                    pe.wait_ge(slot_full[s], i * 64 + q * 16 + fills(at + j))
                    pe.wait_ge(sem("gu_read"), i * NFX + q * 7 + (NF + (j + 1 if j < 3 else j)))
                    w = ring[:, s * SLOTW:s * SLOTW + 2048].rearrange("p (h k n) -> p h k n", h=2, k=KD)
                    for u in range(2):
                        for k in range(KD):
                            last = mm(banks[j % 4][:, 128 * u:128 * u + 128], w[:, u, k], hgT[:, k, :],
                                      start=k == 0, stop=k == KD - 1)
                    last.then_inc(sem("gu_full"), 1)

                def down(j, q, first=False, last_=False):
                    s = slot_of(at + j)
                    pe.wait_ge(sem("gu_read"), i * NFX + q * 7 + (NF + j + 4))
                    for u in range(2):
                        last = mm(banks[4 + u][:, :], aX[:, j, :], ring[:, s * SLOTW + 2048 + 512 * u:s * SLOTW + 2560 + 512 * u],
                           start=first, stop=last_, skip_group_check=True)
                    last.then_inc(sem("slots_free"), 1)

                for j in range(7):
                    up(j, 0)
                    if j:
                        down(j - 1, 0, first=j == 1)
                with pe.Fori(1, NFX // 7) as q:
                    for j in range(7):
                        up(j, q)
                        down(j - 1, q) if j else down(6, q - 1)
                down(6, NFX // 7 - 1, last_=True)
                pe.wait_ge(sem("y_lo_ready"), i + 1)
                pe.wait_ge(sem("y_hi_ready"), i + 1)
                pe.wait_ge(sem("gates_ready"), i + 1)
                for k in range(KD):
                    if k >= 2:
                        pe.wait_ge(sem("scatter_read"), i * KD + (KD + k - 1))
                    mm(banks[6 + k % 2][:, 0:T], ysb[:, 128 * k:128 * k + 128], gT, start=True, stop=True
                       ).then_inc(sem("scattered"), 1)
            pe.wait_ge(sem("y_final"), KD)
            for g, (t0, n) in enumerate(TB):
                for f in range(2):
                    o = use(("y", g, f))
                    for k in range(4):
                        last = nc.tensor.transpose(o[0:n, 128 * k:128 * k + 128],
                                                   xT[:, (4 * f + k) * T + t0:(4 * f + k) * T + t0 + n], ident)
                    full(last, ("y", g, f))

        @block.scalar
        def _(act):
            A = nc.scalar.activation
            own = [0]

            def link(ins):
                own[0] += 1
                ins.then_inc(sem("scalar_step"), 1)
                act.wait_ge(sem("scalar_step"), own[0])

            def finish_norm(l, name, n, cols=T):
                r = RMS[l, name]
                dst = rstd[:, r % 2, 0:cols]
                if r >= 2:
                    act.wait_ge(normed, r - 1)
                take(act, ("ss", l, name))
                done(A(dst, ps(("ss", l, name))[:, 0:cols], ACT.Ln, bias=eps, scale=1.0 / n), ("ss", l, name))
                await_done(act, ("ss", l, name))
                A(dst, dst, ACT.Exp, scale=-0.5).then_inc(rstd_ready, 1)

            act.wait_ge(sem("cond_loaded"), 16)
            act.wait_ge(sem("scond_cleared"), 1)
            A(scond[:, :, 0:2], condT, ACT.Silu).then_inc(sem("cond_silu"), 1)
            for l in range(DEPTH):
                nc.scalar.preload_act_table_set("natural_log_exp_and_others")
                if l == 0:
                    act.wait_ge(sem("lb_diff"), 1)
                    A(lbw[:, 12:20], lbw[:, 4:12], ACT.Exp).then_inc(sem("lb_exp"), 1)
                    act.wait_ge(sem("xT_ready"), KD)
                    act.wait_ge(sem("eps_ready"), 1)
                else:
                    act.wait_ge(sem("ffn_x_ready"), KD)
                A(sq8_f, xT[:, :], ACT.Square).then_inc(squares_ready, 1)
                finish_norm(l, "n1", D)
                nc.scalar.preload_act_table_set("sigmoid_and_others")
                for j in range(NP):
                    name = ("p", l, j)
                    take(act, name)
                    if j < PQ:
                        done(A(proj[:, j], ps(name)[:, 0:T], ACT.Sigmoid, scale=-1.0), name)
                    elif j < PI or j >= PG:
                        i = j - PQ if j < PI else 4 + j - PG
                        if 8 * l + i >= 2:
                            act.wait_ge(sem("silu_done"), 8 * l + i - 1)
                        A(sg1[:, i % 2], ps(name)[:, 0:T], ACT.Sigmoid).then_inc(sem("sigmoid_ready"), 1)
                    else:
                        done(A(proj[:, j], ps(name)[:, 0:T], ACT.Copy), name)
                nc.scalar.preload_act_table_set("natural_log_exp_and_others")
                for j in (PC, PC + 1, PK, PCQ, PCQ + 1, PCQ + 2):
                    await_done(act, ("p", l, j))
                A(sq4[:, 0:2], proj[:, PC:PC + 2], ACT.Square).then_inc(squares_ready, 1)
                A(sq1[:, 0], proj[:, PK], ACT.Square).then_inc(squares_ready, 1)
                finish_norm(l, "ckv", KVL)
                A(sq4[:, 0:3], proj[:, PCQ:PCQ + 3], ACT.Square).then_inc(squares_ready, 1)
                finish_norm(l, "kpe", ROPE)
                finish_norm(l, "cq", QL)
                act.wait_ge(sem("k_ready"), 4 * (l + 1))
                A(tmp, kf, ACT.Ln, scale=-1.0, bias=1.0).then_inc(sem("logf_ready"), 1)
                act.wait_ge(sem("diff_ready"), 6 * l + 1)
                A(tmp, tmp, ACT.Exp).then_inc(sem("diff_exp"), 1)
                act.wait_ge(sem("diff_ready"), 6 * l + 2)
                A(tmp, tmp, ACT.Exp).then_inc(sem("diff_exp"), 1)
                for h in range(HEADS):
                    act.wait_ge(sem("diff_ready"), 6 * l + 3 + h)
                    for b in range(NB_):
                        e = hT[:, b * T:(b + 1) * T].rearrange("p (c s) -> p c s", s=CH)[:, :, 0:SUB * (b + 1)]
                        last = A(e, e, ACT.Exp)
                    last.then_inc(sem("diff_exp"), 1)
                A(bcum, bcum, ACT.Exp).then_inc(sem("eb_ready"), 1)
                for h in range(HEADS):
                    name = "o%d" % h
                    r = RMS[l, name]
                    take(act, ("o", l, h))
                    A(sq1[:, r % 2], ps(("o", l, h))[:, 0:T], ACT.Square).then_inc(squares_ready, 1)
                    if h:
                        finish_norm(l, "o%d" % (h - 1), 128)
                finish_norm(l, "o3", 128)
                for pre, cnt, width in (("q", 6, lambda j: T), ("k", 8, lambda j: (T, PAST)[j % 2])):
                    for j in range(cnt):
                        r = RMS[l, pre + str(j)]
                        take(act, (pre, l, j))
                        A(sq1[:, r % 2, 0:width(j)], ps((pre, l, j))[:, 0:width(j)], ACT.Square).then_inc(squares_ready, 1)
                        if j:
                            finish_norm(l, pre + str(j - 1), 64 if pre == "q" and j - 1 >= 4 else 128, width(j - 1))
                    finish_norm(l, pre + str(cnt - 1), 64 if pre == "q" else 128, width(cnt - 1))
                for b, (t0, n) in enumerate(VBLK):
                    take(act, ("v", l, b))
                    A(vals[0:n, b], ps(("v", l, b))[0:n, :], ACT.Copy).then_inc(sem("vals_ready"), 1)
                    act.wait_ge(sem("vals_ready"), 5 * l + b + 1)
                    act.sem_inc(bank_free[PLAN["v", l, b][0]], 1)
                for i in range(13):
                    if i < 12:
                        h, b = divmod(i, 3)
                        k0, nk, q0, nq = QB[b]
                        name = ("s", l, h, b)
                        act.wait_ge(sem("negmax_ready"), 12 * l + i + 1)
                        A(probs[0:nq, i % 2, 0:nk], ps(name)[0:nq, 0:nk], ACT.Exp, bias=negmax[0:nq, i:i + 1],
                          scale=SCALE, accum_out=rowsum[0:nq, i:i + 1]).then_inc(sem("exp_ready"), 1)
                for h in range(HEADS):
                    act.wait_ge(sem("omla_ready"), 4 * l + h + 1)
                A(sq4[:, :], proj[:, PI:PI + 4], ACT.Square).then_inc(squares_ready, 1)
                finish_norm(l, "om", 512)
                act.wait_ge(sem("x1_ready"), KD * (l + 1))
                A(sq8_f, xT[:, :], ACT.Square).then_inc(squares_ready, 1)
                finish_norm(l, "n2", D)
                if l == 0:
                    nc.scalar.preload_act_table_set("silu_and_others")

                    def silu(q, j):
                        act.wait_ge(sem("gu_full"), q * 7 + j + 1)
                        act.wait_ge(sem("gu_read"), q * 7 + (j + 2 if j else 3))
                        A(sig_up[:, j % 2], banks[2 * (j % 4)][:, 0:T], ACT.Silu).then_inc(sem("silu_up"), 1)

                    with act.Fori(0, 3) as q:
                        for j in range(7):
                            silu(q, j)
                    silu(3, 0)
            act.wait_ge(sem("logit_diff"), 1)
            nc.scalar.preload_act_table_set("exp_and_others")
            A(rt[:, 48:72], rt[:, 48:72], ACT.Exp).then_inc(sem("logit_exp"), 1)
            nc.scalar.preload_act_table_set("silu_and_others")
            act.wait_ge(sem("ids_ready"), 1)
            n_items = act.value_load(ids[0:1, ITEMS:ITEMS + 1], min_val=NX, max_val=ITEMS)
            with act.Fori(0, n_items) as i:
                act.wait_ge(sem("gathered"), i * 2 + 1)
                A(hgT[:, 0:4], banks[6][:, :].rearrange("p (k n) -> p k n", k=4), ACT.Copy).then_inc(sem("hg_lo_ready"), 1)
                act.wait_ge(sem("gates_turned"), i + 1)
                A(gT, banks[6][:, 0:T], ACT.Copy).then_inc(sem("gates_ready"), 1)
                with act.Fori(0, NFX // 7) as q:
                    for j in range(7):
                        n = i * NFX + q * 7
                        act.wait_ge(sem("gu_full"), n + (NF + j + 1))
                        act.wait_ge(sem("gu_read"), n + (NF + (j + 1 if j < 3 else j)))
                        A(sgX[:, j % 4], banks[j % 4][:, 0:128], ACT.Silu).then_inc(sem("silu_up"), 1)
                act.wait_ge(sem("slots_free"), i * NFX + (NFX + NSLOT))
                A(ysb[:, 0:512], banks[4][:, :], ACT.Copy).then_inc(sem("y_lo_ready"), 1)

        @block.vector
        def _(dve):
            v = nc.vector
            own = [0]

            def link(ins):
                own[0] += 1
                ins.then_inc(sem("vector_step"), 1)
                dve.wait_ge(sem("vector_step"), own[0])

            def scaled(l, name, dst, src, w):
                r = RMS[l, name]
                return v.scalar_tensor_tensor(dst, src, w, rstd[:, r % 2, 0:dst.shape[-1]], ALU.mult, ALU.mult)

            def modulate(l, which, name):
                r = RMS[l, name]
                dve.wait_ge(rstd_ready, r + 1)
                for k in range(KD):
                    for g, t0, n in GRP:
                        last = v.scalar_tensor_tensor(hT[:, k * T + t0:k * T + t0 + n], xT[:, k * T + t0:k * T + t0 + n],
                                                      gain[:, which, k, g:g + 1], rstd[:, r % 2, t0:t0 + n],
                                                      ALU.mult, ALU.mult)
                last.then_inc(normed, 1)
                dve.wait_ge(normed, r + 1)
                sh = 0 if which == 0 else 24
                for k in range(KD):
                    for g, t0, n in GRP:
                        a = hT[:, k * T + t0:k * T + t0 + n]
                        last = v.tensor_scalar(a, a, mods[:, sh + k, g:g + 1], None, ALU.add)
                last.then_inc(sem("h1_ready" if which == 0 else "h2_ready"), 1)

            def mask_scores(l, h):
                name = ("sc", l, h)
                take(dve, name)
                cm = cst[:, CCM:CCM + 128]
                link(v.tensor_tensor(sT[:, h, 0:256].rearrange("p (g n) -> p g n", g=2),
                                     ps(name)[:, 0:256].rearrange("p (g n) -> p g n", g=2),
                                     cm.unsqueeze(1).to_broadcast([128, 2, 128]), ALU.mult))
                done(v.tensor_tensor(sT[0:32, h, 256:T], ps(name)[0:32, 256:T], cm[0:32, 0:32], ALU.mult), name)

            def omla(l, h):
                take(dve, ("oT", l, h))
                done(v.tensor_copy(proj[:, PI + h], ps(("oT", l, h))[:, 0:T]), ("oT", l, h))
                await_done(dve, ("oT", l, h))
                dve.sem_inc(sem("omla_ready"), 1)

            def add_gated(name, k, col, signal):
                take(dve, name)
                for g, t0, n in GRP:
                    x = xT[:, k * T + t0:k * T + t0 + n]
                    last = v.scalar_tensor_tensor(x, ps(name)[:, t0:t0 + n], mods[:, col + k, g:g + 1], x,
                                                  ALU.mult, ALU.add)
                done(last, name)
                await_done(dve, name)
                dve.sem_inc(sem(signal), 1)

            v.memset(scond, 0.0).then_inc(sem("scond_cleared"), 1)
            v.memset(eps, EPS).then_inc(sem("eps_ready"), 1)
            dve.wait_ge(sem("vecs_loaded"), 16)
            dve.wait_ge(sem("consts_loaded"), 16)
            link(v.tensor_tensor(lbw[:, 0:4], V(0, VLB, 4), V(1, VLB, 4), ALU.max))
            v.tensor_tensor(lbw[:, 4:8], V(0, VLB, 4), lbw[:, 0:4], ALU.subtract)
            link(v.tensor_tensor(lbw[:, 8:12], V(1, VLB, 4), lbw[:, 0:4], ALU.subtract))
            v.memset(oml[:, 0, :], 1.0).then_inc(sem("lb_diff"), 1)
            dve.wait_ge(sem("lb_exp"), 1)
            link(v.tensor_tensor(lbw[:, 0:4], lbw[:, 12:16], lbw[:, 16:20], ALU.add))
            link(v.reciprocal(lbw[:, 0:4], lbw[:, 0:4]))
            link(v.tensor_tensor(oml[:, 1, :], lbw[:, 0:4], lbw[:, 12:16], ALU.mult))
            for k in range(KD):
                take(dve, ("x", k))
                done(v.tensor_copy(xT[:, k * T:(k + 1) * T], ps(("x", k))[:, 0:T]), ("x", k))
            for k in range(KD):
                await_done(dve, ("x", k))
                dve.sem_inc(sem("xT_ready"), 1)
            for l in range(DEPTH):
                for j in range(17):
                    if j < 16:
                        name = ("mod", l, j)
                        take(dve, name)
                        if l and j == 0:
                            dve.wait_ge(sem("rows_out0"), 64)
                            dve.wait_ge(sem("rows_out1"), 32)
                        done(v.tensor_copy(kv_tok[:, j % 2, :], ps(name)[:, 0:384]), name)
                        await_done(dve, name)
                        dve.sem_inc(sem("modrow_ready"), 1)
                    if j:
                        name = ("modT", l, j - 1)
                        take(dve, name)
                        done(v.tensor_reduce(mods[:, 3 * j - 3:3 * j, :],
                                             ps(name)[:, 0:384].rearrange("p (f r g) -> p f g r", f=3, r=4)[:, :, 0:2, :],
                                             AX.X, ALU.add), name)
                await_done(dve, ("modT", l, 15))
                await_done(dve, ("modT", l, 14))
                link(v.tensor_tensor(mods, mods, V(l, VB, 48).unsqueeze(2).to_broadcast([128, 48, 2]), ALU.add))
                for which, c, vn in ((0, 8, VN1), (1, 32, VN2)):
                    for g in range(2):
                        last = v.scalar_tensor_tensor(gain[:, which, :, g], mods[:, c:c + 8, g], 1.0, V(l, vn, 8),
                                                      ALU.add, ALU.mult)
                link(last)
                modulate(l, 0, "n1")
                for j in list(range(PQ, PI)) + list(range(PG, NP)):
                    i = j - PQ if j < PI else 4 + j - PG
                    name = ("p", l, j)
                    dve.wait_ge(sem("sigmoid_ready"), 8 * l + i + 1)
                    v.tensor_tensor(proj[:, j], ps(name)[:, 0:T], sg1[:, i % 2], ALU.mult).then_inc(sem("silu_done"), 1)
                    dve.wait_ge(sem("silu_done"), 8 * l + i + 1)
                    dve.sem_inc(bank_free[PLAN[name][0]], 1)
                r = RMS[l, "ckv"]
                dve.wait_ge(rstd_ready, r + 1)
                for k in range(2):
                    last = scaled(l, "ckv", ckv_all[:, k, 0:T], proj[:, PC + k], V(l, VKV + k))
                last.then_inc(normed, 1)
                dve.wait_ge(rstd_ready, r + 2)
                scaled(l, "kpe", kpe_all[:, 0:T], proj[:, PK], V(l, VKR)).then_inc(normed, 1)
                dve.wait_ge(rstd_ready, r + 3)
                for k in range(3):
                    last = scaled(l, "cq", proj[:, PCQ + k], proj[:, PCQ + k], V(l, VQA + k))
                last.then_inc(normed, 1)
                take(dve, ("rotk", l))
                done(v.tensor_tensor(rot_tmp[:, :], ps(("rotk", l))[:, 0:T], sin, ALU.mult), ("rotk", l))
                link(v.tensor_tensor(kpe_all[:, 0:T], kpe_all[:, 0:T], cos, ALU.mult))
                await_done(dve, ("rotk", l))
                v.tensor_tensor(kpe_all[:, 0:T], kpe_all[:, 0:T], rot_tmp[:, :], ALU.add).then_inc(sem("kpe_ready"), 1)
                dve.wait_ge(sem("kpe_ready"), l + 1)
                for h in range(HEADS):
                    await_done(dve, ("p", l, PF + h))
                for h in range(HEADS):
                    v.tensor_scalar(kf[:, h * T:(h + 1) * T], kf[:, h * T:(h + 1) * T], oml[:, l, h:h + 1], None,
                                    ALU.mult).then_inc(sem("k_ready"), 1)
                dve.wait_ge(sem("logf_ready"), l + 1)
                link(v.tensor_tensor_scan(bcum, cst[:, CRS:CRS + HEADS * T], tmp, 0.0, ALU.mult, ALU.add))
                b4 = bcum.rearrange("p (c b s) -> p c b s", b=NB_, s=SUB)
                b3 = bcum.rearrange("p (c s) -> p c s", s=CH)
                ref3 = ref.rearrange("p (c b) -> p c b", b=NB_)
                link(v.memset(ref3[:, :, 0], 0.0))
                link(v.tensor_copy(ref3[:, :, 1:NB_], b4[:, :, 0:NB_ - 1, SUB - 1]))
                v.tensor_tensor(tmp.rearrange("p (n s) -> p n s", s=SUB), bcum.rearrange("p (n s) -> p n s", s=SUB),
                                ref.unsqueeze(2).to_broadcast([128, HEADS * T // SUB, SUB]), ALU.subtract
                                ).then_inc(sem("diff_ready"), 1)
                dve.wait_ge(sem("diff_exp"), 6 * l + 1)
                link(v.tensor_tensor(qt_f, qf, tmp, ALU.mult))
                v.tensor_tensor(tmp.rearrange("p (c s) -> p c s", s=CH),
                                b3[:, :, CH - 1:CH].to_broadcast([128, HEADS * NC_, CH]), b3, ALU.subtract
                                ).then_inc(sem("diff_ready"), 1)
                dve.wait_ge(sem("diff_exp"), 6 * l + 2)
                v.tensor_tensor(tmp, tmp, kf, ALU.mult).then_inc(sem("kd_ready"), 1)
                def to_tokens(kind, dst):
                    for h in range(HEADS):
                        name = (kind, l, h)
                        take(dve, name)
                        s = ps(name)[:, 0:384].rearrange("p (g n) -> p g n", g=3)
                        v.tensor_copy(dst[:, 0:2, 128 * h:128 * h + 128], s[:, 0:2]).then_inc(
                            sem("v_tok_ready" if kind == "vt" else "kd_tok_ready"), 1)
                        v.tensor_copy(dst[0:32, 2, 128 * h:128 * h + 128], s[0:32, 2]).then_inc(
                            sem("v_tok_ready" if kind == "vt" else "kd_tok_ready"), 1)
                        dve.wait_ge(sem("v_tok_ready" if kind == "vt" else "kd_tok_ready"), 8 * l + 2 * h + 2)
                        dve.sem_inc(bank_free[PLAN[kind, l, h][0]], 1)

                to_tokens("vt", v_tok)
                for j in range(3):
                    name = ("cache", l, j)
                    take(dve, name)
                    dst = ckv_all[:, j, T:KEYS] if j < 2 else kpe_all[:, T:KEYS]
                    done(v.tensor_copy(dst, ps(name)[:, 0:PAST]), name)
                for j in range(3):
                    await_done(dve, ("cache", l, j))
                dve.sem_inc(sem("ckv_all_ready"), 2)
                to_tokens("kd", kd_tok)
                link(v.memset(hT[:, :], 0.0))
                for h in range(HEADS):
                    if h:
                        take(dve, ("sc", l, h - 1))
                    bh = bcum[:, h * T:(h + 1) * T].rearrange("p (c s) -> p c s", s=CH)
                    kh = kf[:, h * T:(h + 1) * T].rearrange("p (c s) -> p c s", s=CH)
                    for b in range(NB_):
                        n = SUB * (b + 1)
                        e = hT[:, b * T:(b + 1) * T].rearrange("p (c s) -> p c s", s=CH)[:, :, 0:n]
                        last = v.tensor_tensor(e, ref3[:, h * NC_:(h + 1) * NC_, b:b + 1].to_broadcast([128, NC_, n]),
                                               bh[:, :, 0:n], ALU.subtract)
                    last.then_inc(sem("diff_ready"), 1)
                    if h:
                        mask_scores(l, h - 1)
                    dve.wait_ge(sem("diff_exp"), 6 * l + 3 + h)
                    for b in range(NB_):
                        n = SUB * (b + 1)
                        e = hT[:, b * T:(b + 1) * T].rearrange("p (c s) -> p c s", s=CH)[:, :, 0:n]
                        last = v.tensor_tensor(e, e, kh[:, :, 0:n], ALU.mult)
                    last.then_inc(sem("kt_ready"), 1)
                take(dve, ("sc", l, 3))
                mask_scores(l, 3)
                dve.wait_ge(sem("eb_ready"), l + 1)
                v.tensor_tensor(qf, qf, bcum, ALU.mult).then_inc(sem("qe_ready"), 1)
                for c in range(NC_):
                    name = ("u", l, c)
                    take(dve, name)
                    if 2 <= c < NC_ - 1:
                        dve.wait_ge(sem("state_used"), 7 * l + c - 1)
                    if l and c in (1, NC_ - 1):
                        dve.wait_ge(sem("state_out"), 32)
                    if c == NC_ - 1:
                        dve.wait_ge(sem("state_loaded"), 16 * (l + 1))
                    for h in range(HEADS):
                        hs = slice(128 * h, 128 * h + 128)
                        dec = bcum[:, h * T + CH * c + CH - 1:h * T + CH * c + CH]
                        if c == 0:
                            last = v.tensor_copy(states[:, 1, hs], ps(name)[:, hs])
                        elif c < NC_ - 1:
                            last = v.scalar_tensor_tensor(states[:, (c + 1) % 2, hs], states[:, c % 2, hs], dec,
                                                          ps(name)[:, hs], ALU.mult, ALU.add)
                        else:
                            last = v.scalar_tensor_tensor(s_new[:, hs], s_smp[:, hs], dec, ps(name)[:, hs],
                                                          ALU.mult, ALU.add)
                    done(last, name)
                    await_done(dve, name)
                    if c < NC_ - 1:
                        dve.sem_inc(sem("state_ready"), 1)
                    if c == NC_ - 1:
                        dve.sem_inc(sem("state_new"), 1)
                for h in range(HEADS):
                    r = RMS[l, "o%d" % h]
                    dve.wait_ge(rstd_ready, r + 1)
                    done(v.scalar_tensor_tensor(sg1[:, h % 2], ps(("o", l, h))[:, 0:T], V(l, VON), rstd[:, r % 2],
                                                ALU.mult, ALU.mult), ("o", l, h))
                    await_done(dve, ("o", l, h))
                    dve.sem_inc(normed, 1)
                    v.tensor_tensor(proj[:, PG + h], proj[:, PG + h], sg1[:, h % 2], ALU.mult).then_inc(sem("mix_ready"), 1)
                def rotate(j):
                    take(dve, ("rotq", l, j))
                    done(v.tensor_tensor(rot_tmp[:, :], ps(("rotq", l, j))[:, 0:T], sin, ALU.mult), ("rotq", l, j))
                    link(v.tensor_tensor(qpe[:, j], qpe[:, j], cos, ALU.mult))
                    await_done(dve, ("rotq", l, j))
                    v.tensor_tensor(qpe[:, j], qpe[:, j], rot_tmp[:, :], ALU.add).then_inc(sem("qpe_ready"), 1)
                    dve.wait_ge(sem("qpe_ready"), 2 * l + j + 1)

                for j in range(6):
                    r = RMS[l, "q%d" % j]
                    dve.wait_ge(rstd_ready, r + 1)
                    dst, w = (qn[:, j], V(l, VQN)) if j < 4 else (qpe[:, j - 4], V(l, VQR))
                    done(scaled(l, "q%d" % j, dst, ps(("q", l, j))[:, 0:T], w), ("q", l, j))
                    await_done(dve, ("q", l, j))
                    dve.sem_inc(normed, 1)
                for j in range(2):
                    rotate(j)
                for j in range(8):
                    t0, n = ((0, T), (T, PAST))[j % 2]
                    r = RMS[l, "k%d" % j]
                    dve.wait_ge(rstd_ready, r + 1)
                    done(scaled(l, "k%d" % j, kn[:, j // 2, t0:t0 + n], ps(("k", l, j))[:, 0:n], V(l, VKN)), ("k", l, j))
                    await_done(dve, ("k", l, j))
                    dve.sem_inc(normed, 1)
                for g, (t0, n) in enumerate(TB):
                    take(dve, ("ckvo", l, g))
                    if 3 * l + g >= 2:
                        dve.wait_ge(sem("rows_out%d" % ((l + g) % 2)), 32 * ((3 * l + g) // 2))
                    done(v.tensor_copy(kv_tok[0:n, (3 * l + g) % 2, :],
                                       ps(("ckvo", l, g))[0:n, 0:384]), ("ckvo", l, g))
                    await_done(dve, ("ckvo", l, g))
                    dve.sem_inc(sem("kv_tok_ready"), 1)
                for i in range(14):
                    if i < 12:
                        h, b = divmod(i, 3)
                        k0, nk, q0, nq = QB[b]
                        name = ("s", l, h, b)
                        take(dve, name)
                        link(v.reduce_max(rowmax[0:nq, i:i + 1], ps(name)[0:nq, 0:nk], AX.X))
                        v.tensor_scalar(negmax[0:nq, i:i + 1], rowmax[0:nq, i:i + 1], -SCALE, None, ALU.mult
                                        ).then_inc(sem("negmax_ready"), 1)
                    if 1 <= i < 13:
                        h, b = divmod(i - 1, 3)
                        k0, nk, q0, nq = QB[b]
                        dve.wait_ge(sem("exp_ready"), 12 * l + i)
                        dve.sem_inc(bank_free[PLAN["s", l, h, b][0]], 1)
                        link(v.reciprocal(rinv[0:nq, i - 1:i], rowsum[0:nq, i - 1:i]))
                        pr = probs[0:nq, (i - 1) % 2, 0:nk]
                        v.tensor_scalar(pr, pr, rinv[0:nq, i - 1:i], None, ALU.mult).then_inc(sem("probs_ready"), 1)
                        name = ("pT", l, h, b)
                        take(dve, name)
                        for n_, kb in enumerate(BLK_OF[b]):
                            n = VBLK[kb][1]
                            last = v.tensor_copy(pT[0:n, (i - 1) % 2, nq * n_:nq * n_ + nq], ps(name)[0:n, nq * n_:nq * n_ + nq])
                        done(last, name)
                        await_done(dve, name)
                        dve.sem_inc(sem("pT_ready"), 1)
                        if i >= 2 and (i - 2) % 3 == 2:
                            omla(l, (i - 2) // 3)
                omla(l, 3)
                r = RMS[l, "om"]
                dve.wait_ge(rstd_ready, r + 1)
                for h in range(HEADS):
                    last = scaled(l, "om", proj[:, PI + h], proj[:, PI + h], V(l, VMO + h))
                last.then_inc(normed, 1)
                dve.wait_ge(normed, r + 1)
                dve.sem_inc(sem("mix_ready"), 1)
                for k in range(KD):
                    add_gated(("wo", l, k), k, 16, "x1_ready")
                modulate(l, 1, "n2")
                if l == 0:
                    dve.sem_inc(sem("gu_read"), 3)

                    def mul(q, j):
                        dve.wait_ge(sem("silu_up"), q * 7 + j + 1)
                        v.tensor_tensor(arena[:, bass.ds(q * (7 * T) + j * T, T)],
                                        banks[2 * (j % 4) + 1][:, 0:T], sig_up[:, j % 2], ALU.mult
                                        ).then_inc(sem("gu_read"), 1)

                    with dve.Fori(0, 3) as q:
                        for j in range(7):
                            mul(q, j)
                    mul(3, 0)
                    for k in range(KD):
                        add_gated(("down", k), k, 40, "ffn_x_ready")
            def r3(a):
                return rt[:, a:a + 24].rearrange("p (g e) -> p g e", g=3)

            logit, chosen, ex, gate, key, order = r3(0), r3(24), r3(48), r3(80), r3(104), r3(248)
            top, total = rt[:, 72:75], rt[:, 75:78]
            nblk, end, start = rt[:, 128:136], rt[:, 136:144], rt[:, 144:152]
            base, eid = rt[:, 152:164], rt[:, 164:176]
            keyi = rt[:, 176:212].rearrange("p (g i) -> p g i", g=3)
            gatei = rt[:, 212:248].rearrange("p (g i) -> p g i", g=3)
            for g, (t0, n) in enumerate(TB):
                for f in range(2):
                    take(dve, ("ht", g, f))
                    done(v.tensor_copy(h_tok[0:n, g, 512 * f:512 * f + 512], ps(("ht", g, f))[0:n, :]), ("ht", g, f))
            for g in range(3):
                for f in range(2):
                    await_done(dve, ("ht", g, f))
            link(v.memset(logit[:, :, :], 0.0))
            take(dve, ("logits",))
            link(v.tensor_copy(rt[:, 0:16], ps(("logits",))[:, 0:16]))
            done(v.tensor_copy(rt[0:32, 16:24], ps(("logits",))[0:32, 16:24]), ("logits",))
            await_done(dve, ("logits",))
            link(v.tensor_reduce(top, logit, AX.X, ALU.max))
            v.tensor_tensor(ex, logit, top.unsqueeze(2).to_broadcast([128, 3, NX]), ALU.subtract
                            ).then_inc(sem("logit_diff"), 1)
            c4 = cmp8.rearrange("p (g e f) -> p g e f", g=3, e=NX)
            d4 = cmp8b.rearrange("p (g e f) -> p g e f", g=3, e=NX)
            lt = cst[:, CLT:CLT + 64].rearrange("p (e f) -> p e f", e=NX)
            for g in range(3):
                other = logit[:, g].unsqueeze(1).to_broadcast([128, NX, NX])
                this = logit[:, g].unsqueeze(2).to_broadcast([128, NX, NX])
                link(v.tensor_tensor(c4[:, g], other, this, ALU.is_gt))
                link(v.tensor_tensor(d4[:, g], other, this, ALU.is_equal))
                link(v.tensor_tensor(d4[:, g], d4[:, g], lt, ALU.mult))
            link(v.tensor_tensor(cmp8, cmp8, cmp8b, ALU.add))
            link(v.tensor_reduce(order, c4, AX.X, ALU.add))
            link(v.tensor_scalar(chosen, order, 1.5, None, ALU.is_lt))
            link(v.memset(chosen[32:64, 2], 0.0))
            link(v.memset(chosen[64:128, 2], 0.0))
            dve.sem_inc(sem("chosen_ready"), 1)
            dve.wait_ge(sem("logit_exp"), 1)
            link(v.tensor_tensor(ex, ex, chosen, ALU.mult))
            link(v.tensor_reduce(total, ex, AX.X, ALU.add))
            link(v.tensor_scalar(total, total, 1e-30, None, ALU.max))
            link(v.reciprocal(total, total))
            link(v.tensor_tensor(gate, ex, total.unsqueeze(2).to_broadcast([128, 3, NX]), ALU.mult))
            take(dve, ("rank",))
            rank = ps(("rank",))[:, 0:24].rearrange("p (g e) -> p g e", g=3)
            count = ps(("rank",))[:, 24:32]
            link(v.tensor_tensor(key, rank, chosen, ALU.mult))
            link(v.tensor_scalar(order, chosen, 1e4, -1e4, ALU.mult, ALU.add))
            link(v.tensor_tensor(key, key, order, ALU.add))
            link(v.tensor_scalar(nblk, count, SLOTS_X + 0.5, None, ALU.is_gt))
            done(v.tensor_scalar(start, count, 2 * SLOTS_X + 0.5, 1.0, ALU.is_gt, ALU.add), ("rank",))
            await_done(dve, ("rank",))
            link(v.tensor_tensor(nblk, nblk, start, ALU.add))
            link(v.tensor_tensor_scan(end, ones[:, 0:NX], nblk, 0.0, ALU.mult, ALU.add))
            link(v.tensor_tensor(start, end, nblk, ALU.subtract))
            oh = cmpi.rearrange("p (i e) -> p i e", e=NX)
            o2 = cmpi2.rearrange("p (i e) -> p i e", e=NX)
            full3 = [128, ITEMS, NX]
            it = cst[:, CIT:CIT + ITEMS].unsqueeze(2).to_broadcast(full3)
            link(v.tensor_tensor(oh, end.unsqueeze(1).to_broadcast(full3), it, ALU.is_gt))
            link(v.tensor_tensor(o2, start.unsqueeze(1).to_broadcast(full3), it, ALU.is_gt))
            link(v.tensor_tensor(oh, oh, o2, ALU.subtract))
            link(v.tensor_tensor(o2, it, start.unsqueeze(1).to_broadcast(full3), ALU.subtract))
            link(v.tensor_tensor(o2, o2, oh, ALU.mult))
            link(v.tensor_reduce(base, o2, AX.X, ALU.add))
            link(v.tensor_scalar(base, base, float(SLOTS_X), None, ALU.mult))
            link(v.tensor_tensor(o2, oh, cst[:, CEX:CEX + NX].unsqueeze(1).to_broadcast(full3), ALU.mult))
            link(v.tensor_reduce(eid, o2, AX.X, ALU.add))
            link(v.tensor_copy(ids[:, 0:ITEMS], eid))
            link(v.tensor_copy(ids[:, ITEMS:ITEMS + 1], end[:, NX - 1:NX]))
            dve.sem_inc(sem("ids_ready"), 1)
            for g in range(3):
                link(v.tensor_tensor(o2, oh, key[:, g].unsqueeze(1).to_broadcast(full3), ALU.mult))
                link(v.tensor_reduce(keyi[:, g], o2, AX.X, ALU.add))
                link(v.tensor_tensor(keyi[:, g], keyi[:, g], base, ALU.subtract))
                link(v.tensor_tensor(o2, oh, gate[:, g].unsqueeze(1).to_broadcast(full3), ALU.mult))
                link(v.tensor_reduce(gatei[:, g], o2, AX.X, ALU.add))
            link(v.memset(acc[:, :, :], 0.0))
            dve.sem_inc(sem("scatter_read"), KD)
            n_items = dve.value_load(ids[0:1, ITEMS:ITEMS + 1], min_val=NX, max_val=ITEMS)
            io = cst[:, CIO:CIO + 128].unsqueeze(1).to_broadcast([128, 3, 128])
            with dve.Fori(0, n_items) as i:
                v.tensor_tensor(pick, io, keyi[:, :, bass.ds(i, 1)].to_broadcast([128, 3, 128]), ALU.is_equal
                                ).then_inc(sem("pick_made"), 1)
                dve.wait_ge(sem("pick_made"), i + 1)
                v.tensor_tensor(pickg, pick, gatei[:, :, bass.ds(i, 1)].to_broadcast([128, 3, 128]), ALU.mult
                                ).then_inc(sem("pick_ready"), 1)
                dve.wait_ge(sem("gathered"), i * 2 + 2)
                v.tensor_copy(hgT[:, 4:8], banks[7][:, :].rearrange("p (k n) -> p k n", k=4)
                              ).then_inc(sem("hg_hi_ready"), 1)
                with dve.Fori(0, NFX // 7) as q:
                    for j in range(7):
                        n = i * NFX + q * 7
                        dve.wait_ge(sem("silu_up"), n + (NF + j + 1))
                        v.tensor_tensor(aX[:, j], banks[j % 4][:, 128:256], sgX[:, j % 4], ALU.mult
                                        ).then_inc(sem("gu_read"), 1)
                dve.wait_ge(sem("slots_free"), i * NFX + (NFX + NSLOT))
                v.tensor_copy(ysb[:, 512:1024], banks[5][:, :]).then_inc(sem("y_hi_ready"), 1)
                for k in range(KD):
                    dve.wait_ge(sem("scattered"), i * KD + (k + 1))
                    v.tensor_tensor(acc[:, k], acc[:, k], banks[6 + k % 2][:, 0:T], ALU.add
                                    ).then_inc(sem("scatter_read"), 1)
                dve.wait_ge(sem("scatter_read"), i * KD + 2 * KD)
            for k in range(KD):
                for g, t0, n in GRP:
                    x = xT[:, k * T + t0:k * T + t0 + n]
                    last = v.scalar_tensor_tensor(x, acc[:, k, t0:t0 + n], mods[:, 40 + k, g:g + 1], x, ALU.mult, ALU.add)
                last.then_inc(sem("y_final"), 1)
            for g, (t0, n) in enumerate(TB):
                for f in range(2):
                    take(dve, ("y", g, f))
                    v.tensor_copy(y_tok[0:n, g, 512 * f:512 * f + 512], ps(("y", g, f))[0:n, :]).then_inc(sem("y_ready"), 1)

        @block.gpsimd
        def _(pool):
            for l in range(DEPTH):
                if l:
                    take(pool, ("cache", l - 1, 2))
                    pool.wait_ge(sem("state_new"), l)
                    take(pool, ("o", l - 1, 3))
                for k, src in ((0, cache_in[0][l]), (256, cache_in[1][l]), (320, cache_in[1][l])):
                    n = 256 if k == 0 else ROPE
                    pool.dma_start(cache_tok[:, :, k:k + n], src.rearrange("(b p) n -> p b n", p=128)
                                   ).then_inc(sem("cache_loaded"), 16)
                pool.dma_start(s_smp[:, :].rearrange("p (h n) -> p h n", h=HEADS),
                               state_in[l].rearrange("h k v -> k h v")).then_inc(sem("state_loaded"), 16)
                pool.wait_ge(sem("state_ready"), 8 * (l + 1))
                pool.dma_start(s_out[0][l].rearrange("h k v -> k h v"),
                               states[:, 0].rearrange("p (h n) -> p h n", h=HEADS)).then_inc(sem("state_out"), 16)
                pool.wait_ge(sem("state_new"), l + 1)
                pool.dma_start(s_out[1][l].rearrange("h k v -> k h v"),
                               s_new[:, :].rearrange("p (h n) -> p h n", h=HEADS)).then_inc(sem("state_out"), 16)
                for g, (t0, n) in enumerate(TB):
                    pool.wait_ge(sem("kv_tok_ready"), 3 * l + g + 1)
                    src = kv_tok[0:n, (3 * l + g) % 2]
                    out, r0 = (kv_out[0], t0) if g < 2 else (kv_out[1], 0)
                    pool.dma_start(out[0][l][r0:r0 + n, :], src[:, 0:KVL]).then_inc(sem("rows_out%d" % ((l + g) % 2)), 16)
                    pool.dma_start(out[1][l][r0:r0 + n, :], src[:, KVL:KVL + ROPE]).then_inc(sem("rows_out%d" % ((l + g) % 2)), 16)
            pool.wait_ge(sem("x1_ready"), KD * DEPTH)
            pool.dma_start(router, w_router).then_inc(sem("router_loaded"), 16)
            for g, (t0, n) in enumerate(TB):
                pool.wait_ge(sem("y_ready"), 2 * g + 2)
                out, r0 = (y_out[0], t0) if g < 2 else (y_out[1], 0)
                pool.dma_start(out[r0:r0 + n, :], y_tok[0:n, g]).then_inc(sem("y_stored"), 16)
            pool.wait_ge(sem("y_stored"), 48)
            pool.wait_ge(sem("state_out"), 32 * DEPTH)
            pool.wait_ge(sem("rows_out0"), 96)
            pool.wait_ge(sem("rows_out1"), 96)


def kernel(**x):
    import concourse.bacc as bacc
    from concourse.bass_utils import run_bass_kernel_spmd as run

    def slabs(w, per):
        *lead, k, n = w.shape
        w = w.reshape(*lead, k // 128, 128, n // (128 * per), per, 128)
        a = len(lead)
        return w.transpose(*range(a), a + 2, a + 1, a + 3, a, a + 4).reshape(*lead, n // (128 * per), 128, -1)

    def col(v):
        return v.reshape(v.shape[0], -1, 128).transpose(0, 2, 1)

    x = {k: np.asarray(v) for k, v in x.items()}
    w = x["w_in"]
    H = 512
    kpe = w[:, :, 4 * H + QL + KVL:]
    win = np.concatenate([w[:, :, H:2 * H], w[:, :, 0:H], w[:, :, 2 * H:3 * H], w[:, :, 4 * H + QL:4 * H + QL + KVL],
                          kpe, kpe, w[:, :, 4 * H:4 * H + QL], w[:, :, 3 * H:4 * H]], axis=2)
    q = x["mla_wqb"].reshape(DEPTH, QL, HEADS, 128 + ROPE)
    wqb = np.concatenate([q[..., :128].reshape(DEPTH, QL, -1), q[..., 128:].reshape(DEPTH, QL, -1)], axis=2)
    kv = x["mla_wkvb"].reshape(DEPTH, KVL, HEADS, 256)
    wkvb = np.concatenate([kv[..., :128].reshape(DEPTH, KVL, -1), kv[..., 128:].reshape(DEPTH, KVL, -1)], axis=2)
    g, u = (x[n][0].reshape(KD, 128, NF, 128).transpose(2, 1, 0, 3).reshape(NF, 128, D) for n in ("ffn_w_gate", "ffn_w_up"))
    wup = np.concatenate([g, u], axis=2)
    eg, eu = (x[n][0].reshape(NX, KD, 128, NFX, 128).transpose(0, 3, 2, 1, 4).reshape(NX * NFX, 128, D)
              for n in ("moe_w_gate", "moe_w_up"))
    wmoe = np.concatenate([eg, eu, x["moe_w_down"][0].reshape(NX * NFX, 128, D)], axis=2)
    two = lambda v: np.concatenate([v, v], axis=1)
    vecs = np.concatenate([col(x["ada_b"]), col(x["norm1_w"]), col(x["norm2_w"]), col(x["hg_onorm_w"]),
                           col(x["mla_qa_norm_w"]), col(x["mla_kva_norm_w"]), col(x["mla_qn_nope_w"]),
                           col(two(x["mla_qn_rope_w"])), col(x["mla_kn_nope_w"]), col(two(x["mla_kn_rope_w"])),
                           col(x["mla_onorm_w"]), col(x["hg_lower_bounds"])], axis=2)
    vecs = vecs.transpose(1, 0, 2).reshape(128, -1)
    cond = np.stack([x["c_prompt"][0], x["c_sample"][0]], axis=1).reshape(KD, 128, 2).transpose(1, 0, 2).reshape(128, -1)
    arrays = {
        "consts": constants(), "vecs": vecs, "cond": cond,
        "x_in": np.concatenate([x["x_prompt"][0], x["x_sample"][0]], axis=0),
        "state_in": x["state_hgrn"][:, 0], "cache_ckv_in": x["cache_ckv"][:, 0], "cache_kpe_in": x["cache_kpe"][:, 0],
        "w_ada": x["ada_w"].reshape(DEPTH, KD, 128, 16, 384).transpose(0, 3, 2, 1, 4).reshape(DEPTH, 16, 128, -1), "w_win": slabs(win, 2),
        "w_wqb": wqb.reshape(DEPTH, 3, 128, -1).transpose(0, 2, 1, 3).reshape(DEPTH, 1, 128, -1),
        "w_wkvb": wkvb.reshape(DEPTH, 2, 128, -1).transpose(0, 2, 1, 3).reshape(DEPTH, 1, 128, -1),
        "w_wo": slabs(x["w_o"], 2), "w_up": wup, "w_down": slabs(x["ffn_w_down"][0], 1),
        "w_router": x["moe_router"][0].reshape(KD, 128, NX).transpose(1, 0, 2), "w_moe": wmoe,
    }
    arrays = {k: np.ascontiguousarray(v) for k, v in arrays.items()}
    nc = bacc.Bacc("TRN2", target_bir_lowering=False, num_devices=1)
    a = {k: nc.dram_tensor(k, v.shape, F32, kind="ExternalInput").ap() for k, v in arrays.items()}
    outs = {"y_prompt": (SEQ, D), "y_sample": (DEC, D), "s_prompt": (DEPTH, HEADS, 128, 128),
            "ckv_prompt": (DEPTH, SEQ, KVL), "kpe_prompt": (DEPTH, SEQ, ROPE),
            "s_sample": (DEPTH, HEADS, 128, 128), "ckv_sample": (DEPTH, DEC, KVL), "kpe_sample": (DEPTH, DEC, ROPE)}
    o = {k: nc.dram_tensor(k, s, F32, kind="ExternalOutput").ap() for k, s in outs.items()}
    build(nc, a["consts"], a["vecs"], a["cond"], a["x_in"], a["state_in"], (a["cache_ckv_in"], a["cache_kpe_in"]),
          a["w_ada"], a["w_win"], a["w_wqb"], a["w_wkvb"], a["w_wo"], a["w_up"], a["w_down"], a["w_router"], a["w_moe"],
          (o["y_prompt"], o["y_sample"]), (o["s_prompt"], o["s_sample"]),
          ((o["ckv_prompt"], o["kpe_prompt"]), (o["ckv_sample"], o["kpe_sample"])))
    r = run(nc, [arrays], core_ids=[0]).results[0]
    y_p, y_s = r["y_prompt"][None], r["y_sample"][None]
    return (y_p, y_s, r["s_prompt"][:, None], r["ckv_prompt"][:, None], r["kpe_prompt"][:, None],
            r["s_sample"][:, None], r["ckv_sample"][:, None], r["kpe_sample"][:, None])
```

```python
import numpy as np
import concourse.bass as bass
from concourse import mybir
from contextlib import ExitStack

F32 = mybir.dt.float32
F32R = mybir.dt.float32r
I32 = mybir.dt.int32
ALU = mybir.AluOpType
ACT = mybir.ActivationFunctionType
AX = mybir.AxisListType

D, SEQ, DEC, PAST, DEPTH = 1024, 256, 32, 256, 2
T = SEQ + DEC
KD = D // 128
HEADS = 4
QL, KVL, ROPE = 384, 256, 64
SCALE = (128 + ROPE) ** -0.5
FF, FX, NX = 2816, 3584, 8
NF, NFX = FF // 128, FX // 128
EPS = 1e-6
KEYS = T + PAST
CH, SUB = 32, 4
NC_, NB_ = T // CH, CH // SUB
SLOTS_X = 128
ITEMS = 12
GRP = ((0, 0, SEQ), (1, SEQ, DEC))
TB = ((0, 128), (128, 128), (256, 32))
NSLOT, SLOTW = 6, 3072
XSLOT = 4
SCATTER = ((), (0, 1), (2, 3), (4, 5, 6, 7))
ARENA = 16224
PF, PQ, PG, PI, PC, PK, PCQ, NP = 0, 4, 8, 12, 16, 18, 19, 22
VB, VN1, VN2, VON, VQA, VKV, VQN, VQR, VKN, VKR, VMO, VLB, NV = 0, 48, 56, 64, 65, 68, 70, 71, 72, 73, 74, 78, 82
CI, CO, CO64, CROT, CCOS, CSIN, CCM, CRS, CU, CIO, CLT, CMQ, CMK, CIT, CEX, NCST = np.cumsum(
    [0, 128, 128, 128, 128, T, T, 128, HEADS * T, 128, 128, 64, 128, 128, ITEMS, NX]).tolist()


def constants():
    c = np.zeros((128, NCST), np.float32)
    p = np.arange(128)
    c[:, CI:CI + 128] = np.eye(128)
    c[:, CO:CO + 128] = 1.0
    c[:, CO64:CO64 + 128] = p[:, None] // 64 == p[None, :] // 64
    for h in (0, 64):
        for m in range(32):
            c[h + 32 + m, CROT + h + m] = -1.0
            c[h + m, CROT + h + 32 + m] = 1.0
    inv = (10000.0 ** (-np.arange(32, dtype=np.float32) / 32)).astype(np.float32)
    pos = np.concatenate([np.arange(SEQ), PAST + np.arange(DEC)]).astype(np.float32)
    ang = (pos[None, :] * inv[p % 32][:, None]).astype(np.float32)
    c[:, CCOS:CCOS + T] = np.cos(ang.astype(np.float64))
    c[:, CSIN:CSIN + T] = np.sin(ang.astype(np.float64))
    s, t = p[:, None], p[None, :]
    c[:, CCM:CCM + 128] = (s // CH == t // CH) & (s <= t)
    c[:, CRS:CRS + HEADS * T] = np.arange(HEADS * T)[None, :] % CH != 0
    c[:, CU:CU + 128] = s < t
    c[:, CIO:CIO + 128] = t
    e = np.arange(NX)
    c[:, CLT:CLT + 64] = (e[None, :] < e[:, None]).reshape(1, 64)
    c[0, CMQ:CMQ + 128] = p < 64
    c[0, CMK:CMK + 128] = np.where(p < 64, 0.0, -1e30)
    c[:, CIT:CIT + ITEMS] = np.arange(ITEMS)
    c[:, CEX:CEX + NX] = e
    return c


STREAM = [(n, l, k, w) for l in range(DEPTH) for n, k, w in
          [("ada", 16, 3072), ("win", 11, 2048), ("wqb", 1, 2304), ("wkvb", 1, 2048), ("wo", 4, 2048)]
          + [("up", NF, 2048), ("down", KD, FF)] * (l == 0)]
START = {}
_at = 0
for _n, _l, _k, _w in STREAM:
    START[_n, _l] = _at
    _at += _k
START["moe", 1] = _at


def slot_of(at):
    return at % NSLOT


def fills(at):
    return 16 * (at // NSLOT + 1)


def psum_plan():
    plan, count, at = {}, [0] * 8, [0]

    def use(name, bank=None):
        if bank is None:
            bank = at[0] % 8
            at[0] += 1
        plan[name] = (bank, count[bank])
        count[bank] += 1

    for k in range(KD):
        use(("x", k))
    for l in range(DEPTH):
        for j in range(16):
            use(("mod", l, j))
            if j:
                use(("modT", l, j - 1))
        use(("modT", l, 15))
        use(("ss", l, "n1"))
        for j in range(NP):
            use(("p", l, j))
        for s in ("ckv", "kpe", "cq"):
            use(("ss", l, s))
        use(("rotk", l))
        for h in range(HEADS):
            use(("vt", l, h))
        for j in range(3):
            use(("cache", l, j))
        for h in range(HEADS):
            use(("kd", l, h))
        for h in range(HEADS):
            use(("sc", l, h))
        for h in range(HEADS):
            use(("o", l, h), h)
        for c in range(NC_):
            use(("u", l, c), 4 + c % 4)
        for h in range(HEADS):
            use(("ss", l, "o%d" % h), 4 + h)
        for j in range(6):
            use(("q", l, j))
            if j:
                use(("ss", l, "q%d" % (j - 1)))
        use(("ss", l, "q5"))
        for j in range(2):
            use(("rotq", l, j))
        for j in range(8):
            use(("k", l, j))
            if j:
                use(("ss", l, "k%d" % (j - 1)))
        use(("ss", l, "k7"))
        for b in range(5):
            use(("v", l, b))
        for g in range(3):
            use(("ckvo", l, g))
        for h in range(HEADS):
            use(("oT", l, h), h % 2)
            for b in range(3):
                use(("s", l, h, b), 2 + (3 * h + b) % 3)
                use(("pT", l, h, b), 5 + (3 * h + b) % 3)
        use(("ss", l, "om"))
        for k in range(KD):
            use(("wo", l, k))
        use(("ss", l, "n2"))
        if l == 0:
            for k in range(KD):
                use(("down", k))
        else:
            for g in range(3):
                for f in range(2):
                    use(("ht", g, f))
            use(("logits",))
            use(("rank",))
    for g in range(3):
        for f in range(2):
            use(("y", g, f))
    return plan, count


def build(nc, consts, vecs, cond, x_in, state_in, cache_in, w_ada, w_win, w_wqb, w_wkvb, w_wo,
          w_up, w_down, w_router, w_moe, y_out, s_out, kv_out):
    PLAN, _ = psum_plan()
    ctx = ExitStack()
    with ctx:
        scope = [ctx]

        def sb(name, cols, dt=F32):
            return scope[0].enter_context(nc.sbuf_tensor(name, [128, cols], dt))

        sems = {}

        def sem(name):
            if name not in sems:
                sems[name] = ctx.enter_context(nc.semaphore(name))
            return sems[name]

        cst = sb("cst", NCST)
        vec = sb("vec", DEPTH * NV)
        xT = sb("xT", KD * T)
        hT = sb("hT", KD * T)
        misc = sb("misc", 580)
        scond = sb("scond", KD * 32)[:, :].rearrange("p (k g) -> p k g", g=32)
        scope[0] = ExitStack()
        ring = sb("ring", NSLOT * SLOTW)
        arena = sb("arena", ARENA)
        ktil = sb("ktil", NB_ * T)

        arena_at = [0]

        def cut(cols, at=None):
            if at is None:
                at = arena_at[0]
                arena_at[0] += cols
            assert at + cols <= ARENA, at + cols
            return arena[:, at:at + cols]

        def tiles(ap, n):
            return ap.rearrange("p (n t) -> p n t", n=n)

        proj_f = cut(NP * T)
        proj = tiles(proj_f, NP)
        kf, qf = proj_f[:, PF * T:(PF + 4) * T], proj_f[:, PQ * T:(PQ + 4) * T]
        ckv_all = tiles(cut(2 * KEYS), 2)
        kpe_all = cut(KEYS)
        qpe = tiles(cut(2 * T), 2)
        bcum = cut(HEADS * T)
        tmp = cut(HEADS * T)
        qt_f = cut(HEADS * T)
        tok0 = arena_at[0]
        kd_tok = tiles(cut(3 * 512), 3)
        v_tok = tiles(cut(3 * 512), 3)
        sq4 = tiles(cut(4 * T), 4)
        kn = tiles(cut(HEADS * KEYS, 0), HEADS)
        vals = tiles(cut(5 * 512, tok0), 5)
        qn = tiles(qt_f, HEADS)
        sT = tiles(tmp, HEADS)
        qt = tiles(qt_f, HEADS)
        sq8_f = cut(KD * T, 0)
        x_tok = tiles(cut(3 * D, 0), 3)
        aT = tiles(cut(NF * T, 0), NF)
        sig_up = tiles(cut(2 * T, NF * T), 2)
        rot_tmp = sb("rot_tmp", T)
        sq1 = tiles(sb("sq1", 2 * T)[:, :], 2)
        rstd = tiles(sb("rstd", 2 * T)[:, :], 2)
        sg1 = tiles(sb("sg1", 2 * T)[:, :], 2)
        states = tiles(sb("states", 2 * 512)[:, :], 2)
        s_smp = sb("s_smp", 512)
        s_new = sb("s_new", 512)
        cache_tok = tiles(sb("cache_tok", 2 * 384)[:, :], 2)
        probs = tiles(sb("probs", 2 * T)[:, :], 2)
        pT = tiles(sb("pT", 2 * T)[:, :], 2)
        kv_tok = tiles(sb("kv_tok", 2 * 384)[:, :], 2)
        ref = misc[:, 288:288 + HEADS * T // SUB]
        scope[0].close()
        scope[0] = ctx
        xring = sb("xring", XSLOT * SLOTW)
        w_hi = tiles(sb("w_hi", 2 * 2 * D, F32R)[:, :], 2)
        w_lo = tiles(sb("w_lo", 2 * 2 * D, F32R)[:, :], 2)
        wd_hi = tiles(sb("wd_hi", 4 * D, F32R)[:, :], 4)
        wd_lo = tiles(sb("wd_lo", 4 * D, F32R)[:, :], 4)
        hg_hi = tiles(sb("hg_hi", D, F32R)[:, :], KD)
        hg_lo = tiles(sb("hg_lo", D, F32R)[:, :], KD)
        at_hi = tiles(sb("at_hi", 4 * 128, F32R)[:, :], 4)
        at_lo = tiles(sb("at_lo", 4 * 128, F32R)[:, :], 4)
        sgX = tiles(sb("sgX", 2 * 128)[:, :], 2)
        aX = tiles(sb("aX", 2 * 128)[:, :], 2)
        h_tok = tiles(sb("h_tok", 3 * D)[:, :], 3)
        y_tok = h_tok
        ysb = sb("ysb", D)
        acc = tiles(hT[:, :], KD)
        pick = tiles(sb("pick", 3 * 128)[:, :], 3)
        pickg = tiles(sb("pickg", 3 * 128)[:, :], 3)
        gT = sb("gT", T)[:, :]
        cmp8, cmp8b = sb("cmp8", 3 * 64)[:, :], sb("cmp8b", 3 * 64)[:, :]
        cmpi, cmpi2 = sb("cmpi", ITEMS * NX)[:, :], sb("cmpi2", ITEMS * NX)[:, :]
        router = tiles(sb("router", KD * NX)[:, :], KD)
        rt = sb("rt", 272)

        mods = misc[:, 0:96].rearrange("p (f g) -> p f g", g=2)
        gain = misc[:, 96:128].rearrange("p (n k g) -> p n k g", n=2, g=2)
        condT = misc[:, 128:144].rearrange("p (k g) -> p k g", g=2)
        eps = misc[:, 160:161]
        lbw = misc[:, 164:184]
        oml = misc[:, 184:192].rearrange("p (l h) -> p l h", l=2)
        rowmax = misc[:, 192:216]
        negmax = misc[:, 216:240]
        rowsum = misc[:, 240:264]
        rinv = misc[:, 264:288]
        ids = ctx.enter_context(nc.sbuf_tensor("ids", [128, 16], I32))

        banks = [ctx.enter_context(nc.psum_tensor("bank%d" % b, [128, 512], F32)) for b in range(8)]
        bank_full = [sem("bank_full%d" % b) for b in range(8)]
        bank_free = [sem("bank_free%d" % b) for b in range(8)]
        slot_full = [sem("slot_full%d" % s) for s in range(NSLOT)]
        xslot_full = [sem("xslot_full%d" % s) for s in range(XSLOT)]

        ident, ones, ones64 = cst[:, CI:CI + 128], cst[:, CO:CO + 128], cst[:, CO64:CO64 + 128]
        rot, cos, sin = cst[:, CROT:CROT + 128], cst[:, CCOS:CCOS + T], cst[:, CSIN:CSIN + T]

        def V(l, col, n=1):
            return vec[:, l * NV + col:l * NV + col + n]

        def kt_buf(h):
            return ktil if h % 2 == 0 else hT

        def ps(name):
            return banks[PLAN[name][0]]

        def take(eng, name):
            b, n = PLAN[name]
            eng.wait_ge(bank_full[b], n + 1)

        def done(ins, name):
            ins.then_inc(bank_free[PLAN[name][0]], 1)

        def await_done(eng, name):
            b, n = PLAN[name]
            eng.wait_ge(bank_free[b], n + 1)

        rms_order = []
        for l in range(DEPTH):
            rms_order += [(l, s) for s in ["n1", "ckv", "kpe", "cq"] + ["o%d" % h for h in range(4)]
                          + ["q%d" % j for j in range(6)] + ["k%d" % j for j in range(8)] + ["om", "n2"]]
        RMS = {n: i for i, n in enumerate(rms_order)}
        squares_ready, rstd_ready, normed = sem("squares_ready"), sem("rstd_ready"), sem("normed")
        def used_up(at):
            name, l, first = max(((n, l, f) for (n, l), f in START.items() if f <= at), key=lambda x: x[2])
            j = at - first
            if name == "up":
                return sem("gu_full"), j + 1
            last = {"ada": ("mod", l, j), "win": ("p", l, 2 * j + 1), "wqb": ("q", l, 5), "wkvb": ("v", l, 4),
                    "wo": ("wo", l, 2 * j + 1), "down": ("down", j)}[name]
            b, n = PLAN[last]
            return bank_full[b], n + 1

        QB = ((0, 128, 0, 128), (0, 256, 128, 128), (SEQ, T, SEQ, DEC))
        VBLK = ((0, 128), (128, 128), (256, 32), (288, 128), (416, 128))
        BLK_OF = ((0,), (0, 1), (2, 3, 4))
        block = ctx.enter_context(nc.Block())

        @block.sync
        def _(sp):
            sp.dma_start(cst[:, :], consts).then_inc(sem("consts_loaded"), 16)
            sp.dma_start(misc[:, 128:144], cond).then_inc(sem("cond_loaded"), 16)
            sp.dma_start(vec[:, :], vecs).then_inc(sem("vecs_loaded"), 16)
            for g, (t0, n) in enumerate(TB):
                sp.dma_start(x_tok[0:n, g, :], x_in[t0:t0 + n, :]).then_inc(sem("x_loaded"), 16)

            def slab(at, src, width):
                if at >= NSLOT:
                    sp.wait_ge(*used_up(at - NSLOT))
                sp.dma_start(ring[:, slot_of(at) * SLOTW:slot_of(at) * SLOTW + width], src
                             ).then_inc(slot_full[slot_of(at)], 16)

            src = {"ada": w_ada, "win": w_win, "wqb": w_wqb, "wkvb": w_wkvb, "wo": w_wo,
                   "up": w_up, "down": w_down}
            for name, l, k, w in STREAM:
                first = START[name, l]
                for j in range(k):
                    a = src[name][l, j] if name not in ("up", "down") else src[name][j]
                    slab(first + j, a, w)
            sp.wait_ge(*used_up(START["moe", 1] - 1))
            sp.sem_inc(sem("lo_done"), 3 * XSLOT)

            def expert_slabs(i, q, base):
                for j in range(XSLOT):
                    sp.wait_ge(sem("lo_done"), i * (3 * NFX) + q * (3 * XSLOT) + (3 * j + 3))
                    sp.dma_start(xring[:, j * SLOTW:(j + 1) * SLOTW],
                                 w_moe[bass.ds(base + q * XSLOT + j, 1)].rearrange("a p n -> (a p) n")
                                 ).then_inc(xslot_full[j], 16)

            for j in range(XSLOT):
                sp.dma_start(xring[:, j * SLOTW:(j + 1) * SLOTW], w_moe[j]).then_inc(xslot_full[j], 16)
            with sp.Fori(1, NFX // XSLOT) as q:
                expert_slabs(0, q, 0)
            sp.wait_ge(sem("ids_ready"), 1)
            n_items = sp.value_load(ids[0:1, ITEMS:ITEMS + 1], min_val=NX, max_val=ITEMS)
            with sp.Fori(1, n_items) as i:
                e = sp.value_load(ids[0:1, bass.ds(i, 1)], min_val=0, max_val=NX - 1)
                with sp.Fori(0, NFX // XSLOT) as q:
                    expert_slabs(i, q, e * NFX)

        @block.tensor
        def _(pe):
            mm = nc.tensor.matmul

            def use(name):
                b, n = PLAN[name]
                if n:
                    pe.wait_ge(bank_free[b], n)
                return banks[b]

            def full(ins, name):
                ins.then_inc(bank_full[PLAN[name][0]], 1)

            def slab(at, width):
                pe.wait_ge(slot_full[slot_of(at)], fills(at))
                return ring[:, slot_of(at) * SLOTW:slot_of(at) * SLOTW + width]

            def sum_squares(l, name, src, mat=ones):
                o = use(("ss", l, name))
                pe.wait_ge(squares_ready, RMS[l, name] + 1)
                for k, a in enumerate(src):
                    last = mm(o[:, 0:a.shape[1]], mat, a, start=k == 0, stop=k == len(src) - 1)
                full(last, ("ss", l, name))

            pe.wait_ge(sem("consts_loaded"), 16)
            pe.wait_ge(sem("x_loaded"), 48)
            for k in range(KD):
                o = use(("x", k))
                for g, (t0, n) in enumerate(TB):
                    last = nc.tensor.transpose(o[:, t0:t0 + n], x_tok[0:n, g, 128 * k:128 * k + 128], ident[0:n, 0:n])
                full(last, ("x", k))
            pe.wait_ge(sem("cond_silu"), 1)
            for l in range(DEPTH):
                def turn_mod(j):
                    o = use(("modT", l, j))
                    pe.wait_ge(sem("modrow_ready"), 16 * l + j + 1)
                    for f in range(3):
                        last = nc.tensor.transpose(o[:, 128 * f:128 * f + 128], kv_tok[:, j % 2, 128 * f:128 * f + 128], ident)
                    full(last, ("modT", l, j))

                for j in range(16):
                    o = use(("mod", l, j))
                    w = slab(START["ada", l] + j, 3072).rearrange("p (k n) -> p k n", k=KD)
                    for k in range(KD):
                        r = 32 * (k % 4)
                        last = mm(o[r:r + 32, 0:384], scond[:, k, :], w[:, k], start=k < 4, stop=k >= 4)
                    full(last, ("mod", l, j))
                    if j:
                        turn_mod(j - 1)
                turn_mod(15)
                sum_squares(l, "n1", [sq8_f[:, k * T:(k + 1) * T] for k in range(KD)])
                pe.wait_ge(sem("h1_ready"), l + 1)
                for j in range(NP):
                    o = use(("p", l, j))
                    w = slab(START["win", l] + j // 2, 2048).rearrange("p (f k n) -> p f k n", f=2, k=KD)
                    for k in range(KD):
                        last = mm(o[:, 0:T], w[:, j % 2, k], hT[:, k * T:(k + 1) * T], start=k == 0, stop=k == KD - 1)
                    full(last, ("p", l, j))
                sum_squares(l, "ckv", [sq4[:, k] for k in range(2)])
                sum_squares(l, "kpe", [sq1[:, 0]], ones64)
                sum_squares(l, "cq", [sq4[:, k] for k in range(3)])
                o = use(("rotk", l))
                pe.wait_ge(normed, RMS[l, "kpe"] + 1)
                full(mm(o[:, 0:T], rot, kpe_all[:, 0:T], start=True, stop=True), ("rotk", l))
                for h in range(HEADS):
                    o = use(("vt", l, h))
                    await_done(pe, ("p", l, PI + h))
                    for g, (t0, n) in enumerate(TB):
                        last = nc.tensor.transpose(o[0:n, 128 * g:128 * g + 128], proj[:, PI + h, t0:t0 + n], ident)
                    full(last, ("vt", l, h))
                pe.wait_ge(sem("cache_loaded"), 48 * (l + 1))
                for j in range(3):
                    o = use(("cache", l, j))
                    for b in range(2):
                        last = nc.tensor.transpose(o[:, 128 * b:128 * b + 128], cache_tok[:, b, 128 * j:128 * j + 128], ident)
                    full(last, ("cache", l, j))
                pe.wait_ge(sem("kd_ready"), l + 1)
                for h in range(HEADS):
                    o = use(("kd", l, h))
                    for g, (t0, n) in enumerate(TB):
                        last = nc.tensor.transpose(o[0:n, 128 * g:128 * g + 128],
                                                   tmp[:, h * T + t0:h * T + t0 + n], ident)
                    full(last, ("kd", l, h))
                for h in range(HEADS):
                    o = use(("sc", l, h))
                    pe.wait_ge(sem("kt_ready"), 4 * l + h + 1)
                    for g, (t0, n) in enumerate(TB):
                        for b in range(NB_):
                            dst = o[0:n, t0:t0 + n].rearrange("p (c b s) -> p c b s", b=NB_, s=SUB)[:, :, b, :]
                            q = qt[:, h, t0:t0 + n].rearrange("p (c b s) -> p c b s", b=NB_, s=SUB)[:, :, b, :]
                            last = mm(dst, kt_buf(h)[:, b * T + t0:b * T + t0 + n], q, start=True, stop=True)
                    full(last, ("sc", l, h))
                for h in range(HEADS):
                    o = use(("o", l, h))
                    await_done(pe, ("sc", l, h))
                    if h == 0:
                        pe.wait_ge(sem("v_tok_ready"), 8 * (l + 1))
                    for g, (t0, n) in enumerate(TB):
                        mm(o[:, t0:t0 + n], v_tok[0:n, g, 128 * h:128 * h + 128], sT[0:n, h, t0:t0 + n],
                           start=g == 0, stop=False, skip_group_check=True)
                pe.wait_ge(sem("kd_tok_ready"), 8 * (l + 1))
                pe.wait_ge(sem("qe_ready"), l + 1)

                def inter(c):
                    if c < NC_ - 1:
                        pe.wait_ge(sem("state_ready"), 8 * l + c)
                        s = states[:, c % 2]
                    else:
                        pe.wait_ge(sem("state_loaded"), 16 * (l + 1))
                        s = s_smp
                    for h in range(HEADS):
                        last = mm(banks[h][:, CH * c:CH * c + CH], s[:, 128 * h:128 * h + 128],
                                  qf[:, h * T + CH * c:h * T + CH * c + CH],
                                  start=False, stop=True, skip_group_check=True)
                        if c == NC_ - 1:
                            full(last, ("o", l, h))
                    if c < NC_ - 1:
                        last.then_inc(sem("state_used"), 1)

                for c in range(NC_):
                    o = use(("u", l, c))
                    g, r = divmod(CH * c, 128)
                    for h in range(HEADS):
                        last = mm(o[:, 128 * h:128 * h + 128], kd_tok[r:r + CH, g, 128 * h:128 * h + 128],
                                  v_tok[r:r + CH, g, 128 * h:128 * h + 128], start=True, stop=True)
                    full(last, ("u", l, c))
                    if c >= 2:
                        inter(c - 1)
                inter(NC_ - 1)
                for h in range(HEADS):
                    sum_squares(l, "o%d" % h, [sq1[:, RMS[l, "o%d" % h] % 2]])
                wq = slab(START["wqb", l], 2304).rearrange("p (k n) -> p k n", k=3)
                pe.wait_ge(normed, RMS[l, "cq"] + 1)
                for j in range(6):
                    o = use(("q", l, j))
                    for k in range(3):
                        last = mm(o[:, 0:T], wq[:, k, 128 * j:128 * j + 128], proj[:, PCQ + k, :],
                                  start=k == 0, stop=k == 2)
                    full(last, ("q", l, j))
                    if j:
                        sum_squares(l, "q%d" % (j - 1), [sq1[:, RMS[l, "q%d" % (j - 1)] % 2]],
                                    ones64 if j - 1 >= 4 else ones)
                sum_squares(l, "q5", [sq1[:, RMS[l, "q5"] % 2]], ones64)
                for j in range(2):
                    o = use(("rotq", l, j))
                    pe.wait_ge(normed, RMS[l, "q%d" % (4 + j)] + 1)
                    full(mm(o[:, 0:T], rot, qpe[:, j, :], start=True, stop=True), ("rotq", l, j))
                wk = slab(START["wkvb", l], 2048).rearrange("p (k n) -> p k n", k=2)
                pe.wait_ge(sem("ckv_all_ready"), 2 * (l + 1))
                for j in range(8):
                    h, (t0, n) = j // 2, ((0, T), (T, PAST))[j % 2]
                    o = use(("k", l, j))
                    for k in range(2):
                        last = mm(o[:, 0:n], wk[:, k, 128 * h:128 * h + 128], ckv_all[:, k, t0:t0 + n],
                                  start=k == 0, stop=k == 1)
                    full(last, ("k", l, j))
                    if j:
                        sum_squares(l, "k%d" % (j - 1), [sq1[:, RMS[l, "k%d" % (j - 1)] % 2, 0:(T, PAST)[(j - 1) % 2]]])
                sum_squares(l, "k7", [sq1[:, RMS[l, "k7"] % 2, 0:PAST]])
                for b, (t0, n) in enumerate(VBLK):
                    o = use(("v", l, b))
                    for k in range(2):
                        last = mm(o[0:n, :], ckv_all[:, k, t0:t0 + n], wk[:, k, 512:1024], start=k == 0, stop=k == 1)
                    full(last, ("v", l, b))
                pe.wait_ge(sem("kpe_ready"), l + 1)
                for g, (t0, n) in enumerate(TB):
                    o = use(("ckvo", l, g))
                    for k in range(2):
                        nc.tensor.transpose(o[0:n, 128 * k:128 * k + 128], ckv_all[:, k, t0:t0 + n], ident)
                    full(nc.tensor.transpose(o[0:n, 256:384], kpe_all[:, t0:t0 + n], ident), ("ckvo", l, g))
                pe.wait_ge(sem("qpe_ready"), 2 * (l + 1))
                pe.wait_ge(normed, RMS[l, "k7"] + 1)
                pe.wait_ge(sem("vals_ready"), 5 * (l + 1))

                def scores(h, b):
                    k0, nk, q0, nq = QB[b]
                    o = use(("s", l, h, b))
                    r = 64 * (h % 2)
                    mm(o[0:nq, 0:nk], qn[:, h, q0:q0 + nq], kn[:, h, k0:k0 + nk], start=True, stop=False)
                    if b < 2:
                        mm(o[0:nq, nk - 128:nk], cst[0:1, CMQ:CMQ + 128], cst[0:1, CMK:CMK + 128],
                           start=False, stop=False, skip_group_check=True)
                    last = mm(o[0:nq, 0:nk], qpe[r:r + 64, h // 2, q0:q0 + nq], kpe_all[r:r + 64, k0:k0 + nk],
                              start=False, stop=True)
                    full(last, ("s", l, h, b))

                def mix(h, b):
                    k0, nk, q0, nq = QB[b]
                    i = 3 * h + b
                    o = use(("pT", l, h, b))
                    pe.wait_ge(sem("probs_ready"), 12 * l + i + 1)
                    for n_, kb in enumerate(BLK_OF[b]):
                        t0, n = VBLK[kb]
                        last = nc.tensor.transpose(o[0:n, nq * n_:nq * n_ + nq], probs[0:nq, i % 2, t0 - k0:t0 - k0 + n],
                                                   ident[0:nq, 0:nq])
                    full(last, ("pT", l, h, b))

                def weigh(h, b):
                    k0, nk, q0, nq = QB[b]
                    i = 3 * h + b
                    o = use(("oT", l, h)) if b == 0 else ps(("oT", l, h))
                    pe.wait_ge(sem("pT_ready"), 12 * l + i + 1)
                    for n_, kb in enumerate(BLK_OF[b]):
                        t0, n = VBLK[kb]
                        last = mm(o[:, q0:q0 + nq], vals[0:n, kb, 128 * h:128 * h + 128],
                                  pT[0:n, i % 2, nq * n_:nq * n_ + nq],
                                  start=n_ == 0, stop=n_ == len(BLK_OF[b]) - 1)
                    if b == 2:
                        full(last, ("oT", l, h))

                todo = [(h, b) for h in range(HEADS) for b in range(3)]
                for i in range(14):
                    if i < 12:
                        scores(*todo[i])
                    if 1 <= i < 13:
                        mix(*todo[i - 1])
                    if i >= 2:
                        weigh(*todo[i - 2])
                sum_squares(l, "om", [sq4[:, k] for k in range(4)])
                pe.wait_ge(sem("mix_ready"), 5 * (l + 1))
                for k in range(KD):
                    o = use(("wo", l, k))
                    w = slab(START["wo", l] + k // 2, 2048).rearrange("p (f k n) -> p f k n", f=2, k=KD)
                    for j in range(8):
                        m = proj[:, (PG + j) if j < 4 else (PI + j - 4), :]
                        last = mm(o[:, 0:T], w[:, k % 2, j], m, start=j == 0, stop=j == 7)
                    full(last, ("wo", l, k))
                sum_squares(l, "n2", [sq8_f[:, k * T:(k + 1) * T] for k in range(KD)])
                pe.wait_ge(sem("h2_ready"), l + 1)
                if l == 0:
                    for b in range(8):
                        n = min(n for nm, (bb, n) in PLAN.items() if bb == b and (nm[0] == "down" or nm[1:2] == (1,)))
                        pe.wait_ge(bank_free[b], n)

                    def up(at, q, j):
                        s = slot_of(at + j)
                        pe.wait_ge(sem("gu_read"), q * NSLOT + j + 1)
                        pe.wait_ge(slot_full[s], q * 16 + fills(at + j))
                        w = ring[:, s * SLOTW:s * SLOTW + 2048].rearrange("p (h k n) -> p h k n", h=2, k=KD)
                        for u in range(2):
                            for k in range(KD):
                                last = mm(banks[2 * (j % 3) + u][:, 0:T], w[:, u, k], hT[:, k * T:(k + 1) * T],
                                          start=k == 0, stop=k == KD - 1)
                        last.then_inc(sem("gu_full"), 1)

                    with pe.Fori(0, NF // NSLOT) as q:
                        for j in range(NSLOT):
                            up(START["up", 0], q, j)
                    for j in range(NF % NSLOT):
                        up(START["up", 0], NF // NSLOT, j)
                    pe.wait_ge(sem("gu_read"), NF + 3)
                    for k in range(KD):
                        o = use(("down", k))
                        w = slab(START["down", 0] + k, FF).rearrange("p (f n) -> p f n", f=NF)
                        for f in range(NF):
                            last = mm(o[:, 0:T], w[:, f], aT[:, f], start=f == 0, stop=f == NF - 1)
                        full(last, ("down", k))
            for g, (t0, n) in enumerate(TB):
                for f in range(2):
                    o = use(("ht", g, f))
                    for k in range(4):
                        last = nc.tensor.transpose(o[0:n, 128 * k:128 * k + 128],
                                                   hT[:, (4 * f + k) * T + t0:(4 * f + k) * T + t0 + n], ident)
                    full(last, ("ht", g, f))
            o = use(("logits",))
            pe.wait_ge(sem("router_loaded"), 16)
            for g, (t0, n) in enumerate(TB):
                for k in range(KD):
                    last = mm(o[0:n, NX * g:NX * g + NX], hT[:, k * T + t0:k * T + t0 + n], router[:, k],
                              start=k == 0, stop=k == KD - 1)
            full(last, ("logits",))
            o = use(("rank",))
            pe.wait_ge(sem("chosen_ready"), 1)
            chosen = rt[:, 24:48].rearrange("p (g e) -> p g e", g=3)
            for g in range(3):
                for b in range(g + 1):
                    mm(o[:, NX * g:NX * g + NX], cst[:, CU:CU + 128] if b == g else ones, chosen[:, b],
                       start=b == 0, stop=b == g)
            for b in range(3):
                last = mm(o[:, 24:32], ones, chosen[:, b], start=b == 0, stop=b == 2)
            full(last, ("rank",))
            for b in range(8):
                n = max(n for nm, (bb, n) in PLAN.items() if bb == b and nm[0] != "y")
                pe.wait_ge(bank_free[b], n + 1)
            pe.wait_ge(sem("ids_ready"), 1)
            last_item = pe.value_load(ids[0:1, ITEMS + 1:ITEMS + 2], min_val=NX - 1, max_val=ITEMS - 1)
            pe.sem_inc(sem("down_done"), XSLOT)

            def gather(i):
                pe.wait_ge(sem("pick_ready"), i + 1)
                pe.wait_ge(sem("scatter_read"), i * KD + KD)
                pe.wait_ge(sem("gates_ready"), i + 1)
                for k in range(KD):
                    for g, (t0, n) in enumerate(TB):
                        last = mm(banks[6 + k // 4][:, 128 * (k % 4):128 * (k % 4) + 128],
                                  h_tok[0:n, g, 128 * k:128 * k + 128], pick[0:n, g, :], start=g == 0, stop=g == 2)
                    if k % 4 == 3:
                        last.then_inc(sem("gathered"), 1)

            def scatter(i, some=range(KD)):
                pe.wait_ge(sem("y_lo_ready"), i + 1)
                pe.wait_ge(sem("y_hi_ready"), i + 1)
                pe.wait_ge(sem("gates_ready"), i + 1)
                for k in some:
                    if k >= 2:
                        pe.wait_ge(sem("scatter_read"), i * KD + (KD + k - 1))
                    mm(banks[6 + k % 2][:, 0:T], ysb[:, 128 * k:128 * k + 128], gT, start=True, stop=True
                       ).then_inc(sem("scattered"), 1)

            def gates(i):
                pe.wait_ge(sem("pickg_ready"), i + 1)
                pe.wait_ge(sem("scatter_read"), i * KD + (2 * KD - 1))
                for g, (t0, n) in enumerate(TB):
                    last = nc.tensor.transpose(banks[6][:, t0:t0 + n], pickg[0:n, g, :], ident[0:n, 0:n])
                last.then_inc(sem("gates_turned"), 1)

            def item(i, more):
                pe.wait_ge(sem("hg_split"), i * 2 + 2)

                def gate_up(q, j):
                    pe.wait_ge(sem("lo_done"), i * (3 * NFX) + q * (3 * XSLOT) + (3 * j + 14))
                    pe.wait_ge(sem("at_split"), i * NFX + q * XSLOT + (j + 1))
                    for k in range(KD):
                        cols = slice(256 * k, 256 * k + 256)
                        mm(banks[j][:, 0:256], hg_hi[:, k], w_hi[:, j % 2, cols], start=k == 0, stop=False)
                        mm(banks[j][:, 0:256], hg_hi[:, k], w_lo[:, j % 2, cols], start=False, stop=False)
                        last = mm(banks[j][:, 0:256], hg_lo[:, k], w_hi[:, j % 2, cols], start=False, stop=k == KD - 1)
                    last.then_inc(sem("gate_up_full"), 1)

                def turn(q, j):
                    pe.wait_ge(sem("a_ready"), i * NFX + q * XSLOT + (j + 3))
                    nc.tensor.transpose(banks[j % 4][:, 256:384], aX[:, j % 2], ident).then_inc(sem("turned"), 1)

                def down(q, j, first=False):
                    pe.wait_ge(sem("at_split"), i * NFX + q * XSLOT + (j + 5))
                    pe.wait_ge(sem("lo_done"), i * (3 * NFX) + q * (3 * XSLOT) + (3 * j + 15))
                    for n, (a, w) in enumerate(((at_hi, wd_hi), (at_hi, wd_lo), (at_lo, wd_hi))):
                        for u in range(2):
                            last = mm(banks[4 + u][:, :], a[:, j % 4], w[:, j % 4, 512 * u:512 * u + 512],
                                      start=first and n == 0, stop=False, skip_group_check=True)
                    last.then_inc(sem("down_done"), 1)

                for j in range(4):
                    gate_up(0, j)
                    if j >= 1:
                        turn(0, j - 1)
                    scatter(i, SCATTER[j])
                    if j == 3:
                        gates(i)
                    if j >= 2:
                        down(0, j - 2, first=j == 2)
                with pe.Fori(1, NFX // XSLOT) as q:
                    for j in range(4):
                        gate_up(q, j)
                        turn(q, j - 1)
                        down(q, j - 2)
                if more:
                    gather(i + 1)
                turn(NFX // XSLOT, -1)
                down(NFX // XSLOT, -2)
                down(NFX // XSLOT, -1)

            gather(0)
            with pe.Fori(0, last_item) as i:
                item(i, True)
            item(last_item, False)
            scatter(last_item + 1)
            pe.wait_ge(sem("y_final"), KD)
            for g, (t0, n) in enumerate(TB):
                for f in range(2):
                    o = use(("y", g, f))
                    for k in range(4):
                        last = nc.tensor.transpose(o[0:n, 128 * k:128 * k + 128],
                                                   xT[:, (4 * f + k) * T + t0:(4 * f + k) * T + t0 + n], ident)
                    full(last, ("y", g, f))

        @block.scalar
        def _(act):
            A = nc.scalar.activation
            own = [0]

            def link(ins):
                own[0] += 1
                ins.then_inc(sem("scalar_step"), 1)
                act.wait_ge(sem("scalar_step"), own[0])

            def finish_norm(l, name, n, cols=T):
                r = RMS[l, name]
                dst = rstd[:, r % 2, 0:cols]
                if r >= 2:
                    act.wait_ge(normed, r - 1)
                take(act, ("ss", l, name))
                done(A(dst, ps(("ss", l, name))[:, 0:cols], ACT.Ln, bias=eps, scale=1.0 / n), ("ss", l, name))
                await_done(act, ("ss", l, name))
                A(dst, dst, ACT.Exp, scale=-0.5).then_inc(rstd_ready, 1)

            act.wait_ge(sem("cond_loaded"), 16)
            act.wait_ge(sem("scond_cleared"), 1)
            A(scond[:, :, 0:2], condT, ACT.Silu).then_inc(sem("cond_silu"), 1)
            for l in range(DEPTH):
                nc.scalar.preload_act_table_set("natural_log_exp_and_others")
                if l == 0:
                    act.wait_ge(sem("lb_diff"), 1)
                    A(lbw[:, 12:20], lbw[:, 4:12], ACT.Exp).then_inc(sem("lb_exp"), 1)
                    act.wait_ge(sem("xT_ready"), KD)
                    act.wait_ge(sem("eps_ready"), 1)
                else:
                    act.wait_ge(sem("ffn_x_ready"), KD)
                A(sq8_f, xT[:, :], ACT.Square).then_inc(squares_ready, 1)
                finish_norm(l, "n1", D)
                nc.scalar.preload_act_table_set("sigmoid_and_others")
                for j in range(PI):
                    name = ("p", l, j)
                    take(act, name)
                    if j < PQ:
                        done(A(proj[:, j], ps(name)[:, 0:T], ACT.Sigmoid, scale=-1.0), name)
                    else:
                        i = j - PQ
                        if 8 * l + i >= 2:
                            act.wait_ge(sem("silu_done"), 8 * l + i - 1)
                        A(sg1[:, i % 2], ps(name)[:, 0:T], ACT.Sigmoid).then_inc(sem("sigmoid_ready"), 1)
                nc.scalar.preload_act_table_set("natural_log_exp_and_others")

                def plain(tiles_):
                    for j in tiles_:
                        take(act, ("p", l, j))
                        done(A(proj[:, j], ps(("p", l, j))[:, 0:T], ACT.Copy), ("p", l, j))

                def key_decays(h):
                    act.wait_ge(sem("diff_ready"), 6 * l + 3 + h)
                    for b in range(NB_):
                        e = kt_buf(h)[:, b * T:(b + 1) * T].rearrange("p (c s) -> p c s", s=CH)[:, :, 0:SUB * (b + 1)]
                        last = A(e, e, ACT.Exp)
                    last.then_inc(sem("diff_exp"), 1)

                act.wait_ge(sem("k_ready"), 4 * (l + 1))
                A(tmp, kf, ACT.Ln, scale=-1.0, bias=1.0).then_inc(sem("logf_ready"), 1)
                plain(range(PI, PI + 2))
                act.wait_ge(sem("diff_ready"), 6 * l + 1)
                A(tmp, tmp, ACT.Exp).then_inc(sem("diff_exp"), 1)
                plain(range(PI + 2, PI + 3))
                act.wait_ge(sem("diff_ready"), 6 * l + 2)
                A(tmp, tmp, ACT.Exp).then_inc(sem("diff_exp"), 1)
                plain(range(PI + 3, PC + 1))
                key_decays(0)
                plain(range(PC + 1, NP))
                for j in (PC, PC + 1, PK, PCQ, PCQ + 1, PCQ + 2):
                    await_done(act, ("p", l, j))
                A(sq4[:, 0:2], proj[:, PC:PC + 2], ACT.Square).then_inc(squares_ready, 1)
                A(sq1[:, 0], proj[:, PK], ACT.Square).then_inc(squares_ready, 1)
                finish_norm(l, "ckv", KVL)
                A(sq4[:, 0:3], proj[:, PCQ:PCQ + 3], ACT.Square).then_inc(squares_ready, 1)
                finish_norm(l, "kpe", ROPE)
                finish_norm(l, "cq", QL)
                for h in range(1, HEADS):
                    key_decays(h)
                A(bcum, bcum, ACT.Exp).then_inc(sem("eb_ready"), 1)
                for h in range(HEADS):
                    name = "o%d" % h
                    r = RMS[l, name]
                    take(act, ("o", l, h))
                    A(sq1[:, r % 2], ps(("o", l, h))[:, 0:T], ACT.Square).then_inc(squares_ready, 1)
                    if h:
                        finish_norm(l, "o%d" % (h - 1), 128)
                finish_norm(l, "o3", 128)
                for pre, cnt, width in (("q", 6, lambda j: T), ("k", 8, lambda j: (T, PAST)[j % 2])):
                    for j in range(cnt):
                        r = RMS[l, pre + str(j)]
                        take(act, (pre, l, j))
                        A(sq1[:, r % 2, 0:width(j)], ps((pre, l, j))[:, 0:width(j)], ACT.Square).then_inc(squares_ready, 1)
                        if j:
                            finish_norm(l, pre + str(j - 1), 64 if pre == "q" and j - 1 >= 4 else 128, width(j - 1))
                    finish_norm(l, pre + str(cnt - 1), 64 if pre == "q" else 128, width(cnt - 1))
                for b, (t0, n) in enumerate(VBLK):
                    take(act, ("v", l, b))
                    A(vals[0:n, b], ps(("v", l, b))[0:n, :], ACT.Copy).then_inc(sem("vals_ready"), 1)
                    act.wait_ge(sem("vals_ready"), 5 * l + b + 1)
                    act.sem_inc(bank_free[PLAN["v", l, b][0]], 1)
                for i in range(13):
                    if i < 12:
                        h, b = divmod(i, 3)
                        k0, nk, q0, nq = QB[b]
                        name = ("s", l, h, b)
                        act.wait_ge(sem("negmax_ready"), 12 * l + i + 1)
                        A(probs[0:nq, i % 2, 0:nk], ps(name)[0:nq, 0:nk], ACT.Exp, bias=negmax[0:nq, i:i + 1],
                          scale=SCALE, accum_out=rowsum[0:nq, i:i + 1]).then_inc(sem("exp_ready"), 1)
                for h in range(HEADS):
                    act.wait_ge(sem("omla_ready"), 4 * l + h + 1)
                A(sq4[:, :], proj[:, PI:PI + 4], ACT.Square).then_inc(squares_ready, 1)
                finish_norm(l, "om", 512)
                act.wait_ge(sem("x1_ready"), KD * (l + 1))
                A(sq8_f, xT[:, :], ACT.Square).then_inc(squares_ready, 1)
                finish_norm(l, "n2", D)
                if l == 0:
                    nc.scalar.preload_act_table_set("silu_and_others")

                    def silu(q, j):
                        act.wait_ge(sem("gu_full"), q * NSLOT + j + 1)
                        act.wait_ge(sem("gu_read"), q * NSLOT + j + 2)
                        A(sig_up[:, j % 2], banks[2 * (j % 3)][:, 0:T], ACT.Silu).then_inc(sem("silu_up"), 1)

                    with act.Fori(0, NF // NSLOT) as q:
                        for j in range(NSLOT):
                            silu(q, j)
                    for j in range(NF % NSLOT):
                        silu(NF // NSLOT, j)
            act.wait_ge(sem("logit_diff"), 1)
            nc.scalar.preload_act_table_set("exp_and_others")
            A(rt[:, 48:72], rt[:, 48:72], ACT.Exp).then_inc(sem("logit_exp"), 1)
            nc.scalar.preload_act_table_set("silu_and_others")

            def split_hi(i, q, j):
                s = j % 4 * SLOTW
                act.wait_ge(xslot_full[j % 4], i * (16 * NFX // XSLOT) + q * 16 + 16 * (j // 4 + 1))
                for p in range(2):
                    A(w_hi[:, j % 2, D * p:D * p + D], xring[:, s + D * p:s + D * p + D], ACT.Copy
                      ).then_inc(sem("hi_done"), 1)
                act.wait_ge(sem("down_done"), i * NFX + q * XSLOT + (j + 1))
                A(wd_hi[:, j % 4], xring[:, s + 2 * D:s + 3 * D], ACT.Copy).then_inc(sem("hi_done"), 1)

            def tokens_hi(i):
                for b in range(2):
                    act.wait_ge(sem("gathered"), i * 2 + (b + 1))
                    A(hg_hi[:, 4 * b:4 * b + 4], banks[6 + b][:, :].rearrange("p (k n) -> p k n", k=4), ACT.Copy
                      ).then_inc(sem("hg_rounded"), 1)

            def item(i, more):
                def silu(q, j):
                    act.wait_ge(sem("gate_up_full"), i * NFX + q * XSLOT + (j + 1))
                    act.wait_ge(sem("a_ready"), i * NFX + q * XSLOT + (j + 1))
                    A(sgX[:, j % 2], banks[j][:, 0:128], ACT.Silu).then_inc(sem("silu_x"), 1)

                def hidden_hi(q, j):
                    act.wait_ge(sem("turned"), i * NFX + q * XSLOT + (j + 1))
                    act.wait_ge(sem("down_done"), i * NFX + q * XSLOT + (j + 1))
                    A(at_hi[:, j % 4], banks[j % 4][:, 256:384], ACT.Copy).then_inc(sem("at_rounded"), 1)

                for j in range(4):
                    silu(0, j)
                    if j:
                        hidden_hi(0, j - 1)
                    split_hi(i, 0, j + 2)
                    if j == 3:
                        act.wait_ge(sem("gates_turned"), i + 1)
                        A(gT, banks[6][:, 0:T], ACT.Copy).then_inc(sem("gates_ready"), 1)
                with act.Fori(1, NFX // XSLOT - 1) as q:
                    for j in range(4):
                        silu(q, j)
                        hidden_hi(q, j - 1)
                        split_hi(i, q, j + 2)
                q = NFX // XSLOT - 1
                for j in range(4):
                    silu(q, j)
                    hidden_hi(q, j - 1)
                    if j < 3 and (j < 2 or more):
                        split_hi(i, q, j + 2)
                if more:
                    tokens_hi(i + 1)
                hidden_hi(q, 3)
                if more:
                    split_hi(i, q, 5)
                act.wait_ge(sem("down_done"), i * NFX + (NFX + XSLOT))
                A(ysb[:, 0:512], banks[4][:, :], ACT.Copy).then_inc(sem("y_lo_ready"), 1)

            split_hi(0, 0, 0)
            act.wait_ge(sem("ids_ready"), 1)
            last_item = act.value_load(ids[0:1, ITEMS + 1:ITEMS + 2], min_val=NX - 1, max_val=ITEMS - 1)
            tokens_hi(0)
            split_hi(0, 0, 1)
            with act.Fori(0, last_item) as i:
                item(i, True)
            item(last_item, False)

        @block.vector
        def _(dve):
            v = nc.vector
            own = [0]

            def link(ins):
                own[0] += 1
                ins.then_inc(sem("vector_step"), 1)
                dve.wait_ge(sem("vector_step"), own[0])

            def scaled(l, name, dst, src, w):
                r = RMS[l, name]
                return v.scalar_tensor_tensor(dst, src, w, rstd[:, r % 2, 0:dst.shape[-1]], ALU.mult, ALU.mult)

            def modulate(l, which, name):
                r = RMS[l, name]
                dve.wait_ge(rstd_ready, r + 1)
                for k in range(KD):
                    for g, t0, n in GRP:
                        last = v.scalar_tensor_tensor(hT[:, k * T + t0:k * T + t0 + n], xT[:, k * T + t0:k * T + t0 + n],
                                                      gain[:, which, k, g:g + 1], rstd[:, r % 2, t0:t0 + n],
                                                      ALU.mult, ALU.mult)
                last.then_inc(normed, 1)
                dve.wait_ge(normed, r + 1)
                sh = 0 if which == 0 else 24
                for k in range(KD):
                    for g, t0, n in GRP:
                        a = hT[:, k * T + t0:k * T + t0 + n]
                        last = v.tensor_scalar(a, a, mods[:, sh + k, g:g + 1], None, ALU.add)
                last.then_inc(sem("h1_ready" if which == 0 else "h2_ready"), 1)

            def mask_scores(l, h):
                name = ("sc", l, h)
                take(dve, name)
                cm = cst[:, CCM:CCM + 128]
                link(v.tensor_tensor(sT[:, h, 0:256].rearrange("p (g n) -> p g n", g=2),
                                     ps(name)[:, 0:256].rearrange("p (g n) -> p g n", g=2),
                                     cm.unsqueeze(1).to_broadcast([128, 2, 128]), ALU.mult))
                done(v.tensor_tensor(sT[0:32, h, 256:T], ps(name)[0:32, 256:T], cm[0:32, 0:32], ALU.mult), name)

            def omla(l, h):
                take(dve, ("oT", l, h))
                done(v.tensor_copy(proj[:, PI + h], ps(("oT", l, h))[:, 0:T]), ("oT", l, h))
                await_done(dve, ("oT", l, h))
                dve.sem_inc(sem("omla_ready"), 1)

            def add_gated(name, k, col, signal):
                take(dve, name)
                for g, t0, n in GRP:
                    x = xT[:, k * T + t0:k * T + t0 + n]
                    last = v.scalar_tensor_tensor(x, ps(name)[:, t0:t0 + n], mods[:, col + k, g:g + 1], x,
                                                  ALU.mult, ALU.add)
                done(last, name)
                await_done(dve, name)
                dve.sem_inc(sem(signal), 1)

            v.memset(scond, 0.0).then_inc(sem("scond_cleared"), 1)
            v.memset(eps, EPS).then_inc(sem("eps_ready"), 1)
            link(v.memset(ktil[:, :], 0.0))
            dve.wait_ge(sem("vecs_loaded"), 16)
            dve.wait_ge(sem("consts_loaded"), 16)
            link(v.tensor_tensor(lbw[:, 0:4], V(0, VLB, 4), V(1, VLB, 4), ALU.max))
            v.tensor_tensor(lbw[:, 4:8], V(0, VLB, 4), lbw[:, 0:4], ALU.subtract)
            link(v.tensor_tensor(lbw[:, 8:12], V(1, VLB, 4), lbw[:, 0:4], ALU.subtract))
            v.memset(oml[:, 0, :], 1.0).then_inc(sem("lb_diff"), 1)
            dve.wait_ge(sem("lb_exp"), 1)
            link(v.tensor_tensor(lbw[:, 0:4], lbw[:, 12:16], lbw[:, 16:20], ALU.add))
            link(v.reciprocal(lbw[:, 0:4], lbw[:, 0:4]))
            link(v.tensor_tensor(oml[:, 1, :], lbw[:, 0:4], lbw[:, 12:16], ALU.mult))
            for k in range(KD):
                take(dve, ("x", k))
                done(v.tensor_copy(xT[:, k * T:(k + 1) * T], ps(("x", k))[:, 0:T]), ("x", k))
            for k in range(KD):
                await_done(dve, ("x", k))
                dve.sem_inc(sem("xT_ready"), 1)
            for l in range(DEPTH):
                for j in range(17):
                    if j < 16:
                        name = ("mod", l, j)
                        take(dve, name)
                        if l and j == 0:
                            dve.wait_ge(sem("rows_out0"), 64)
                            dve.wait_ge(sem("rows_out1"), 32)
                        done(v.tensor_copy(kv_tok[:, j % 2, :], ps(name)[:, 0:384]), name)
                        await_done(dve, name)
                        dve.sem_inc(sem("modrow_ready"), 1)
                    if j:
                        name = ("modT", l, j - 1)
                        take(dve, name)
                        done(v.tensor_reduce(mods[:, 3 * j - 3:3 * j, :],
                                             ps(name)[:, 0:384].rearrange("p (f r g) -> p f g r", f=3, r=4)[:, :, 0:2, :],
                                             AX.X, ALU.add), name)
                await_done(dve, ("modT", l, 15))
                await_done(dve, ("modT", l, 14))
                link(v.tensor_tensor(mods, mods, V(l, VB, 48).unsqueeze(2).to_broadcast([128, 48, 2]), ALU.add))
                for which, c, vn in ((0, 8, VN1), (1, 32, VN2)):
                    for g in range(2):
                        last = v.scalar_tensor_tensor(gain[:, which, :, g], mods[:, c:c + 8, g], 1.0, V(l, vn, 8),
                                                      ALU.add, ALU.mult)
                link(last)
                modulate(l, 0, "n1")
                for h in range(HEADS):
                    await_done(dve, ("p", l, PF + h))
                for h in range(HEADS):
                    v.tensor_scalar(kf[:, h * T:(h + 1) * T], kf[:, h * T:(h + 1) * T], oml[:, l, h:h + 1], None,
                                    ALU.mult).then_inc(sem("k_ready"), 1)
                for j in range(PQ, PI):
                    i = j - PQ
                    name = ("p", l, j)
                    dve.wait_ge(sem("sigmoid_ready"), 8 * l + i + 1)
                    v.tensor_tensor(proj[:, j], ps(name)[:, 0:T], sg1[:, i % 2], ALU.mult).then_inc(sem("silu_done"), 1)
                    dve.wait_ge(sem("silu_done"), 8 * l + i + 1)
                    dve.sem_inc(bank_free[PLAN[name][0]], 1)
                dve.wait_ge(sem("logf_ready"), l + 1)
                link(v.tensor_tensor_scan(bcum, cst[:, CRS:CRS + HEADS * T], tmp, 0.0, ALU.mult, ALU.add))
                b4 = bcum.rearrange("p (c b s) -> p c b s", b=NB_, s=SUB)
                b3 = bcum.rearrange("p (c s) -> p c s", s=CH)
                ref3 = ref.rearrange("p (c b) -> p c b", b=NB_)
                link(v.memset(ref3[:, :, 0], 0.0))
                link(v.tensor_copy(ref3[:, :, 1:NB_], b4[:, :, 0:NB_ - 1, SUB - 1]))
                v.tensor_tensor(tmp.rearrange("p (n s) -> p n s", s=SUB), bcum.rearrange("p (n s) -> p n s", s=SUB),
                                ref.unsqueeze(2).to_broadcast([128, HEADS * T // SUB, SUB]), ALU.subtract
                                ).then_inc(sem("diff_ready"), 1)
                dve.wait_ge(sem("diff_exp"), 6 * l + 1)
                link(v.tensor_tensor(qt_f, qf, tmp, ALU.mult))
                v.tensor_tensor(tmp.rearrange("p (c s) -> p c s", s=CH),
                                b3[:, :, CH - 1:CH].to_broadcast([128, HEADS * NC_, CH]), b3, ALU.subtract
                                ).then_inc(sem("diff_ready"), 1)
                dve.wait_ge(sem("diff_exp"), 6 * l + 2)
                v.tensor_tensor(tmp, tmp, kf, ALU.mult).then_inc(sem("kd_ready"), 1)

                def lay_out_keys(h):
                    bh = bcum[:, h * T:(h + 1) * T].rearrange("p (c s) -> p c s", s=CH)
                    for b in range(NB_):
                        n = SUB * (b + 1)
                        e = kt_buf(h)[:, b * T:(b + 1) * T].rearrange("p (c s) -> p c s", s=CH)[:, :, 0:n]
                        last = v.tensor_tensor(e, ref3[:, h * NC_:(h + 1) * NC_, b:b + 1].to_broadcast([128, NC_, n]),
                                               bh[:, :, 0:n], ALU.subtract)
                    last.then_inc(sem("diff_ready"), 1)

                def finish_keys(h):
                    kh = kf[:, h * T:(h + 1) * T].rearrange("p (c s) -> p c s", s=CH)
                    dve.wait_ge(sem("diff_exp"), 6 * l + 3 + h)
                    for b in range(NB_):
                        n = SUB * (b + 1)
                        e = kt_buf(h)[:, b * T:(b + 1) * T].rearrange("p (c s) -> p c s", s=CH)[:, :, 0:n]
                        last = v.tensor_tensor(e, e, kh[:, :, 0:n], ALU.mult)
                    last.then_inc(sem("kt_ready"), 1)

                lay_out_keys(0)
                finish_keys(0)
                r = RMS[l, "ckv"]
                dve.wait_ge(rstd_ready, r + 1)
                for k in range(2):
                    last = scaled(l, "ckv", ckv_all[:, k, 0:T], proj[:, PC + k], V(l, VKV + k))
                last.then_inc(normed, 1)
                dve.wait_ge(rstd_ready, r + 2)
                scaled(l, "kpe", kpe_all[:, 0:T], proj[:, PK], V(l, VKR)).then_inc(normed, 1)
                dve.wait_ge(rstd_ready, r + 3)
                for k in range(3):
                    last = scaled(l, "cq", proj[:, PCQ + k], proj[:, PCQ + k], V(l, VQA + k))
                last.then_inc(normed, 1)
                take(dve, ("rotk", l))
                done(v.tensor_tensor(rot_tmp[:, :], ps(("rotk", l))[:, 0:T], sin, ALU.mult), ("rotk", l))
                link(v.tensor_tensor(kpe_all[:, 0:T], kpe_all[:, 0:T], cos, ALU.mult))
                await_done(dve, ("rotk", l))
                v.tensor_tensor(kpe_all[:, 0:T], kpe_all[:, 0:T], rot_tmp[:, :], ALU.add).then_inc(sem("kpe_ready"), 1)
                dve.wait_ge(sem("kpe_ready"), l + 1)
                def to_tokens(kind, dst):
                    for h in range(HEADS):
                        name = (kind, l, h)
                        take(dve, name)
                        s = ps(name)[:, 0:384].rearrange("p (g n) -> p g n", g=3)
                        v.tensor_copy(dst[:, 0:2, 128 * h:128 * h + 128], s[:, 0:2]).then_inc(
                            sem("v_tok_ready" if kind == "vt" else "kd_tok_ready"), 1)
                        v.tensor_copy(dst[0:32, 2, 128 * h:128 * h + 128], s[0:32, 2]).then_inc(
                            sem("v_tok_ready" if kind == "vt" else "kd_tok_ready"), 1)
                        dve.wait_ge(sem("v_tok_ready" if kind == "vt" else "kd_tok_ready"), 8 * l + 2 * h + 2)
                        dve.sem_inc(bank_free[PLAN[kind, l, h][0]], 1)

                take(dve, ("p", l, NP - 1))
                link(v.memset(hT[:, :], 0.0))
                lay_out_keys(1)
                to_tokens("vt", v_tok)
                finish_keys(1)
                for j in range(3):
                    name = ("cache", l, j)
                    take(dve, name)
                    dst = ckv_all[:, j, T:KEYS] if j < 2 else kpe_all[:, T:KEYS]
                    done(v.tensor_copy(dst, ps(name)[:, 0:PAST]), name)
                for j in range(3):
                    await_done(dve, ("cache", l, j))
                dve.sem_inc(sem("ckv_all_ready"), 2)
                to_tokens("kd", kd_tok)
                for h in range(2, HEADS):
                    take(dve, ("sc", l, h - 2))
                    lay_out_keys(h)
                    mask_scores(l, h - 2)
                    finish_keys(h)
                take(dve, ("sc", l, 2))
                mask_scores(l, 2)
                take(dve, ("sc", l, 3))
                mask_scores(l, 3)
                dve.wait_ge(sem("eb_ready"), l + 1)
                v.tensor_tensor(qf, qf, bcum, ALU.mult).then_inc(sem("qe_ready"), 1)
                for c in range(NC_):
                    name = ("u", l, c)
                    take(dve, name)
                    if 2 <= c < NC_ - 1:
                        dve.wait_ge(sem("state_used"), 7 * l + c - 1)
                    if l and c in (1, NC_ - 1):
                        dve.wait_ge(sem("state_out"), 32)
                    if c == NC_ - 1:
                        dve.wait_ge(sem("state_loaded"), 16 * (l + 1))
                    for h in range(HEADS):
                        hs = slice(128 * h, 128 * h + 128)
                        dec = bcum[:, h * T + CH * c + CH - 1:h * T + CH * c + CH]
                        if c == 0:
                            last = v.tensor_copy(states[:, 1, hs], ps(name)[:, hs])
                        elif c < NC_ - 1:
                            last = v.scalar_tensor_tensor(states[:, (c + 1) % 2, hs], states[:, c % 2, hs], dec,
                                                          ps(name)[:, hs], ALU.mult, ALU.add)
                        else:
                            last = v.scalar_tensor_tensor(s_new[:, hs], s_smp[:, hs], dec, ps(name)[:, hs],
                                                          ALU.mult, ALU.add)
                    done(last, name)
                    await_done(dve, name)
                    if c < NC_ - 1:
                        dve.sem_inc(sem("state_ready"), 1)
                    if c == NC_ - 1:
                        dve.sem_inc(sem("state_new"), 1)
                for h in range(HEADS):
                    r = RMS[l, "o%d" % h]
                    dve.wait_ge(rstd_ready, r + 1)
                    done(v.scalar_tensor_tensor(sg1[:, h % 2], ps(("o", l, h))[:, 0:T], V(l, VON), rstd[:, r % 2],
                                                ALU.mult, ALU.mult), ("o", l, h))
                    await_done(dve, ("o", l, h))
                    dve.sem_inc(normed, 1)
                    v.tensor_tensor(proj[:, PG + h], proj[:, PG + h], sg1[:, h % 2], ALU.mult).then_inc(sem("mix_ready"), 1)
                def rotate(j):
                    take(dve, ("rotq", l, j))
                    done(v.tensor_tensor(rot_tmp[:, :], ps(("rotq", l, j))[:, 0:T], sin, ALU.mult), ("rotq", l, j))
                    link(v.tensor_tensor(qpe[:, j], qpe[:, j], cos, ALU.mult))
                    await_done(dve, ("rotq", l, j))
                    v.tensor_tensor(qpe[:, j], qpe[:, j], rot_tmp[:, :], ALU.add).then_inc(sem("qpe_ready"), 1)
                    dve.wait_ge(sem("qpe_ready"), 2 * l + j + 1)

                for j in range(6):
                    r = RMS[l, "q%d" % j]
                    dve.wait_ge(rstd_ready, r + 1)
                    dst, w = (qn[:, j], V(l, VQN)) if j < 4 else (qpe[:, j - 4], V(l, VQR))
                    done(scaled(l, "q%d" % j, dst, ps(("q", l, j))[:, 0:T], w), ("q", l, j))
                    await_done(dve, ("q", l, j))
                    dve.sem_inc(normed, 1)
                for j in range(2):
                    rotate(j)
                for j in range(8):
                    t0, n = ((0, T), (T, PAST))[j % 2]
                    r = RMS[l, "k%d" % j]
                    dve.wait_ge(rstd_ready, r + 1)
                    done(scaled(l, "k%d" % j, kn[:, j // 2, t0:t0 + n], ps(("k", l, j))[:, 0:n], V(l, VKN)), ("k", l, j))
                    await_done(dve, ("k", l, j))
                    dve.sem_inc(normed, 1)
                for g, (t0, n) in enumerate(TB):
                    take(dve, ("ckvo", l, g))
                    if 3 * l + g >= 2:
                        dve.wait_ge(sem("rows_out%d" % ((l + g) % 2)), 32 * ((3 * l + g) // 2))
                    done(v.tensor_copy(kv_tok[0:n, (3 * l + g) % 2, :],
                                       ps(("ckvo", l, g))[0:n, 0:384]), ("ckvo", l, g))
                    await_done(dve, ("ckvo", l, g))
                    dve.sem_inc(sem("kv_tok_ready"), 1)
                for i in range(14):
                    if i < 12:
                        h, b = divmod(i, 3)
                        k0, nk, q0, nq = QB[b]
                        name = ("s", l, h, b)
                        take(dve, name)
                        link(v.reduce_max(rowmax[0:nq, i:i + 1], ps(name)[0:nq, 0:nk], AX.X))
                        v.tensor_scalar(negmax[0:nq, i:i + 1], rowmax[0:nq, i:i + 1], -SCALE, None, ALU.mult
                                        ).then_inc(sem("negmax_ready"), 1)
                    if 1 <= i < 13:
                        h, b = divmod(i - 1, 3)
                        k0, nk, q0, nq = QB[b]
                        dve.wait_ge(sem("exp_ready"), 12 * l + i)
                        dve.sem_inc(bank_free[PLAN["s", l, h, b][0]], 1)
                        link(v.reciprocal(rinv[0:nq, i - 1:i], rowsum[0:nq, i - 1:i]))
                        pr = probs[0:nq, (i - 1) % 2, 0:nk]
                        v.tensor_scalar(pr, pr, rinv[0:nq, i - 1:i], None, ALU.mult).then_inc(sem("probs_ready"), 1)
                        name = ("pT", l, h, b)
                        take(dve, name)
                        for n_, kb in enumerate(BLK_OF[b]):
                            n = VBLK[kb][1]
                            last = v.tensor_copy(pT[0:n, (i - 1) % 2, nq * n_:nq * n_ + nq], ps(name)[0:n, nq * n_:nq * n_ + nq])
                        done(last, name)
                        await_done(dve, name)
                        dve.sem_inc(sem("pT_ready"), 1)
                        if i >= 2 and (i - 2) % 3 == 2:
                            omla(l, (i - 2) // 3)
                omla(l, 3)
                r = RMS[l, "om"]
                dve.wait_ge(rstd_ready, r + 1)
                for h in range(HEADS):
                    last = scaled(l, "om", proj[:, PI + h], proj[:, PI + h], V(l, VMO + h))
                last.then_inc(normed, 1)
                dve.wait_ge(normed, r + 1)
                dve.sem_inc(sem("mix_ready"), 1)
                for k in range(KD):
                    add_gated(("wo", l, k), k, 16, "x1_ready")
                modulate(l, 1, "n2")
                if l == 0:
                    dve.sem_inc(sem("gu_read"), 3)

                    def mul(q, j):
                        dve.wait_ge(sem("silu_up"), q * NSLOT + j + 1)
                        v.tensor_tensor(arena[:, bass.ds(q * (NSLOT * T) + j * T, T)],
                                        banks[2 * (j % 3) + 1][:, 0:T], sig_up[:, j % 2], ALU.mult
                                        ).then_inc(sem("gu_read"), 1)

                    with dve.Fori(0, NF // NSLOT) as q:
                        for j in range(NSLOT):
                            mul(q, j)
                    for j in range(NF % NSLOT):
                        mul(NF // NSLOT, j)
                    for k in range(KD):
                        add_gated(("down", k), k, 40, "ffn_x_ready")
            def r3(a):
                return rt[:, a:a + 24].rearrange("p (g e) -> p g e", g=3)

            logit, chosen, ex, gate, key, order = r3(0), r3(24), r3(48), r3(80), r3(104), r3(248)
            top, total = rt[:, 72:75], rt[:, 75:78]
            nblk, end, start = rt[:, 128:136], rt[:, 136:144], rt[:, 144:152]
            base, eid = rt[:, 152:164], rt[:, 164:176]
            keyi = rt[:, 176:212].rearrange("p (g i) -> p g i", g=3)
            gatei = rt[:, 212:248].rearrange("p (g i) -> p g i", g=3)
            for g, (t0, n) in enumerate(TB):
                for f in range(2):
                    take(dve, ("ht", g, f))
                    done(v.tensor_copy(h_tok[0:n, g, 512 * f:512 * f + 512], ps(("ht", g, f))[0:n, :]), ("ht", g, f))
            for g in range(3):
                for f in range(2):
                    await_done(dve, ("ht", g, f))
            link(v.memset(logit[:, :, :], 0.0))
            take(dve, ("logits",))
            link(v.tensor_copy(rt[:, 0:16], ps(("logits",))[:, 0:16]))
            done(v.tensor_copy(rt[0:32, 16:24], ps(("logits",))[0:32, 16:24]), ("logits",))
            await_done(dve, ("logits",))
            link(v.tensor_reduce(top, logit, AX.X, ALU.max))
            v.tensor_tensor(ex, logit, top.unsqueeze(2).to_broadcast([128, 3, NX]), ALU.subtract
                            ).then_inc(sem("logit_diff"), 1)
            c4 = cmp8.rearrange("p (g e f) -> p g e f", g=3, e=NX)
            d4 = cmp8b.rearrange("p (g e f) -> p g e f", g=3, e=NX)
            lt = cst[:, CLT:CLT + 64].rearrange("p (e f) -> p e f", e=NX)
            for g in range(3):
                other = logit[:, g].unsqueeze(1).to_broadcast([128, NX, NX])
                this = logit[:, g].unsqueeze(2).to_broadcast([128, NX, NX])
                link(v.tensor_tensor(c4[:, g], other, this, ALU.is_gt))
                link(v.tensor_tensor(d4[:, g], other, this, ALU.is_equal))
                link(v.tensor_tensor(d4[:, g], d4[:, g], lt, ALU.mult))
            link(v.tensor_tensor(cmp8, cmp8, cmp8b, ALU.add))
            link(v.tensor_reduce(order, c4, AX.X, ALU.add))
            link(v.tensor_scalar(chosen, order, 1.5, None, ALU.is_lt))
            link(v.memset(chosen[32:64, 2], 0.0))
            link(v.memset(chosen[64:128, 2], 0.0))
            dve.sem_inc(sem("chosen_ready"), 1)
            dve.wait_ge(sem("logit_exp"), 1)
            link(v.tensor_tensor(ex, ex, chosen, ALU.mult))
            link(v.tensor_reduce(total, ex, AX.X, ALU.add))
            link(v.tensor_scalar(total, total, 1e-30, None, ALU.max))
            link(v.reciprocal(total, total))
            link(v.tensor_tensor(gate, ex, total.unsqueeze(2).to_broadcast([128, 3, NX]), ALU.mult))
            take(dve, ("rank",))
            rank = ps(("rank",))[:, 0:24].rearrange("p (g e) -> p g e", g=3)
            count = ps(("rank",))[:, 24:32]
            link(v.tensor_tensor(key, rank, chosen, ALU.mult))
            link(v.tensor_scalar(order, chosen, 1e4, -1e4, ALU.mult, ALU.add))
            link(v.tensor_tensor(key, key, order, ALU.add))
            link(v.tensor_scalar(nblk, count, SLOTS_X + 0.5, None, ALU.is_gt))
            done(v.tensor_scalar(start, count, 2 * SLOTS_X + 0.5, 1.0, ALU.is_gt, ALU.add), ("rank",))
            await_done(dve, ("rank",))
            link(v.tensor_tensor(nblk, nblk, start, ALU.add))
            link(v.tensor_tensor_scan(end, ones[:, 0:NX], nblk, 0.0, ALU.mult, ALU.add))
            link(v.tensor_tensor(start, end, nblk, ALU.subtract))
            oh = cmpi.rearrange("p (i e) -> p i e", e=NX)
            o2 = cmpi2.rearrange("p (i e) -> p i e", e=NX)
            full3 = [128, ITEMS, NX]
            it = cst[:, CIT:CIT + ITEMS].unsqueeze(2).to_broadcast(full3)
            link(v.tensor_tensor(oh, end.unsqueeze(1).to_broadcast(full3), it, ALU.is_gt))
            link(v.tensor_tensor(o2, start.unsqueeze(1).to_broadcast(full3), it, ALU.is_gt))
            link(v.tensor_tensor(oh, oh, o2, ALU.subtract))
            link(v.tensor_tensor(o2, it, start.unsqueeze(1).to_broadcast(full3), ALU.subtract))
            link(v.tensor_tensor(o2, o2, oh, ALU.mult))
            link(v.tensor_reduce(base, o2, AX.X, ALU.add))
            link(v.tensor_scalar(base, base, float(SLOTS_X), None, ALU.mult))
            link(v.tensor_tensor(o2, oh, cst[:, CEX:CEX + NX].unsqueeze(1).to_broadcast(full3), ALU.mult))
            link(v.tensor_reduce(eid, o2, AX.X, ALU.add))
            link(v.tensor_copy(ids[:, 0:ITEMS], eid))
            link(v.tensor_copy(ids[:, ITEMS:ITEMS + 1], end[:, NX - 1:NX]))
            link(v.tensor_scalar(end[:, NX - 1:NX], end[:, NX - 1:NX], -1.0, None, ALU.add))
            link(v.tensor_copy(ids[:, ITEMS + 1:ITEMS + 2], end[:, NX - 1:NX]))
            dve.sem_inc(sem("ids_ready"), 1)
            for g in range(3):
                link(v.tensor_tensor(o2, oh, key[:, g].unsqueeze(1).to_broadcast(full3), ALU.mult))
                link(v.tensor_reduce(keyi[:, g], o2, AX.X, ALU.add))
                link(v.tensor_tensor(keyi[:, g], keyi[:, g], base, ALU.subtract))
                link(v.tensor_tensor(o2, oh, gate[:, g].unsqueeze(1).to_broadcast(full3), ALU.mult))
                link(v.tensor_reduce(gatei[:, g], o2, AX.X, ALU.add))
            link(v.memset(acc[:, :, :], 0.0))
            link(v.memset(ysb[:, :], 0.0))
            link(v.memset(gT, 0.0))
            for name in ("y_lo_ready", "y_hi_ready", "gates_ready"):
                dve.sem_inc(sem(name), 1)
            dve.sem_inc(sem("scatter_read"), KD)
            dve.sem_inc(sem("at_split"), XSLOT)
            dve.sem_inc(sem("a_ready"), 2)
            last_item = dve.value_load(ids[0:1, ITEMS + 1:ITEMS + 2], min_val=NX - 1, max_val=ITEMS - 1)
            io = cst[:, CIO:CIO + 128].unsqueeze(1).to_broadcast([128, 3, 128])

            def choose(i):
                v.tensor_tensor(pick, io, keyi[:, :, bass.ds(i, 1)].to_broadcast([128, 3, 128]), ALU.is_equal
                                ).then_inc(sem("pick_ready"), 1)

            def split_lo(i, q, j):
                s = j % 4 * SLOTW
                for p in range(3):
                    dve.wait_ge(sem("hi_done"), i * (3 * NFX) + q * (3 * XSLOT) + (3 * j + p + 1))
                    hi, lo = ((w_hi[:, j % 2, D * p:D * p + D], w_lo[:, j % 2, D * p:D * p + D]) if p < 2
                              else (wd_hi[:, j % 4], wd_lo[:, j % 4]))
                    v.tensor_tensor(lo, xring[:, s + D * p:s + D * p + D], hi.bitcast(F32), ALU.subtract
                                    ).then_inc(sem("lo_done"), 1)

            def tokens_lo(i):
                for b in range(2):
                    dve.wait_ge(sem("hg_rounded"), i * 2 + (b + 1))
                    v.tensor_tensor(hg_lo[:, 4 * b:4 * b + 4], banks[6 + b][:, :].rearrange("p (k n) -> p k n", k=4),
                                    hg_hi[:, 4 * b:4 * b + 4].bitcast(F32), ALU.subtract).then_inc(sem("hg_split"), 1)

            def add_scattered(i, some=range(KD)):
                for k in some:
                    dve.wait_ge(sem("scattered"), i * KD + (k + 1))
                    v.tensor_tensor(acc[:, k], acc[:, k], banks[6 + k % 2][:, 0:T], ALU.add
                                    ).then_inc(sem("scatter_read"), 1)

            def item(i, more):
                dve.wait_ge(sem("pick_ready"), i + 1)
                v.tensor_tensor(pickg, pick, gatei[:, :, bass.ds(i, 1)].to_broadcast([128, 3, 128]), ALU.mult
                                ).then_inc(sem("pickg_ready"), 1)

                def multiply(q, j):
                    dve.wait_ge(sem("silu_x"), i * NFX + q * XSLOT + (j + 1))
                    v.tensor_tensor(aX[:, j % 2], banks[j][:, 128:256], sgX[:, j % 2], ALU.mult
                                    ).then_inc(sem("a_ready"), 1)

                def hidden_lo(q, j):
                    dve.wait_ge(sem("at_rounded"), i * NFX + q * XSLOT + (j + 1))
                    v.tensor_tensor(at_lo[:, j % 4], banks[j % 4][:, 256:384], at_hi[:, j % 4].bitcast(F32),
                                    ALU.subtract).then_inc(sem("at_split"), 1)

                for j in range(4):
                    multiply(0, j)
                    if j:
                        hidden_lo(0, j - 1)
                    add_scattered(i, SCATTER[j])
                    if j == 1 and more:
                        dve.wait_ge(sem("pickg_ready"), i + 1)
                        choose(i + 1)
                    if j == 3:
                        dve.wait_ge(sem("scatter_read"), i * KD + 2 * KD)
                    split_lo(i, 0, j + 2)
                with dve.Fori(1, NFX // XSLOT - 1) as q:
                    for j in range(4):
                        multiply(q, j)
                        hidden_lo(q, j - 1)
                        split_lo(i, q, j + 2)
                q = NFX // XSLOT - 1
                for j in range(4):
                    multiply(q, j)
                    hidden_lo(q, j - 1)
                    if j < 3 and (j < 2 or more):
                        split_lo(i, q, j + 2)
                if more:
                    tokens_lo(i + 1)
                hidden_lo(q, 3)
                if more:
                    split_lo(i, q, 5)
                dve.wait_ge(sem("down_done"), i * NFX + (NFX + XSLOT))
                v.tensor_copy(ysb[:, 512:1024], banks[5][:, :]).then_inc(sem("y_hi_ready"), 1)

            choose(0)
            split_lo(0, 0, 0)
            tokens_lo(0)
            split_lo(0, 0, 1)
            with dve.Fori(0, last_item) as i:
                item(i, True)
            item(last_item, False)
            add_scattered(last_item + 1)
            dve.wait_ge(sem("scatter_read"), last_item * KD + 3 * KD)
            for k in range(KD):
                for g, t0, n in GRP:
                    x = xT[:, k * T + t0:k * T + t0 + n]
                    last = v.scalar_tensor_tensor(x, acc[:, k, t0:t0 + n], mods[:, 40 + k, g:g + 1], x, ALU.mult, ALU.add)
                last.then_inc(sem("y_final"), 1)
            for g, (t0, n) in enumerate(TB):
                for f in range(2):
                    take(dve, ("y", g, f))
                    v.tensor_copy(y_tok[0:n, g, 512 * f:512 * f + 512], ps(("y", g, f))[0:n, :]).then_inc(sem("y_ready"), 1)

        @block.gpsimd
        def _(pool):
            for l in range(DEPTH):
                if l:
                    take(pool, ("cache", l - 1, 2))
                    pool.wait_ge(sem("state_new"), l)
                    take(pool, ("o", l - 1, 3))
                for k, src in ((0, cache_in[0][l]), (256, cache_in[1][l]), (320, cache_in[1][l])):
                    n = 256 if k == 0 else ROPE
                    pool.dma_start(cache_tok[:, :, k:k + n], src.rearrange("(b p) n -> p b n", p=128)
                                   ).then_inc(sem("cache_loaded"), 16)
                pool.dma_start(s_smp[:, :].rearrange("p (h n) -> p h n", h=HEADS),
                               state_in[l].rearrange("h k v -> k h v")).then_inc(sem("state_loaded"), 16)
                pool.wait_ge(sem("state_ready"), 8 * (l + 1))
                pool.dma_start(s_out[0][l].rearrange("h k v -> k h v"),
                               states[:, 0].rearrange("p (h n) -> p h n", h=HEADS)).then_inc(sem("state_out"), 16)
                pool.wait_ge(sem("state_new"), l + 1)
                pool.dma_start(s_out[1][l].rearrange("h k v -> k h v"),
                               s_new[:, :].rearrange("p (h n) -> p h n", h=HEADS)).then_inc(sem("state_out"), 16)
                for g, (t0, n) in enumerate(TB):
                    pool.wait_ge(sem("kv_tok_ready"), 3 * l + g + 1)
                    src = kv_tok[0:n, (3 * l + g) % 2]
                    out, r0 = (kv_out[0], t0) if g < 2 else (kv_out[1], 0)
                    pool.dma_start(out[0][l][r0:r0 + n, :], src[:, 0:KVL]).then_inc(sem("rows_out%d" % ((l + g) % 2)), 16)
                    pool.dma_start(out[1][l][r0:r0 + n, :], src[:, KVL:KVL + ROPE]).then_inc(sem("rows_out%d" % ((l + g) % 2)), 16)
            pool.wait_ge(sem("h2_ready"), DEPTH)
            pool.dma_start(router, w_router).then_inc(sem("router_loaded"), 16)
            for g, (t0, n) in enumerate(TB):
                pool.wait_ge(sem("y_ready"), 2 * g + 2)
                out, r0 = (y_out[0], t0) if g < 2 else (y_out[1], 0)
                pool.dma_start(out[r0:r0 + n, :], y_tok[0:n, g]).then_inc(sem("y_stored"), 16)
            pool.wait_ge(sem("y_stored"), 48)
            pool.wait_ge(sem("state_out"), 32 * DEPTH)
            pool.wait_ge(sem("rows_out0"), 96)
            pool.wait_ge(sem("rows_out1"), 96)


def kernel(**x):
    import concourse.bacc as bacc
    from concourse.bass_utils import run_bass_kernel_spmd as run

    def slabs(w, per):
        *lead, k, n = w.shape
        w = w.reshape(*lead, k // 128, 128, n // (128 * per), per, 128)
        a = len(lead)
        return w.transpose(*range(a), a + 2, a + 1, a + 3, a, a + 4).reshape(*lead, n // (128 * per), 128, -1)

    def col(v):
        return v.reshape(v.shape[0], -1, 128).transpose(0, 2, 1)

    x = {k: np.asarray(v) for k, v in x.items()}
    w = x["w_in"]
    H = 512
    kpe = w[:, :, 4 * H + QL + KVL:]
    win = np.concatenate([w[:, :, H:2 * H], w[:, :, 0:H], w[:, :, 3 * H:4 * H], w[:, :, 2 * H:3 * H],
                          w[:, :, 4 * H + QL:4 * H + QL + KVL], kpe, kpe, w[:, :, 4 * H:4 * H + QL]], axis=2)
    q = x["mla_wqb"].reshape(DEPTH, QL, HEADS, 128 + ROPE)
    wqb = np.concatenate([q[..., :128].reshape(DEPTH, QL, -1), q[..., 128:].reshape(DEPTH, QL, -1)], axis=2)
    kv = x["mla_wkvb"].reshape(DEPTH, KVL, HEADS, 256)
    wkvb = np.concatenate([kv[..., :128].reshape(DEPTH, KVL, -1), kv[..., 128:].reshape(DEPTH, KVL, -1)], axis=2)
    g, u = (x[n][0].reshape(KD, 128, NF, 128).transpose(2, 1, 0, 3).reshape(NF, 128, D) for n in ("ffn_w_gate", "ffn_w_up"))
    wup = np.concatenate([g, u], axis=2)
    gu = np.stack([x[n][0].reshape(NX, KD, 128, NFX, 128).transpose(0, 3, 2, 1, 4) for n in ("moe_w_gate", "moe_w_up")],
                  axis=4).reshape(NX * NFX, 128, 2 * D)
    wmoe = np.concatenate([gu, x["moe_w_down"][0].reshape(NX * NFX, 128, D)], axis=2)
    two = lambda v: np.concatenate([v, v], axis=1)
    vecs = np.concatenate([col(x["ada_b"]), col(x["norm1_w"]), col(x["norm2_w"]), col(x["hg_onorm_w"]),
                           col(x["mla_qa_norm_w"]), col(x["mla_kva_norm_w"]), col(x["mla_qn_nope_w"]),
                           col(two(x["mla_qn_rope_w"])), col(x["mla_kn_nope_w"]), col(two(x["mla_kn_rope_w"])),
                           col(x["mla_onorm_w"]), col(x["hg_lower_bounds"])], axis=2)
    vecs = vecs.transpose(1, 0, 2).reshape(128, -1)
    cond = np.stack([x["c_prompt"][0], x["c_sample"][0]], axis=1).reshape(KD, 128, 2).transpose(1, 0, 2).reshape(128, -1)
    arrays = {
        "consts": constants(), "vecs": vecs, "cond": cond,
        "x_in": np.concatenate([x["x_prompt"][0], x["x_sample"][0]], axis=0),
        "state_in": x["state_hgrn"][:, 0], "cache_ckv_in": x["cache_ckv"][:, 0], "cache_kpe_in": x["cache_kpe"][:, 0],
        "w_ada": x["ada_w"].reshape(DEPTH, KD, 128, 16, 384).transpose(0, 3, 2, 1, 4).reshape(DEPTH, 16, 128, -1), "w_win": slabs(win, 2),
        "w_wqb": wqb.reshape(DEPTH, 3, 128, -1).transpose(0, 2, 1, 3).reshape(DEPTH, 1, 128, -1),
        "w_wkvb": wkvb.reshape(DEPTH, 2, 128, -1).transpose(0, 2, 1, 3).reshape(DEPTH, 1, 128, -1),
        "w_wo": slabs(x["w_o"], 2), "w_up": wup, "w_down": slabs(x["ffn_w_down"][0], 1),
        "w_router": x["moe_router"][0].reshape(KD, 128, NX).transpose(1, 0, 2), "w_moe": wmoe,
    }
    arrays = {k: np.ascontiguousarray(v) for k, v in arrays.items()}
    nc = bacc.Bacc("TRN2", target_bir_lowering=False, num_devices=1)
    a = {k: nc.dram_tensor(k, v.shape, F32, kind="ExternalInput").ap() for k, v in arrays.items()}
    outs = {"y_prompt": (SEQ, D), "y_sample": (DEC, D), "s_prompt": (DEPTH, HEADS, 128, 128),
            "ckv_prompt": (DEPTH, SEQ, KVL), "kpe_prompt": (DEPTH, SEQ, ROPE),
            "s_sample": (DEPTH, HEADS, 128, 128), "ckv_sample": (DEPTH, DEC, KVL), "kpe_sample": (DEPTH, DEC, ROPE)}
    o = {k: nc.dram_tensor(k, s, F32, kind="ExternalOutput").ap() for k, s in outs.items()}
    build(nc, a["consts"], a["vecs"], a["cond"], a["x_in"], a["state_in"], (a["cache_ckv_in"], a["cache_kpe_in"]),
          a["w_ada"], a["w_win"], a["w_wqb"], a["w_wkvb"], a["w_wo"], a["w_up"], a["w_down"], a["w_router"], a["w_moe"],
          (o["y_prompt"], o["y_sample"]), (o["s_prompt"], o["s_sample"]),
          ((o["ckv_prompt"], o["kpe_prompt"]), (o["ckv_sample"], o["kpe_sample"])))
    r = run(nc, [arrays], core_ids=[0]).results[0]
    y_p, y_s = r["y_prompt"][None], r["y_sample"][None]
    return (y_p, y_s, r["s_prompt"][:, None], r["ckv_prompt"][:, None], r["kpe_prompt"][:, None],
            r["s_sample"][:, None], r["ckv_sample"][:, None], r["kpe_sample"][:, None])
```

```python
import numpy as np
import concourse.bass as bass
from concourse import mybir
from contextlib import ExitStack

F32 = mybir.dt.float32
F32R = mybir.dt.float32r
I32 = mybir.dt.int32
ALU = mybir.AluOpType
ACT = mybir.ActivationFunctionType
AX = mybir.AxisListType

D, SEQ, DEC, PAST, DEPTH = 1024, 256, 32, 256, 2
T = SEQ + DEC
KD = D // 128
HEADS = 4
QL, KVL, ROPE = 384, 256, 64
SCALE = (128 + ROPE) ** -0.5
FF, FX, NX = 2816, 3584, 8
NF, NFX = FF // 128, FX // 128
EPS = 1e-6
KEYS = T + PAST
CH, SUB = 32, 4
NC_, NB_ = T // CH, CH // SUB
SLOTS_X = 128
ITEMS = 12
GRP = ((0, 0, SEQ), (1, SEQ, DEC))
TB = ((0, 128), (128, 128), (256, 32))
NSLOT, SLOTW = 6, 3072
XSLOT = 4
SCATTER = ((), (0, 1), (2, 3), (4, 5, 6, 7))
ARENA = 16224
PF, PQ, PG, PI, PC, PK, PCQ, NP = 0, 4, 8, 12, 16, 18, 19, 22
VB, VN1, VN2, VON, VQA, VKV, VQN, VQR, VKN, VKR, VMO, VLB, NV = 0, 48, 56, 64, 65, 68, 70, 71, 72, 73, 74, 78, 82
CI, CO, CO64, CROT, CCOS, CSIN, CCM, CRS, CU, CIO, CLT, CMQ, CMK, CIT, CEX, NCST = np.cumsum(
    [0, 128, 128, 128, 128, T, T, 128, HEADS * T, 128, 128, 64, 128, 128, ITEMS, NX]).tolist()


def constants():
    c = np.zeros((128, NCST), np.float32)
    p = np.arange(128)
    c[:, CI:CI + 128] = np.eye(128)
    c[:, CO:CO + 128] = 1.0
    c[:, CO64:CO64 + 128] = p[:, None] // 64 == p[None, :] // 64
    for h in (0, 64):
        for m in range(32):
            c[h + 32 + m, CROT + h + m] = -1.0
            c[h + m, CROT + h + 32 + m] = 1.0
    inv = (10000.0 ** (-np.arange(32, dtype=np.float32) / 32)).astype(np.float32)
    pos = np.concatenate([np.arange(SEQ), PAST + np.arange(DEC)]).astype(np.float32)
    ang = (pos[None, :] * inv[p % 32][:, None]).astype(np.float32)
    c[:, CCOS:CCOS + T] = np.cos(ang.astype(np.float64))
    c[:, CSIN:CSIN + T] = np.sin(ang.astype(np.float64))
    s, t = p[:, None], p[None, :]
    c[:, CCM:CCM + 128] = (s // CH == t // CH) & (s <= t)
    c[:, CRS:CRS + HEADS * T] = np.arange(HEADS * T)[None, :] % CH != 0
    c[:, CU:CU + 128] = s < t
    c[:, CIO:CIO + 128] = t
    e = np.arange(NX)
    c[:, CLT:CLT + 64] = (e[None, :] < e[:, None]).reshape(1, 64)
    c[0, CMQ:CMQ + 128] = p < 64
    c[0, CMK:CMK + 128] = np.where(p < 64, 0.0, -1e30)
    c[:, CIT:CIT + ITEMS] = np.arange(ITEMS)
    c[:, CEX:CEX + NX] = e
    return c


ADA = 16
ADA_AT = {("start", 0): 6, ("h1", 0): 3, ("win", 0): 2, ("n2", 0): 3, ("h1", 1): 3, ("win", 1): 1}
ADA_AT.update({("att", 0, i): 1 for i in range(10)})
ADA_AT.update({("att", 1, i): 1 for i in range(4)})
ADA_AT["att", 1, 4] = 0


def ada_order():
    steps, n = {}, 0
    places = [("start", 0)]
    for l in range(DEPTH):
        places += [("h1", l), ("win", l)] + [("att", l, i) for i in range(12)] + [("n2", l)]
    for place in places:
        mine = steps[place] = []
        for _ in range(ADA_AT.get(place, 0)):
            mine.append(("rows", n))
            if n and ("turn", n - 1) not in steps["start", 0]:
                mine.append(("turn", n - 1))
            n += 1
        if place in (("start", 0), ("att", 1, 4)):
            mine.append(("turn", n - 1))
    assert n == DEPTH * ADA
    return steps


ADA_STEPS = ada_order()


def ada_slabs(place):
    return [n for kind, n in ADA_STEPS[place] if kind == "rows"]


STREAM = [("ada", 0, n, 3072) for n in ada_slabs(("start", 0))]
for _l in range(DEPTH):
    STREAM += [("ada", 0, n, 3072) for n in ada_slabs(("h1", _l))]
    STREAM += [("win", _l, j, 2048) for j in range(11)]
    STREAM += [("ada", 0, n, 3072) for n in ada_slabs(("win", _l))]
    STREAM += [("wqb", _l, 0, 2304), ("wkvb", _l, 0, 2048)]
    STREAM += [("ada", 0, n, 3072) for i in range(12) for n in ada_slabs(("att", _l, i))]
    STREAM += [("wo", _l, j, 2048) for j in range(4)]
    STREAM += [("ada", 0, n, 3072) for n in ada_slabs(("n2", _l))]
    if _l == 0:
        STREAM += [("up", 0, j, 2048) for j in range(NF)] + [("down", 0, j, FF) for j in range(KD)]
POS = {(n, l, j): at for at, (n, l, j, _w) in enumerate(STREAM)}


DOWN_PIECES = 3


def piece_done(n):
    if n < 2 * NF:
        return None, n + 1
    k, p = divmod(n - 2 * NF, DOWN_PIECES)
    return (("down", k), None) if p == DOWN_PIECES - 1 else (None, 2 * NF + k * (DOWN_PIECES - 1) + p + 1)


def slot_of(at):
    return at % NSLOT


def fills(at):
    return 16 * (at // NSLOT + 1)


def psum_plan():
    plan, count, at = {}, [0] * 8, [0]

    def use(name, bank=None):
        if bank is None:
            bank = at[0] % 8
            at[0] += 1
        plan[name] = (bank, count[bank])
        count[bank] += 1

    def ada(place, banks=(None, None)):
        for kind, n in ADA_STEPS[place]:
            use((kind, n), banks[kind == "turn"])

    for k in range(KD):
        use(("x", k))
    for l in range(DEPTH):
        use(("ss", l, "n1"))
        if l == 0:
            ada(("start", 0))
        ada(("h1", l))
        for j in range(NP):
            use(("p", l, j))
        ada(("win", l))
        for s in ("ckv", "kpe", "cq"):
            use(("ss", l, s))
        use(("rotk", l))
        for h in range(HEADS):
            use(("vt", l, h))
        for j in range(3):
            use(("cache", l, j))
        for h in range(HEADS):
            use(("kd", l, h))
        for h in range(HEADS):
            use(("sc", l, h))
        for h in range(HEADS):
            use(("o", l, h), h)
        for c in range(NC_):
            use(("u", l, c), 4 + c % 4)
        for h in range(HEADS):
            use(("ss", l, "o%d" % h), 4 + h)
        for j in range(6):
            use(("q", l, j))
            if j:
                use(("ss", l, "q%d" % (j - 1)))
        use(("ss", l, "q5"))
        for j in range(2):
            use(("rotq", l, j))
        for j in range(8):
            use(("k", l, j))
            if j:
                use(("ss", l, "k%d" % (j - 1)))
        use(("ss", l, "k7"))
        for b in range(5):
            use(("v", l, b))
        for g in range(3):
            use(("ckvo", l, g))
        for i in range(12):
            h, b = divmod(i, 3)
            if b == 0:
                use(("oT", l, h), h % 2)
            use(("s", l, h, b), 2 + i % 2)
            use(("pT", l, h, b), 4 + i % 2)
            ada(("att", l, i), (6, 7))
        use(("ss", l, "om"))
        for k in range(KD):
            use(("wo", l, k))
        use(("ss", l, "n2"))
        ada(("n2", l))
        if l == 0:
            plan["before the dense layer"] = list(count)
            for k in range(KD):
                use(("down", k))
        else:
            use(("logits",))
            for g in range(3):
                for f in range(2):
                    use(("ht", g, f))
            use(("rank",))
    plan["before the experts"] = list(count)
    for f in range(2):
        for g in range(3):
            use(("y", g, f), 3 * f + g)
    return plan, count


def build(nc, consts, vecs, cond, x_in, state_in, cache_in, w_ada, w_win, w_wqb, w_wkvb, w_wo,
          w_up, w_down, w_router, w_moe, y_out, s_out, kv_out):
    PLAN, _ = psum_plan()
    ctx = ExitStack()
    with ctx:
        scope = [ctx]

        def sb(name, cols, dt=F32):
            return scope[0].enter_context(nc.sbuf_tensor(name, [128, cols], dt))

        sems = {}

        def sem(name):
            if name not in sems:
                sems[name] = ctx.enter_context(nc.semaphore(name))
            return sems[name]

        def tiles(ap, n):
            return ap.rearrange("p (n t) -> p n t", n=n)

        cst = sb("cst", NCST)
        vec = sb("vec", DEPTH * NV)
        xT = sb("xT", KD * T)
        hT = sb("hT", KD * T)
        misc = sb("misc", 708)
        scond = sb("scond", KD * 32)[:, :].rearrange("p (k g) -> p k g", g=32)
        scope[0] = outer = ExitStack()
        ring = sb("ring", NSLOT * SLOTW)
        states = tiles(sb("states", 2 * 512)[:, :], 2)
        s_smp = sb("s_smp", 512)
        s_new = sb("s_new", 512)
        cache_tok = tiles(sb("cache_tok", 2 * 384)[:, :], 2)
        modrow = tiles(sb("modrow", 2 * 384)[:, :], 2)
        kv_tok = tiles(sb("kv_tok", 2 * 384)[:, :], 2)
        scope[0] = ExitStack()
        arena = sb("arena", ARENA)
        ktil = sb("ktil", NB_ * T)

        arena_at = [0]

        def cut(cols, at=None):
            if at is None:
                at = arena_at[0]
                arena_at[0] += cols
            assert at + cols <= ARENA, at + cols
            return arena[:, at:at + cols]

        proj_f = cut(NP * T)
        proj = tiles(proj_f, NP)
        kf, qf = proj_f[:, PF * T:(PF + 4) * T], proj_f[:, PQ * T:(PQ + 4) * T]
        ckv_all = tiles(cut(2 * KEYS), 2)
        kpe_all = cut(KEYS)
        qpe = tiles(cut(2 * T), 2)
        bcum = cut(HEADS * T)
        tmp = cut(HEADS * T)
        qt_f = cut(HEADS * T)
        tok0 = arena_at[0]
        kd_tok = tiles(cut(3 * 512), 3)
        v_tok = tiles(cut(3 * 512), 3)
        sq4 = tiles(cut(4 * T), 4)
        kn = tiles(cut(HEADS * KEYS, 0), HEADS)
        vals = tiles(cut(5 * 512, tok0), 5)
        qn = tiles(qt_f, HEADS)
        sT = tiles(tmp, HEADS)
        qt = tiles(qt_f, HEADS)
        sq8_f = cut(KD * T, 0)
        x_tok = tiles(cut(3 * D, 0), 3)
        rot_tmp = sb("rot_tmp", T)
        sq1 = tiles(sb("sq1", 2 * T)[:, :], 2)
        rstd = tiles(sb("rstd", 2 * T)[:, :], 2)
        sg1 = tiles(sb("sg1", 2 * T)[:, :], 2)
        probs = tiles(sb("probs", 2 * T)[:, :], 2)
        pT = tiles(sb("pT", 2 * T)[:, :], 2)
        ref = misc[:, 288:288 + HEADS * T // SUB]
        scope[0].close()
        scope[0] = ExitStack()
        wf_hi = tiles(sb("wf_hi", 2 * D, F32R)[:, :], 2)
        wf_lo = tiles(sb("wf_lo", 2 * D, F32R)[:, :], 2)
        h_hi, h_lo = sb("h_hi", KD * T, F32R), sb("h_lo", KD * T, F32R)
        aT_hi, aT_lo = sb("aT_hi", NF * T, F32R), sb("aT_lo", NF * T, F32R)
        sig_up, a_up = tiles(hT[:, 0:2 * T], 2), tiles(hT[:, 2 * T:4 * T], 2)
        scope[0].close()
        outer.close()
        scope[0] = ctx
        xring = sb("xring", XSLOT * SLOTW)
        w_hi = tiles(sb("w_hi", 2 * 2 * D, F32R)[:, :], 2)
        w_lo = tiles(sb("w_lo", 2 * 2 * D, F32R)[:, :], 2)
        wd_hi = tiles(sb("wd_hi", 4 * D, F32R)[:, :], 4)
        wd_lo = tiles(sb("wd_lo", 4 * D, F32R)[:, :], 4)
        hg_hi = tiles(sb("hg_hi", D, F32R)[:, :], KD)
        hg_lo = tiles(sb("hg_lo", D, F32R)[:, :], KD)
        at_hi = tiles(sb("at_hi", 4 * 128, F32R)[:, :], 4)
        at_lo = tiles(sb("at_lo", 4 * 128, F32R)[:, :], 4)
        sgX = tiles(sb("sgX", 2 * 128)[:, :], 2)
        aX = tiles(sb("aX", 2 * 128)[:, :], 2)
        h_tok = tiles(sb("h_tok", 3 * D)[:, :], 3)
        y_tok = h_tok
        ysb = sb("ysb", D)
        acc = tiles(hT[:, :], KD)
        pick = tiles(sb("pick", 3 * 128)[:, :], 3)
        pickg = tiles(sb("pickg", 3 * 128)[:, :], 3)
        gT = sb("gT", T)[:, :]
        cmp8, cmp8b = sb("cmp8", 3 * 64)[:, :], sb("cmp8b", 3 * 64)[:, :]
        cmp4 = sb("cmp4", 3 * ITEMS * NX)[:, :]
        cmpi, cmpi2 = sb("cmpi", ITEMS * NX)[:, :], sb("cmpi2", ITEMS * NX)[:, :]
        router = tiles(sb("router", KD * NX)[:, :], KD)
        rt = sb("rt", 272)

        mods = [misc[:, a:a + 96].rearrange("p (f g) -> p f g", g=2) for a in (0, 580)]
        gain = [misc[:, a:a + 32].rearrange("p (n k g) -> p n k g", n=2, g=2) for a in (96, 676)]
        condT = misc[:, 128:144].rearrange("p (k g) -> p k g", g=2)
        eps = misc[:, 160:161]
        lbw = misc[:, 164:184]
        oml = misc[:, 184:192].rearrange("p (l h) -> p l h", l=2)
        rowmax = misc[:, 192:216]
        negmax = misc[:, 216:240]
        rowsum = misc[:, 240:264]
        rinv = misc[:, 264:288]
        ids = ctx.enter_context(nc.sbuf_tensor("ids", [128, 16], I32))

        banks = [ctx.enter_context(nc.psum_tensor("bank%d" % b, [128, 512], F32)) for b in range(8)]
        bank_full = [sem("bank_full%d" % b) for b in range(8)]
        bank_free = [sem("bank_free%d" % b) for b in range(8)]
        slot_full = [sem("slot_full%d" % s) for s in range(NSLOT)]
        xslot_full = [sem("xslot_full%d" % s) for s in range(XSLOT)]

        ident, ones, ones64 = cst[:, CI:CI + 128], cst[:, CO:CO + 128], cst[:, CO64:CO64 + 128]
        rot, cos, sin = cst[:, CROT:CROT + 128], cst[:, CCOS:CCOS + T], cst[:, CSIN:CSIN + T]

        def V(l, col, n=1):
            return vec[:, l * NV + col:l * NV + col + n]

        def kt_buf(h):
            return ktil if h % 2 == 0 else hT

        def ps(name):
            return banks[PLAN[name][0]]

        def take(eng, name):
            b, n = PLAN[name]
            eng.wait_ge(bank_full[b], n + 1)

        def done(ins, name):
            ins.then_inc(bank_free[PLAN[name][0]], 1)

        def await_done(eng, name):
            b, n = PLAN[name]
            eng.wait_ge(bank_free[b], n + 1)

        rms_order = []
        for l in range(DEPTH):
            rms_order += [(l, s) for s in ["n1", "ckv", "kpe", "cq"] + ["o%d" % h for h in range(4)]
                          + ["q%d" % j for j in range(6)] + ["k%d" % j for j in range(8)] + ["om", "n2"]]
        RMS = {n: i for i, n in enumerate(rms_order)}
        squares_ready, rstd_ready, normed = sem("squares_ready"), sem("rstd_ready"), sem("normed")
        def used_up(at):
            name, l, j, _w = STREAM[at]
            if name in ("up", "down"):
                return sem("ffn_lo"), 2 * (j + 1) if name == "up" else 2 * NF + DOWN_PIECES * (j + 1)
            last = {"ada": ("rows", j), "win": ("p", l, 2 * j + 1), "wqb": ("q", l, 5), "wkvb": ("v", l, 4),
                    "wo": ("wo", l, 2 * j + 1)}[name]
            b, n = PLAN[last]
            return bank_full[b], n + 1

        QB = ((0, 128, 0, 128), (0, 256, 128, 128), (SEQ, T, SEQ, DEC))
        VBLK = ((0, 128), (128, 128), (256, 32), (288, 128), (416, 128))
        BLK_OF = ((0,), (0, 1), (2, 3, 4))
        block = ctx.enter_context(nc.Block())

        @block.sync
        def _(sp):
            sp.dma_start(cst[:, :], consts).then_inc(sem("consts_loaded"), 16)
            sp.dma_start(misc[:, 128:144], cond).then_inc(sem("cond_loaded"), 16)
            sp.dma_start(vec[:, :], vecs).then_inc(sem("vecs_loaded"), 16)
            for g, (t0, n) in enumerate(TB):
                sp.dma_start(x_tok[0:n, g, :], x_in[t0:t0 + n, :]).then_inc(sem("x_loaded"), 16)

            def slab(at, src, width):
                if at >= NSLOT:
                    sp.wait_ge(*used_up(at - NSLOT))
                sp.dma_start(ring[:, slot_of(at) * SLOTW:slot_of(at) * SLOTW + width], src
                             ).then_inc(slot_full[slot_of(at)], 16)

            src = {"ada": w_ada, "win": w_win, "wqb": w_wqb, "wkvb": w_wkvb, "wo": w_wo,
                   "up": w_up, "down": w_down}
            for at, (name, l, j, w) in enumerate(STREAM):
                slab(at, src[name][j] if name in ("ada", "up", "down") else src[name][l, j], w)
            sp.wait_ge(*used_up(len(STREAM) - 1))
            sp.sem_inc(sem("lo_done"), 3 * XSLOT)

            def expert_slabs(i, q, base):
                for j in range(XSLOT):
                    sp.wait_ge(sem("lo_done"), i * (3 * NFX) + q * (3 * XSLOT) + (3 * j + 3))
                    sp.dma_start(xring[:, j * SLOTW:(j + 1) * SLOTW],
                                 w_moe[bass.ds(base + q * XSLOT + j, 1)].rearrange("a p n -> (a p) n")
                                 ).then_inc(xslot_full[j], 16)

            for j in range(XSLOT):
                sp.dma_start(xring[:, j * SLOTW:(j + 1) * SLOTW], w_moe[j]).then_inc(xslot_full[j], 16)
            with sp.Fori(1, NFX // XSLOT) as q:
                expert_slabs(0, q, 0)
            sp.wait_ge(sem("ids_ready"), 1)
            n_items = sp.value_load(ids[0:1, ITEMS:ITEMS + 1], min_val=NX, max_val=ITEMS)
            with sp.Fori(1, n_items) as i:
                e = sp.value_load(ids[0:1, bass.ds(i, 1)], min_val=0, max_val=NX - 1)
                with sp.Fori(0, NFX // XSLOT) as q:
                    expert_slabs(i, q, e * NFX)

        @block.tensor
        def _(pe):
            mm = nc.tensor.matmul

            def use(name):
                b, n = PLAN[name]
                if n:
                    pe.wait_ge(bank_free[b], n)
                return banks[b]

            def full(ins, name):
                ins.then_inc(bank_full[PLAN[name][0]], 1)

            def slab(at, width):
                pe.wait_ge(slot_full[slot_of(at)], fills(at))
                return ring[:, slot_of(at) * SLOTW:slot_of(at) * SLOTW + width]

            def sum_squares(l, name, src, mat=ones):
                o = use(("ss", l, name))
                pe.wait_ge(squares_ready, RMS[l, name] + 1)
                for k, a in enumerate(src):
                    last = mm(o[:, 0:a.shape[1]], mat, a, start=k == 0, stop=k == len(src) - 1)
                full(last, ("ss", l, name))

            pe.wait_ge(sem("consts_loaded"), 16)
            pe.wait_ge(sem("x_loaded"), 48)
            for k in range(KD):
                o = use(("x", k))
                for g, (t0, n) in enumerate(TB):
                    last = nc.tensor.transpose(o[:, t0:t0 + n], x_tok[0:n, g, 128 * k:128 * k + 128], ident[0:n, 0:n])
                full(last, ("x", k))

            def modulation(place):
                for kind, n in ADA_STEPS[place]:
                    o = use((kind, n))
                    if kind == "rows":
                        w = slab(POS["ada", 0, n], 3072).rearrange("p (k n) -> p k n", k=KD)
                        for k in range(KD):
                            r = 32 * (k % 4)
                            last = mm(o[r:r + 32, 0:384], scond[:, k, :], w[:, k], start=k < 4, stop=k >= 4)
                    else:
                        pe.wait_ge(sem("modrow_ready"), n + 1)
                        for f in range(3):
                            last = nc.tensor.transpose(o[:, 128 * f:128 * f + 128],
                                                       modrow[:, n % 2, 128 * f:128 * f + 128], ident)
                    full(last, (kind, n))

            for l in range(DEPTH):
                sum_squares(l, "n1", [sq8_f[:, k * T:(k + 1) * T] for k in range(KD)])
                if l == 0:
                    pe.wait_ge(sem("cond_silu"), 1)
                    modulation(("start", 0))
                modulation(("h1", l))
                pe.wait_ge(sem("h1_ready"), l + 1)
                for j in range(NP):
                    o = use(("p", l, j))
                    w = slab(POS["win", l, j // 2], 2048).rearrange("p (f k n) -> p f k n", f=2, k=KD)
                    for k in range(KD):
                        last = mm(o[:, 0:T], w[:, j % 2, k], hT[:, k * T:(k + 1) * T], start=k == 0, stop=k == KD - 1)
                    full(last, ("p", l, j))
                modulation(("win", l))
                sum_squares(l, "ckv", [sq4[:, k] for k in range(2)])
                sum_squares(l, "kpe", [sq1[:, 0]], ones64)
                sum_squares(l, "cq", [sq4[:, k] for k in range(3)])
                o = use(("rotk", l))
                pe.wait_ge(normed, RMS[l, "kpe"] + 1)
                full(mm(o[:, 0:T], rot, kpe_all[:, 0:T], start=True, stop=True), ("rotk", l))
                for h in range(HEADS):
                    o = use(("vt", l, h))
                    await_done(pe, ("p", l, PI + h))
                    for g, (t0, n) in enumerate(TB):
                        last = nc.tensor.transpose(o[0:n, 128 * g:128 * g + 128], proj[:, PI + h, t0:t0 + n], ident)
                    full(last, ("vt", l, h))
                pe.wait_ge(sem("cache_loaded"), 48 * (l + 1))
                for j in range(3):
                    o = use(("cache", l, j))
                    for b in range(2):
                        last = nc.tensor.transpose(o[:, 128 * b:128 * b + 128], cache_tok[:, b, 128 * j:128 * j + 128], ident)
                    full(last, ("cache", l, j))
                pe.wait_ge(sem("kd_ready"), l + 1)
                for h in range(HEADS):
                    o = use(("kd", l, h))
                    for g, (t0, n) in enumerate(TB):
                        last = nc.tensor.transpose(o[0:n, 128 * g:128 * g + 128],
                                                   tmp[:, h * T + t0:h * T + t0 + n], ident)
                    full(last, ("kd", l, h))
                for h in range(HEADS):
                    o = use(("sc", l, h))
                    pe.wait_ge(sem("kt_ready"), 4 * l + h + 1)
                    for g, (t0, n) in enumerate(TB):
                        for b in range(NB_):
                            dst = o[0:n, t0:t0 + n].rearrange("p (c b s) -> p c b s", b=NB_, s=SUB)[:, :, b, :]
                            q = qt[:, h, t0:t0 + n].rearrange("p (c b s) -> p c b s", b=NB_, s=SUB)[:, :, b, :]
                            last = mm(dst, kt_buf(h)[:, b * T + t0:b * T + t0 + n], q, start=True, stop=True)
                    full(last, ("sc", l, h))
                for h in range(HEADS):
                    o = use(("o", l, h))
                    await_done(pe, ("sc", l, h))
                    if h == 0:
                        pe.wait_ge(sem("v_tok_ready"), 8 * (l + 1))
                    for g, (t0, n) in enumerate(TB):
                        mm(o[:, t0:t0 + n], v_tok[0:n, g, 128 * h:128 * h + 128], sT[0:n, h, t0:t0 + n],
                           start=g == 0, stop=False, skip_group_check=True)
                pe.wait_ge(sem("kd_tok_ready"), 8 * (l + 1))
                pe.wait_ge(sem("qe_ready"), l + 1)

                def inter(c):
                    if c < NC_ - 1:
                        pe.wait_ge(sem("state_ready"), 8 * l + c)
                        s = states[:, c % 2]
                    else:
                        pe.wait_ge(sem("state_loaded"), 16 * (l + 1))
                        s = s_smp
                    for h in range(HEADS):
                        last = mm(banks[h][:, CH * c:CH * c + CH], s[:, 128 * h:128 * h + 128],
                                  qf[:, h * T + CH * c:h * T + CH * c + CH],
                                  start=False, stop=True, skip_group_check=True)
                        if c == NC_ - 1:
                            full(last, ("o", l, h))
                    if c < NC_ - 1:
                        last.then_inc(sem("state_used"), 1)

                for c in range(NC_):
                    o = use(("u", l, c))
                    g, r = divmod(CH * c, 128)
                    for h in range(HEADS):
                        last = mm(o[:, 128 * h:128 * h + 128], kd_tok[r:r + CH, g, 128 * h:128 * h + 128],
                                  v_tok[r:r + CH, g, 128 * h:128 * h + 128], start=True, stop=True)
                    full(last, ("u", l, c))
                    if c >= 2:
                        inter(c - 1)
                inter(NC_ - 1)
                for h in range(HEADS):
                    sum_squares(l, "o%d" % h, [sq1[:, RMS[l, "o%d" % h] % 2]])
                wq = slab(POS["wqb", l, 0], 2304).rearrange("p (k n) -> p k n", k=3)
                pe.wait_ge(normed, RMS[l, "cq"] + 1)
                for j in range(6):
                    o = use(("q", l, j))
                    for k in range(3):
                        last = mm(o[:, 0:T], wq[:, k, 128 * j:128 * j + 128], proj[:, PCQ + k, :],
                                  start=k == 0, stop=k == 2)
                    full(last, ("q", l, j))
                    if j:
                        sum_squares(l, "q%d" % (j - 1), [sq1[:, RMS[l, "q%d" % (j - 1)] % 2]],
                                    ones64 if j - 1 >= 4 else ones)
                sum_squares(l, "q5", [sq1[:, RMS[l, "q5"] % 2]], ones64)
                for j in range(2):
                    o = use(("rotq", l, j))
                    pe.wait_ge(normed, RMS[l, "q%d" % (4 + j)] + 1)
                    full(mm(o[:, 0:T], rot, qpe[:, j, :], start=True, stop=True), ("rotq", l, j))
                wk = slab(POS["wkvb", l, 0], 2048).rearrange("p (k n) -> p k n", k=2)
                pe.wait_ge(sem("ckv_all_ready"), 2 * (l + 1))
                for j in range(8):
                    h, (t0, n) = j // 2, ((0, T), (T, PAST))[j % 2]
                    o = use(("k", l, j))
                    for k in range(2):
                        last = mm(o[:, 0:n], wk[:, k, 128 * h:128 * h + 128], ckv_all[:, k, t0:t0 + n],
                                  start=k == 0, stop=k == 1)
                    full(last, ("k", l, j))
                    if j:
                        sum_squares(l, "k%d" % (j - 1), [sq1[:, RMS[l, "k%d" % (j - 1)] % 2, 0:(T, PAST)[(j - 1) % 2]]])
                sum_squares(l, "k7", [sq1[:, RMS[l, "k7"] % 2, 0:PAST]])
                for b, (t0, n) in enumerate(VBLK):
                    o = use(("v", l, b))
                    for k in range(2):
                        last = mm(o[0:n, :], ckv_all[:, k, t0:t0 + n], wk[:, k, 512:1024], start=k == 0, stop=k == 1)
                    full(last, ("v", l, b))
                pe.wait_ge(sem("kpe_ready"), l + 1)
                for g, (t0, n) in enumerate(TB):
                    o = use(("ckvo", l, g))
                    for k in range(2):
                        nc.tensor.transpose(o[0:n, 128 * k:128 * k + 128], ckv_all[:, k, t0:t0 + n], ident)
                    full(nc.tensor.transpose(o[0:n, 256:384], kpe_all[:, t0:t0 + n], ident), ("ckvo", l, g))
                pe.wait_ge(sem("qpe_ready"), 2 * (l + 1))
                pe.wait_ge(normed, RMS[l, "k7"] + 1)
                pe.wait_ge(sem("vals_ready"), 5 * (l + 1))

                def scores(h, b):
                    k0, nk, q0, nq = QB[b]
                    o = use(("s", l, h, b))
                    r = 64 * (h % 2)
                    mm(o[0:nq, 0:nk], qn[:, h, q0:q0 + nq], kn[:, h, k0:k0 + nk], start=True, stop=False)
                    if b < 2:
                        mm(o[0:nq, nk - 128:nk], cst[0:1, CMQ:CMQ + 128], cst[0:1, CMK:CMK + 128],
                           start=False, stop=False, skip_group_check=True)
                    last = mm(o[0:nq, 0:nk], qpe[r:r + 64, h // 2, q0:q0 + nq], kpe_all[r:r + 64, k0:k0 + nk],
                              start=False, stop=True)
                    full(last, ("s", l, h, b))

                def mix(h, b):
                    k0, nk, q0, nq = QB[b]
                    i = 3 * h + b
                    o = use(("pT", l, h, b))
                    pe.wait_ge(sem("probs_ready"), 12 * l + i + 1)
                    for n_, kb in enumerate(BLK_OF[b]):
                        t0, n = VBLK[kb]
                        last = nc.tensor.transpose(o[0:n, nq * n_:nq * n_ + nq], probs[0:nq, i % 2, t0 - k0:t0 - k0 + n],
                                                   ident[0:nq, 0:nq])
                    full(last, ("pT", l, h, b))

                def weigh(h, b):
                    k0, nk, q0, nq = QB[b]
                    i = 3 * h + b
                    o = use(("oT", l, h)) if b == 0 else ps(("oT", l, h))
                    pe.wait_ge(sem("pT_ready"), 12 * l + i + 1)
                    for n_, kb in enumerate(BLK_OF[b]):
                        t0, n = VBLK[kb]
                        last = mm(o[:, q0:q0 + nq], vals[0:n, kb, 128 * h:128 * h + 128],
                                  pT[0:n, i % 2, nq * n_:nq * n_ + nq],
                                  start=n_ == 0, stop=n_ == len(BLK_OF[b]) - 1)
                    if b == 2:
                        full(last, ("oT", l, h))

                todo = [(h, b) for h in range(HEADS) for b in range(3)]
                for i in range(14):
                    if i < 12:
                        scores(*todo[i])
                        modulation(("att", l, i))
                    if 1 <= i < 13:
                        mix(*todo[i - 1])
                    if i >= 2:
                        weigh(*todo[i - 2])
                sum_squares(l, "om", [sq4[:, k] for k in range(4)])
                pe.wait_ge(sem("mix_ready"), 5 * (l + 1))
                for k in range(KD):
                    o = use(("wo", l, k))
                    w = slab(POS["wo", l, k // 2], 2048).rearrange("p (f k n) -> p f k n", f=2, k=KD)
                    for j in range(8):
                        m = proj[:, (PG + j) if j < 4 else (PI + j - 4), :]
                        last = mm(o[:, 0:T], w[:, k % 2, j], m, start=j == 0, stop=j == 7)
                    full(last, ("wo", l, k))
                sum_squares(l, "n2", [sq8_f[:, k * T:(k + 1) * T] for k in range(KD)])
                modulation(("n2", l))
                pe.wait_ge(sem("h2_ready"), l + 1)
                if l == 0:
                    for b in range(8):
                        pe.wait_ge(bank_free[b], PLAN["before the dense layer"][b])

                    def three(o, w, a_hi, a_lo, start, stop):
                        mm(o, w[0], a_hi, start=start, stop=False)
                        mm(o, w[1], a_hi, start=False, stop=False)
                        return mm(o, w[0], a_lo, start=False, stop=stop)

                    def up(q, j):
                        pe.wait_ge(sem("gu_read"), q * NSLOT + j + 1)
                        for u in range(2):
                            pe.wait_ge(sem("ffn_lo"), q * (2 * NSLOT) + (2 * j + u + 1))
                            for k in range(KD):
                                w = [x[:, u, 128 * k:128 * k + 128] for x in (wf_hi, wf_lo)]
                                last = three(banks[2 * (j % 3) + u][:, 0:T], w, h_hi[:, k * T:(k + 1) * T],
                                             h_lo[:, k * T:(k + 1) * T], k == 0, k == KD - 1)
                            last.then_inc(sem("ffn_piece_done"), 1)

                    pe.wait_ge(sem("h_split"), 2)
                    with pe.Fori(0, NF // NSLOT) as q:
                        for j in range(NSLOT):
                            up(q, j)
                    for j in range(NF % NSLOT):
                        up(NF // NSLOT, j)
                    pe.wait_ge(sem("gu_read"), NF + 3)
                    pe.wait_ge(sem("a_split"), NF + 2)
                    for k in range(KD):
                        o = use(("down", k))
                        for p in range(DOWN_PIECES):
                            n = 2 * NF + DOWN_PIECES * k + p
                            pe.wait_ge(sem("ffn_lo"), n + 1)
                            for f in range(8 * p, min(8 * p + 8, NF)):
                                c = 128 * (f - 8 * p)
                                w = [x[:, n % 2, c:c + 128] for x in (wf_hi, wf_lo)]
                                last = three(o[:, 0:T], w, aT_hi[:, f * T:(f + 1) * T], aT_lo[:, f * T:(f + 1) * T],
                                             f == 0, f == NF - 1)
                            if p < DOWN_PIECES - 1:
                                last.then_inc(sem("ffn_piece_done"), 1)
                        full(last, ("down", k))
            o = use(("logits",))
            pe.wait_ge(sem("router_loaded"), 16)
            for g, (t0, n) in enumerate(TB):
                for k in range(KD):
                    last = mm(o[0:n, NX * g:NX * g + NX], hT[:, k * T + t0:k * T + t0 + n], router[:, k],
                              start=k == 0, stop=k == KD - 1)
            full(last, ("logits",))
            for g, (t0, n) in enumerate(TB):
                for f in range(2):
                    o = use(("ht", g, f))
                    for k in range(4):
                        last = nc.tensor.transpose(o[0:n, 128 * k:128 * k + 128],
                                                   hT[:, (4 * f + k) * T + t0:(4 * f + k) * T + t0 + n], ident)
                    full(last, ("ht", g, f))
            o = use(("rank",))
            pe.wait_ge(sem("chosen_ready"), 1)
            chosen = rt[:, 24:48].rearrange("p (g e) -> p g e", g=3)
            for g in range(3):
                for b in range(g + 1):
                    mm(o[:, NX * g:NX * g + NX], cst[:, CU:CU + 128] if b == g else ones, chosen[:, b],
                       start=b == 0, stop=b == g)
            for b in range(3):
                last = mm(o[:, 24:32], ones, chosen[:, b], start=b == 0, stop=b == 2)
            full(last, ("rank",))
            for b in range(8):
                pe.wait_ge(bank_free[b], PLAN["before the experts"][b])
            pe.wait_ge(sem("ids_ready"), 1)
            last_item = pe.value_load(ids[0:1, ITEMS + 1:ITEMS + 2], min_val=NX - 1, max_val=ITEMS - 1)
            pe.sem_inc(sem("down_done"), XSLOT)

            def gather(i):
                pe.wait_ge(sem("pick_ready"), i + 1)
                pe.wait_ge(sem("scatter_read"), i * KD + KD)
                pe.wait_ge(sem("gates_ready"), i + 1)
                for k in range(KD):
                    for g, (t0, n) in enumerate(TB):
                        last = mm(banks[6 + k // 4][:, 128 * (k % 4):128 * (k % 4) + 128],
                                  h_tok[0:n, g, 128 * k:128 * k + 128], pick[0:n, g, :], start=g == 0, stop=g == 2)
                    if k % 4 == 3:
                        last.then_inc(sem("gathered"), 1)

            def scatter(i, some=range(KD)):
                pe.wait_ge(sem("y_lo_ready"), i + 1)
                pe.wait_ge(sem("y_hi_ready"), i + 1)
                pe.wait_ge(sem("gates_ready"), i + 1)
                for k in some:
                    if k >= 2:
                        pe.wait_ge(sem("scatter_read"), i * KD + (KD + k - 1))
                    mm(banks[6 + k % 2][:, 0:T], ysb[:, 128 * k:128 * k + 128], gT, start=True, stop=True
                       ).then_inc(sem("scattered"), 1)

            def gates(i):
                pe.wait_ge(sem("pickg_ready"), i + 1)
                pe.wait_ge(sem("scatter_read"), i * KD + (2 * KD - 1))
                for g, (t0, n) in enumerate(TB):
                    last = nc.tensor.transpose(banks[6][:, t0:t0 + n], pickg[0:n, g, :], ident[0:n, 0:n])
                last.then_inc(sem("gates_turned"), 1)

            def item(i, more):
                pe.wait_ge(sem("hg_split"), i * 2 + 2)

                def gate_up(q, j):
                    pe.wait_ge(sem("lo_done"), i * (3 * NFX) + q * (3 * XSLOT) + (3 * j + 14))
                    pe.wait_ge(sem("at_split"), i * NFX + q * XSLOT + (j + 1))
                    for k in range(KD):
                        cols = slice(256 * k, 256 * k + 256)
                        mm(banks[j][:, 0:256], hg_hi[:, k], w_hi[:, j % 2, cols], start=k == 0, stop=False)
                        mm(banks[j][:, 0:256], hg_hi[:, k], w_lo[:, j % 2, cols], start=False, stop=False)
                        last = mm(banks[j][:, 0:256], hg_lo[:, k], w_hi[:, j % 2, cols], start=False, stop=k == KD - 1)
                    last.then_inc(sem("gate_up_full"), 1)

                def turn(q, j):
                    pe.wait_ge(sem("a_ready"), i * NFX + q * XSLOT + (j + 3))
                    nc.tensor.transpose(banks[j % 4][:, 256:384], aX[:, j % 2], ident).then_inc(sem("turned"), 1)

                def down(q, j, first=False):
                    pe.wait_ge(sem("at_split"), i * NFX + q * XSLOT + (j + 5))
                    pe.wait_ge(sem("lo_done"), i * (3 * NFX) + q * (3 * XSLOT) + (3 * j + 15))
                    for n, (a, w) in enumerate(((at_hi, wd_hi), (at_hi, wd_lo), (at_lo, wd_hi))):
                        for u in range(2):
                            last = mm(banks[4 + u][:, :], a[:, j % 4], w[:, j % 4, 512 * u:512 * u + 512],
                                      start=first and n == 0, stop=False, skip_group_check=True)
                    last.then_inc(sem("down_done"), 1)

                for j in range(4):
                    gate_up(0, j)
                    if j >= 1:
                        turn(0, j - 1)
                    scatter(i, SCATTER[j])
                    if j == 3:
                        gates(i)
                    if j >= 2:
                        down(0, j - 2, first=j == 2)
                with pe.Fori(1, NFX // XSLOT) as q:
                    for j in range(4):
                        gate_up(q, j)
                        turn(q, j - 1)
                        down(q, j - 2)
                if more:
                    gather(i + 1)
                turn(NFX // XSLOT, -1)
                down(NFX // XSLOT, -2)
                down(NFX // XSLOT, -1)

            gather(0)
            with pe.Fori(0, last_item) as i:
                item(i, True)
            item(last_item, False)
            scatter(last_item + 1)
            for f in range(2):
                pe.wait_ge(sem("y_final"), 4 * f + 4)
                for g, (t0, n) in enumerate(TB):
                    o = use(("y", g, f))
                    for k in range(4):
                        last = nc.tensor.transpose(o[0:n, 128 * k:128 * k + 128],
                                                   xT[:, (4 * f + k) * T + t0:(4 * f + k) * T + t0 + n], ident)
                    full(last, ("y", g, f))

        @block.scalar
        def _(act):
            A = nc.scalar.activation
            own = [0]

            def link(ins):
                own[0] += 1
                ins.then_inc(sem("scalar_step"), 1)
                act.wait_ge(sem("scalar_step"), own[0])

            def finish_norm(l, name, n, cols=T):
                r = RMS[l, name]
                dst = rstd[:, r % 2, 0:cols]
                if r >= 2:
                    act.wait_ge(normed, r - 1)
                take(act, ("ss", l, name))
                done(A(dst, ps(("ss", l, name))[:, 0:cols], ACT.Ln, bias=eps, scale=1.0 / n), ("ss", l, name))
                await_done(act, ("ss", l, name))
                A(dst, dst, ACT.Exp, scale=-0.5).then_inc(rstd_ready, 1)

            def modulation_rows(place):
                for n in ada_slabs(place):
                    if n >= 2:
                        take(act, ("turn", n - 2))
                    take(act, ("rows", n))
                    done(A(modrow[:, n % 2, :], ps(("rows", n))[:, 0:384], ACT.Copy), ("rows", n))
                    await_done(act, ("rows", n))
                    act.sem_inc(sem("modrow_ready"), 1)

            act.wait_ge(sem("cond_loaded"), 16)
            act.wait_ge(sem("scond_cleared"), 1)
            A(scond[:, :, 0:2], condT, ACT.Silu).then_inc(sem("cond_silu"), 1)
            for l in range(DEPTH):
                nc.scalar.preload_act_table_set("natural_log_exp_and_others")
                if l == 0:
                    act.wait_ge(sem("lb_diff"), 1)
                    A(lbw[:, 12:20], lbw[:, 4:12], ACT.Exp).then_inc(sem("lb_exp"), 1)
                    act.wait_ge(sem("xT_ready"), KD)
                    act.wait_ge(sem("eps_ready"), 1)
                else:
                    act.wait_ge(sem("ffn_x_ready"), KD)
                A(sq8_f, xT[:, :], ACT.Square).then_inc(squares_ready, 1)
                finish_norm(l, "n1", D)
                if l == 0:
                    modulation_rows(("start", 0))
                modulation_rows(("h1", l))
                nc.scalar.preload_act_table_set("sigmoid_and_others")
                for j in range(PI):
                    name = ("p", l, j)
                    take(act, name)
                    if j < PQ:
                        done(A(proj[:, j], ps(name)[:, 0:T], ACT.Sigmoid, scale=-1.0), name)
                    else:
                        i = j - PQ
                        if 8 * l + i >= 2:
                            act.wait_ge(sem("silu_done"), 8 * l + i - 1)
                        A(sg1[:, i % 2], ps(name)[:, 0:T], ACT.Sigmoid).then_inc(sem("sigmoid_ready"), 1)
                nc.scalar.preload_act_table_set("natural_log_exp_and_others")

                def plain(tiles_):
                    for j in tiles_:
                        take(act, ("p", l, j))
                        done(A(proj[:, j], ps(("p", l, j))[:, 0:T], ACT.Copy), ("p", l, j))

                def key_decays(h):
                    act.wait_ge(sem("diff_ready"), 6 * l + 3 + h)
                    for b in range(NB_):
                        e = kt_buf(h)[:, b * T:(b + 1) * T].rearrange("p (c s) -> p c s", s=CH)[:, :, 0:SUB * (b + 1)]
                        last = A(e, e, ACT.Exp)
                    last.then_inc(sem("diff_exp"), 1)

                act.wait_ge(sem("k_ready"), 4 * (l + 1))
                A(tmp, kf, ACT.Ln, scale=-1.0, bias=1.0).then_inc(sem("logf_ready"), 1)
                plain(range(PI, PI + 2))
                act.wait_ge(sem("diff_ready"), 6 * l + 1)
                A(tmp, tmp, ACT.Exp).then_inc(sem("diff_exp"), 1)
                plain(range(PI + 2, PI + 3))
                act.wait_ge(sem("diff_ready"), 6 * l + 2)
                A(tmp, tmp, ACT.Exp).then_inc(sem("diff_exp"), 1)
                plain(range(PI + 3, PC + 1))
                key_decays(0)
                plain(range(PC + 1, NP))
                for j in (PC, PC + 1, PK, PCQ, PCQ + 1, PCQ + 2):
                    await_done(act, ("p", l, j))
                A(sq4[:, 0:2], proj[:, PC:PC + 2], ACT.Square).then_inc(squares_ready, 1)
                A(sq1[:, 0], proj[:, PK], ACT.Square).then_inc(squares_ready, 1)
                modulation_rows(("win", l))
                finish_norm(l, "ckv", KVL)
                A(sq4[:, 0:3], proj[:, PCQ:PCQ + 3], ACT.Square).then_inc(squares_ready, 1)
                finish_norm(l, "kpe", ROPE)
                finish_norm(l, "cq", QL)
                for h in range(1, HEADS):
                    key_decays(h)
                A(bcum, bcum, ACT.Exp).then_inc(sem("eb_ready"), 1)
                for h in range(HEADS):
                    name = "o%d" % h
                    r = RMS[l, name]
                    take(act, ("o", l, h))
                    A(sq1[:, r % 2], ps(("o", l, h))[:, 0:T], ACT.Square).then_inc(squares_ready, 1)
                    if h:
                        finish_norm(l, "o%d" % (h - 1), 128)
                finish_norm(l, "o3", 128)
                for pre, cnt, width in (("q", 6, lambda j: T), ("k", 8, lambda j: (T, PAST)[j % 2])):
                    for j in range(cnt):
                        r = RMS[l, pre + str(j)]
                        take(act, (pre, l, j))
                        A(sq1[:, r % 2, 0:width(j)], ps((pre, l, j))[:, 0:width(j)], ACT.Square).then_inc(squares_ready, 1)
                        if j:
                            finish_norm(l, pre + str(j - 1), 64 if pre == "q" and j - 1 >= 4 else 128, width(j - 1))
                    finish_norm(l, pre + str(cnt - 1), 64 if pre == "q" else 128, width(cnt - 1))
                for b, (t0, n) in enumerate(VBLK):
                    take(act, ("v", l, b))
                    A(vals[0:n, b], ps(("v", l, b))[0:n, :], ACT.Copy).then_inc(sem("vals_ready"), 1)
                    act.wait_ge(sem("vals_ready"), 5 * l + b + 1)
                    act.sem_inc(bank_free[PLAN["v", l, b][0]], 1)
                for i in range(13):
                    if i < 12:
                        h, b = divmod(i, 3)
                        k0, nk, q0, nq = QB[b]
                        name = ("s", l, h, b)
                        act.wait_ge(sem("negmax_ready"), 12 * l + i + 1)
                        A(probs[0:nq, i % 2, 0:nk], ps(name)[0:nq, 0:nk], ACT.Exp, bias=negmax[0:nq, i:i + 1],
                          scale=SCALE, accum_out=rowsum[0:nq, i:i + 1]).then_inc(sem("exp_ready"), 1)
                        modulation_rows(("att", l, i))
                for h in range(HEADS):
                    act.wait_ge(sem("omla_ready"), 4 * l + h + 1)
                A(sq4[:, :], proj[:, PI:PI + 4], ACT.Square).then_inc(squares_ready, 1)
                finish_norm(l, "om", 512)
                act.wait_ge(sem("x1_ready"), KD * (l + 1))
                A(sq8_f, xT[:, :], ACT.Square).then_inc(squares_ready, 1)
                finish_norm(l, "n2", D)
                modulation_rows(("n2", l))
                if l == 0:
                    nc.scalar.preload_act_table_set("silu_and_others")

                    def round_up_piece(q, j, u):
                        s = slot_of(POS["up", 0, 0] + j) * SLOTW + u * D
                        act.wait_ge(slot_full[slot_of(POS["up", 0, 0] + j)], q * 16 + fills(POS["up", 0, 0] + j))
                        A(wf_hi[:, u], ring[:, s:s + D], ACT.Copy).then_inc(sem("ffn_hi"), 1)

                    def round_down_piece(d):
                        use_, count = piece_done(2 * NF + d - 2)
                        if use_:
                            take(act, use_)
                        else:
                            act.wait_ge(sem("ffn_piece_done"), count)
                        at = POS["down", 0, d // DOWN_PIECES]
                        c, n = D * (d % DOWN_PIECES), min(D, FF - D * (d % DOWN_PIECES))
                        act.wait_ge(slot_full[slot_of(at)], fills(at))
                        A(wf_hi[:, d % 2, 0:n], ring[:, slot_of(at) * SLOTW + c:slot_of(at) * SLOTW + c + n], ACT.Copy
                          ).then_inc(sem("ffn_hi"), 1)

                    def hidden(q, j, following):
                        act.wait_ge(sem("ffn_piece_done"), q * (2 * NSLOT) + (2 * j + 1))
                        following(0)
                        act.wait_ge(sem("gu_read"), q * NSLOT + j + 2)
                        A(sig_up[:, j % 2], banks[2 * (j % 3)][:, 0:T], ACT.Silu).then_inc(sem("silu_up"), 1)
                        act.wait_ge(sem("ffn_piece_done"), q * (2 * NSLOT) + (2 * j + 2))
                        following(1)
                        act.wait_ge(sem("gu_read"), q * NSLOT + j + 4)
                        A(aT_hi[:, bass.ds(q * (NSLOT * T) + j * T, T)], a_up[:, j % 2], ACT.Copy
                          ).then_inc(sem("a_rounded"), 1)

                    for u in range(2):
                        round_up_piece(0, 0, u)
                    for b in range(2):
                        act.wait_ge(sem("h2_ready"), 1)
                        A(h_hi[:, b * 4 * T:(b + 1) * 4 * T], hT[:, b * 4 * T:(b + 1) * 4 * T], ACT.Copy
                          ).then_inc(sem("h_rounded"), 1)
                    with act.Fori(0, NF // NSLOT) as q:
                        for j in range(NSLOT):
                            hidden(q, j, lambda u: round_up_piece(q, j + 1, u))
                    q = NF // NSLOT
                    for j in range(NF % NSLOT):
                        hidden(q, j, (lambda u: round_up_piece(q, j + 1, u)) if j < NF % NSLOT - 1 else round_down_piece)
                    for d in range(2, KD * DOWN_PIECES):
                        round_down_piece(d)
            nc.scalar.preload_act_table_set("exp_and_others")
            for g, (t0, n) in enumerate(TB):
                for f in range(2):
                    take(act, ("ht", g, f))
                    done(A(h_tok[0:n, g, 512 * f:512 * f + 512], ps(("ht", g, f))[0:n, :], ACT.Copy), ("ht", g, f))
            act.wait_ge(sem("logit_diff"), 1)
            A(rt[:, 48:72], rt[:, 48:72], ACT.Exp).then_inc(sem("logit_exp"), 1)
            nc.scalar.preload_act_table_set("silu_and_others")

            def split_hi(i, q, j):
                s = j % 4 * SLOTW
                act.wait_ge(xslot_full[j % 4], i * (16 * NFX // XSLOT) + q * 16 + 16 * (j // 4 + 1))
                for p in range(2):
                    A(w_hi[:, j % 2, D * p:D * p + D], xring[:, s + D * p:s + D * p + D], ACT.Copy
                      ).then_inc(sem("hi_done"), 1)
                act.wait_ge(sem("down_done"), i * NFX + q * XSLOT + (j + 1))
                A(wd_hi[:, j % 4], xring[:, s + 2 * D:s + 3 * D], ACT.Copy).then_inc(sem("hi_done"), 1)

            def tokens_hi(i):
                for b in range(2):
                    act.wait_ge(sem("gathered"), i * 2 + (b + 1))
                    A(hg_hi[:, 4 * b:4 * b + 4], banks[6 + b][:, :].rearrange("p (k n) -> p k n", k=4), ACT.Copy
                      ).then_inc(sem("hg_rounded"), 1)

            def item(i, more):
                def silu(q, j):
                    act.wait_ge(sem("gate_up_full"), i * NFX + q * XSLOT + (j + 1))
                    act.wait_ge(sem("a_ready"), i * NFX + q * XSLOT + (j + 1))
                    A(sgX[:, j % 2], banks[j][:, 0:128], ACT.Silu).then_inc(sem("silu_x"), 1)

                def hidden_hi(q, j):
                    act.wait_ge(sem("turned"), i * NFX + q * XSLOT + (j + 1))
                    act.wait_ge(sem("down_done"), i * NFX + q * XSLOT + (j + 1))
                    A(at_hi[:, j % 4], banks[j % 4][:, 256:384], ACT.Copy).then_inc(sem("at_rounded"), 1)

                for j in range(4):
                    silu(0, j)
                    if j:
                        hidden_hi(0, j - 1)
                    split_hi(i, 0, j + 2)
                    if j == 3:
                        act.wait_ge(sem("gates_turned"), i + 1)
                        A(gT, banks[6][:, 0:T], ACT.Copy).then_inc(sem("gates_ready"), 1)
                with act.Fori(1, NFX // XSLOT - 1) as q:
                    for j in range(4):
                        silu(q, j)
                        hidden_hi(q, j - 1)
                        split_hi(i, q, j + 2)
                q = NFX // XSLOT - 1
                for j in range(4):
                    silu(q, j)
                    hidden_hi(q, j - 1)
                    if j < 3 and (j < 2 or more):
                        split_hi(i, q, j + 2)
                if more:
                    tokens_hi(i + 1)
                hidden_hi(q, 3)
                if more:
                    split_hi(i, q, 5)
                act.wait_ge(sem("down_done"), i * NFX + (NFX + XSLOT))
                A(ysb[:, 0:512], banks[4][:, :], ACT.Copy).then_inc(sem("y_lo_ready"), 1)

            split_hi(0, 0, 0)
            act.wait_ge(sem("ids_ready"), 1)
            last_item = act.value_load(ids[0:1, ITEMS + 1:ITEMS + 2], min_val=NX - 1, max_val=ITEMS - 1)
            tokens_hi(0)
            split_hi(0, 0, 1)
            with act.Fori(0, last_item) as i:
                item(i, True)
            item(last_item, False)
            for g, (t0, n) in enumerate(TB):
                take(act, ("y", g, 0))
                A(y_tok[0:n, g, 0:512], ps(("y", g, 0))[0:n, :], ACT.Copy).then_inc(sem("y_left_ready"), 1)

        @block.vector
        def _(dve):
            v = nc.vector
            own = [0]

            def link(ins):
                own[0] += 1
                ins.then_inc(sem("vector_step"), 1)
                dve.wait_ge(sem("vector_step"), own[0])

            def scaled(l, name, dst, src, w):
                r = RMS[l, name]
                return v.scalar_tensor_tensor(dst, src, w, rstd[:, r % 2, 0:dst.shape[-1]], ALU.mult, ALU.mult)

            def modulation_sums(place):
                for kind, n in ADA_STEPS[place]:
                    if kind == "turn":
                        l, j = divmod(n, ADA)
                        take(dve, ("turn", n))
                        done(v.tensor_reduce(mods[l][:, 3 * j:3 * j + 3, :],
                                             ps(("turn", n))[:, 0:384].rearrange("p (f r g) -> p f g r", f=3, r=4)[:, :, 0:2, :],
                                             AX.X, ALU.add), ("turn", n))
                        await_done(dve, ("turn", n))
                        link(v.tensor_tensor(mods[l][:, 3 * j:3 * j + 3, :], mods[l][:, 3 * j:3 * j + 3, :],
                                             V(l, VB + 3 * j, 3).unsqueeze(2).to_broadcast([128, 3, 2]), ALU.add))

            def modulate(l, which, name):
                c, vn = ((8, VN1), (32, VN2))[which]
                for g in range(2):
                    last = v.scalar_tensor_tensor(gain[l][:, which, :, g], mods[l][:, c:c + 8, g], 1.0, V(l, vn, 8),
                                                  ALU.add, ALU.mult)
                link(last)
                r = RMS[l, name]
                dve.wait_ge(rstd_ready, r + 1)
                for k in range(KD):
                    for g, t0, n in GRP:
                        last = v.scalar_tensor_tensor(hT[:, k * T + t0:k * T + t0 + n], xT[:, k * T + t0:k * T + t0 + n],
                                                      gain[l][:, which, k, g:g + 1], rstd[:, r % 2, t0:t0 + n],
                                                      ALU.mult, ALU.mult)
                last.then_inc(normed, 1)
                dve.wait_ge(normed, r + 1)
                sh = 0 if which == 0 else 24
                for k in range(KD):
                    for g, t0, n in GRP:
                        a = hT[:, k * T + t0:k * T + t0 + n]
                        last = v.tensor_scalar(a, a, mods[l][:, sh + k, g:g + 1], None, ALU.add)
                last.then_inc(sem("h1_ready" if which == 0 else "h2_ready"), 1)

            def mask_scores(l, h):
                name = ("sc", l, h)
                take(dve, name)
                cm = cst[:, CCM:CCM + 128]
                link(v.tensor_tensor(sT[:, h, 0:256].rearrange("p (g n) -> p g n", g=2),
                                     ps(name)[:, 0:256].rearrange("p (g n) -> p g n", g=2),
                                     cm.unsqueeze(1).to_broadcast([128, 2, 128]), ALU.mult))
                done(v.tensor_tensor(sT[0:32, h, 256:T], ps(name)[0:32, 256:T], cm[0:32, 0:32], ALU.mult), name)

            def omla(l, h):
                take(dve, ("oT", l, h))
                done(v.tensor_copy(proj[:, PI + h], ps(("oT", l, h))[:, 0:T]), ("oT", l, h))
                await_done(dve, ("oT", l, h))
                dve.sem_inc(sem("omla_ready"), 1)

            def add_gated(l, name, k, col, signal):
                take(dve, name)
                for g, t0, n in GRP:
                    x = xT[:, k * T + t0:k * T + t0 + n]
                    last = v.scalar_tensor_tensor(x, ps(name)[:, t0:t0 + n], mods[l][:, col + k, g:g + 1], x,
                                                  ALU.mult, ALU.add)
                done(last, name)
                await_done(dve, name)
                dve.sem_inc(sem(signal), 1)

            v.memset(scond, 0.0).then_inc(sem("scond_cleared"), 1)
            v.memset(eps, EPS).then_inc(sem("eps_ready"), 1)
            dve.wait_ge(sem("vecs_loaded"), 16)
            dve.wait_ge(sem("consts_loaded"), 16)
            link(v.tensor_tensor(lbw[:, 0:4], V(0, VLB, 4), V(1, VLB, 4), ALU.max))
            v.tensor_tensor(lbw[:, 4:8], V(0, VLB, 4), lbw[:, 0:4], ALU.subtract)
            link(v.tensor_tensor(lbw[:, 8:12], V(1, VLB, 4), lbw[:, 0:4], ALU.subtract))
            v.memset(oml[:, 0, :], 1.0).then_inc(sem("lb_diff"), 1)
            dve.wait_ge(sem("lb_exp"), 1)
            link(v.tensor_tensor(lbw[:, 0:4], lbw[:, 12:16], lbw[:, 16:20], ALU.add))
            link(v.reciprocal(lbw[:, 0:4], lbw[:, 0:4]))
            link(v.tensor_tensor(oml[:, 1, :], lbw[:, 0:4], lbw[:, 12:16], ALU.mult))
            for k in range(KD):
                take(dve, ("x", k))
                done(v.tensor_copy(xT[:, k * T:(k + 1) * T], ps(("x", k))[:, 0:T]), ("x", k))
            for k in range(KD):
                await_done(dve, ("x", k))
                dve.sem_inc(sem("xT_ready"), 1)
            for l in range(DEPTH):
                if l == 0:
                    modulation_sums(("start", 0))
                modulate(l, 0, "n1")
                modulation_sums(("h1", l))
                for h in range(HEADS):
                    await_done(dve, ("p", l, PF + h))
                for h in range(HEADS):
                    v.tensor_scalar(kf[:, h * T:(h + 1) * T], kf[:, h * T:(h + 1) * T], oml[:, l, h:h + 1], None,
                                    ALU.mult).then_inc(sem("k_ready"), 1)
                for j in range(PQ, PI):
                    i = j - PQ
                    name = ("p", l, j)
                    dve.wait_ge(sem("sigmoid_ready"), 8 * l + i + 1)
                    v.tensor_tensor(proj[:, j], ps(name)[:, 0:T], sg1[:, i % 2], ALU.mult).then_inc(sem("silu_done"), 1)
                    dve.wait_ge(sem("silu_done"), 8 * l + i + 1)
                    dve.sem_inc(bank_free[PLAN[name][0]], 1)
                dve.wait_ge(sem("logf_ready"), l + 1)
                link(v.tensor_tensor_scan(bcum, cst[:, CRS:CRS + HEADS * T], tmp, 0.0, ALU.mult, ALU.add))
                b4 = bcum.rearrange("p (c b s) -> p c b s", b=NB_, s=SUB)
                b3 = bcum.rearrange("p (c s) -> p c s", s=CH)
                ref3 = ref.rearrange("p (c b) -> p c b", b=NB_)
                link(v.memset(ref3[:, :, 0], 0.0))
                link(v.tensor_copy(ref3[:, :, 1:NB_], b4[:, :, 0:NB_ - 1, SUB - 1]))
                v.tensor_tensor(tmp.rearrange("p (n s) -> p n s", s=SUB), bcum.rearrange("p (n s) -> p n s", s=SUB),
                                ref.unsqueeze(2).to_broadcast([128, HEADS * T // SUB, SUB]), ALU.subtract
                                ).then_inc(sem("diff_ready"), 1)
                dve.wait_ge(sem("diff_exp"), 6 * l + 1)
                link(v.tensor_tensor(qt_f, qf, tmp, ALU.mult))
                v.tensor_tensor(tmp.rearrange("p (c s) -> p c s", s=CH),
                                b3[:, :, CH - 1:CH].to_broadcast([128, HEADS * NC_, CH]), b3, ALU.subtract
                                ).then_inc(sem("diff_ready"), 1)
                dve.wait_ge(sem("diff_exp"), 6 * l + 2)
                v.tensor_tensor(tmp, tmp, kf, ALU.mult).then_inc(sem("kd_ready"), 1)

                def lay_out_keys(h):
                    bh = bcum[:, h * T:(h + 1) * T].rearrange("p (c s) -> p c s", s=CH)
                    for b in range(NB_):
                        n = SUB * (b + 1)
                        e = kt_buf(h)[:, b * T:(b + 1) * T].rearrange("p (c s) -> p c s", s=CH)[:, :, 0:n]
                        last = v.tensor_tensor(e, ref3[:, h * NC_:(h + 1) * NC_, b:b + 1].to_broadcast([128, NC_, n]),
                                               bh[:, :, 0:n], ALU.subtract)
                    last.then_inc(sem("diff_ready"), 1)

                def finish_keys(h):
                    kh = kf[:, h * T:(h + 1) * T].rearrange("p (c s) -> p c s", s=CH)
                    dve.wait_ge(sem("diff_exp"), 6 * l + 3 + h)
                    for b in range(NB_):
                        n = SUB * (b + 1)
                        e = kt_buf(h)[:, b * T:(b + 1) * T].rearrange("p (c s) -> p c s", s=CH)[:, :, 0:n]
                        last = v.tensor_tensor(e, e, kh[:, :, 0:n], ALU.mult)
                    last.then_inc(sem("kt_ready"), 1)

                link(v.memset(ktil[:, :], 0.0))
                lay_out_keys(0)
                finish_keys(0)
                r = RMS[l, "ckv"]
                dve.wait_ge(rstd_ready, r + 1)
                for k in range(2):
                    last = scaled(l, "ckv", ckv_all[:, k, 0:T], proj[:, PC + k], V(l, VKV + k))
                last.then_inc(normed, 1)
                dve.wait_ge(rstd_ready, r + 2)
                scaled(l, "kpe", kpe_all[:, 0:T], proj[:, PK], V(l, VKR)).then_inc(normed, 1)
                dve.wait_ge(rstd_ready, r + 3)
                for k in range(3):
                    last = scaled(l, "cq", proj[:, PCQ + k], proj[:, PCQ + k], V(l, VQA + k))
                last.then_inc(normed, 1)
                modulation_sums(("win", l))
                take(dve, ("rotk", l))
                done(v.tensor_tensor(rot_tmp[:, :], ps(("rotk", l))[:, 0:T], sin, ALU.mult), ("rotk", l))
                link(v.tensor_tensor(kpe_all[:, 0:T], kpe_all[:, 0:T], cos, ALU.mult))
                await_done(dve, ("rotk", l))
                v.tensor_tensor(kpe_all[:, 0:T], kpe_all[:, 0:T], rot_tmp[:, :], ALU.add).then_inc(sem("kpe_ready"), 1)
                dve.wait_ge(sem("kpe_ready"), l + 1)
                def to_tokens(kind, dst):
                    for h in range(HEADS):
                        name = (kind, l, h)
                        take(dve, name)
                        s = ps(name)[:, 0:384].rearrange("p (g n) -> p g n", g=3)
                        v.tensor_copy(dst[:, 0:2, 128 * h:128 * h + 128], s[:, 0:2]).then_inc(
                            sem("v_tok_ready" if kind == "vt" else "kd_tok_ready"), 1)
                        v.tensor_copy(dst[0:32, 2, 128 * h:128 * h + 128], s[0:32, 2]).then_inc(
                            sem("v_tok_ready" if kind == "vt" else "kd_tok_ready"), 1)
                        dve.wait_ge(sem("v_tok_ready" if kind == "vt" else "kd_tok_ready"), 8 * l + 2 * h + 2)
                        dve.sem_inc(bank_free[PLAN[kind, l, h][0]], 1)

                take(dve, ("p", l, NP - 1))
                link(v.memset(hT[:, :], 0.0))
                lay_out_keys(1)
                to_tokens("vt", v_tok)
                finish_keys(1)
                for j in range(3):
                    name = ("cache", l, j)
                    take(dve, name)
                    dst = ckv_all[:, j, T:KEYS] if j < 2 else kpe_all[:, T:KEYS]
                    done(v.tensor_copy(dst, ps(name)[:, 0:PAST]), name)
                for j in range(3):
                    await_done(dve, ("cache", l, j))
                dve.sem_inc(sem("ckv_all_ready"), 2)
                to_tokens("kd", kd_tok)
                for h in range(2, HEADS):
                    take(dve, ("sc", l, h - 2))
                    lay_out_keys(h)
                    mask_scores(l, h - 2)
                    finish_keys(h)
                take(dve, ("sc", l, 2))
                mask_scores(l, 2)
                take(dve, ("sc", l, 3))
                mask_scores(l, 3)
                dve.wait_ge(sem("eb_ready"), l + 1)
                v.tensor_tensor(qf, qf, bcum, ALU.mult).then_inc(sem("qe_ready"), 1)
                for c in range(NC_):
                    name = ("u", l, c)
                    take(dve, name)
                    if 2 <= c < NC_ - 1:
                        dve.wait_ge(sem("state_used"), 7 * l + c - 1)
                    if l and c in (1, NC_ - 1):
                        dve.wait_ge(sem("state_out"), 32)
                    if c == NC_ - 1:
                        dve.wait_ge(sem("state_loaded"), 16 * (l + 1))
                    for h in range(HEADS):
                        hs = slice(128 * h, 128 * h + 128)
                        dec = bcum[:, h * T + CH * c + CH - 1:h * T + CH * c + CH]
                        if c == 0:
                            last = v.tensor_copy(states[:, 1, hs], ps(name)[:, hs])
                        elif c < NC_ - 1:
                            last = v.scalar_tensor_tensor(states[:, (c + 1) % 2, hs], states[:, c % 2, hs], dec,
                                                          ps(name)[:, hs], ALU.mult, ALU.add)
                        else:
                            last = v.scalar_tensor_tensor(s_new[:, hs], s_smp[:, hs], dec, ps(name)[:, hs],
                                                          ALU.mult, ALU.add)
                    done(last, name)
                    await_done(dve, name)
                    if c < NC_ - 1:
                        dve.sem_inc(sem("state_ready"), 1)
                    if c == NC_ - 1:
                        dve.sem_inc(sem("state_new"), 1)
                for h in range(HEADS):
                    r = RMS[l, "o%d" % h]
                    dve.wait_ge(rstd_ready, r + 1)
                    done(v.scalar_tensor_tensor(sg1[:, h % 2], ps(("o", l, h))[:, 0:T], V(l, VON), rstd[:, r % 2],
                                                ALU.mult, ALU.mult), ("o", l, h))
                    await_done(dve, ("o", l, h))
                    dve.sem_inc(normed, 1)
                    v.tensor_tensor(proj[:, PG + h], proj[:, PG + h], sg1[:, h % 2], ALU.mult).then_inc(sem("mix_ready"), 1)
                def rotate(j):
                    take(dve, ("rotq", l, j))
                    done(v.tensor_tensor(rot_tmp[:, :], ps(("rotq", l, j))[:, 0:T], sin, ALU.mult), ("rotq", l, j))
                    link(v.tensor_tensor(qpe[:, j], qpe[:, j], cos, ALU.mult))
                    await_done(dve, ("rotq", l, j))
                    v.tensor_tensor(qpe[:, j], qpe[:, j], rot_tmp[:, :], ALU.add).then_inc(sem("qpe_ready"), 1)
                    dve.wait_ge(sem("qpe_ready"), 2 * l + j + 1)

                for j in range(6):
                    r = RMS[l, "q%d" % j]
                    dve.wait_ge(rstd_ready, r + 1)
                    dst, w = (qn[:, j], V(l, VQN)) if j < 4 else (qpe[:, j - 4], V(l, VQR))
                    done(scaled(l, "q%d" % j, dst, ps(("q", l, j))[:, 0:T], w), ("q", l, j))
                    await_done(dve, ("q", l, j))
                    dve.sem_inc(normed, 1)
                for j in range(2):
                    rotate(j)
                for j in range(8):
                    t0, n = ((0, T), (T, PAST))[j % 2]
                    r = RMS[l, "k%d" % j]
                    dve.wait_ge(rstd_ready, r + 1)
                    done(scaled(l, "k%d" % j, kn[:, j // 2, t0:t0 + n], ps(("k", l, j))[:, 0:n], V(l, VKN)), ("k", l, j))
                    await_done(dve, ("k", l, j))
                    dve.sem_inc(normed, 1)
                for g, (t0, n) in enumerate(TB):
                    take(dve, ("ckvo", l, g))
                    if 3 * l + g >= 2:
                        dve.wait_ge(sem("rows_out%d" % ((l + g) % 2)), 32 * ((3 * l + g) // 2))
                    done(v.tensor_copy(kv_tok[0:n, (3 * l + g) % 2, :],
                                       ps(("ckvo", l, g))[0:n, 0:384]), ("ckvo", l, g))
                    await_done(dve, ("ckvo", l, g))
                    dve.sem_inc(sem("kv_tok_ready"), 1)
                for i in range(14):
                    if i < 12:
                        h, b = divmod(i, 3)
                        k0, nk, q0, nq = QB[b]
                        name = ("s", l, h, b)
                        take(dve, name)
                        link(v.reduce_max(rowmax[0:nq, i:i + 1], ps(name)[0:nq, 0:nk], AX.X))
                        v.tensor_scalar(negmax[0:nq, i:i + 1], rowmax[0:nq, i:i + 1], -SCALE, None, ALU.mult
                                        ).then_inc(sem("negmax_ready"), 1)
                    if 1 <= i < 13:
                        h, b = divmod(i - 1, 3)
                        k0, nk, q0, nq = QB[b]
                        dve.wait_ge(sem("exp_ready"), 12 * l + i)
                        dve.sem_inc(bank_free[PLAN["s", l, h, b][0]], 1)
                        link(v.reciprocal(rinv[0:nq, i - 1:i], rowsum[0:nq, i - 1:i]))
                        pr = probs[0:nq, (i - 1) % 2, 0:nk]
                        v.tensor_scalar(pr, pr, rinv[0:nq, i - 1:i], None, ALU.mult).then_inc(sem("probs_ready"), 1)
                        name = ("pT", l, h, b)
                        take(dve, name)
                        for n_, kb in enumerate(BLK_OF[b]):
                            n = VBLK[kb][1]
                            last = v.tensor_copy(pT[0:n, (i - 1) % 2, nq * n_:nq * n_ + nq], ps(name)[0:n, nq * n_:nq * n_ + nq])
                        done(last, name)
                        await_done(dve, name)
                        dve.sem_inc(sem("pT_ready"), 1)
                        if i >= 2 and (i - 2) % 3 == 2:
                            omla(l, (i - 2) // 3)
                    if i < 12:
                        modulation_sums(("att", l, i))
                omla(l, 3)
                r = RMS[l, "om"]
                dve.wait_ge(rstd_ready, r + 1)
                for h in range(HEADS):
                    last = scaled(l, "om", proj[:, PI + h], proj[:, PI + h], V(l, VMO + h))
                last.then_inc(normed, 1)
                dve.wait_ge(normed, r + 1)
                dve.sem_inc(sem("mix_ready"), 1)
                for k in range(KD):
                    add_gated(l, ("wo", l, k), k, 16, "x1_ready")
                modulate(l, 1, "n2")
                modulation_sums(("n2", l))
                if l == 0:
                    dve.sem_inc(sem("gu_read"), 3)
                    dve.sem_inc(sem("a_split"), 2)

                    def up_piece_rest(q, j, u):
                        s = slot_of(POS["up", 0, 0] + j) * SLOTW + u * D
                        dve.wait_ge(sem("ffn_hi"), q * (2 * NSLOT) + (2 * j + u + 1))
                        v.tensor_tensor(wf_lo[:, u], ring[:, s:s + D], wf_hi[:, u].bitcast(F32), ALU.subtract
                                        ).then_inc(sem("ffn_lo"), 1)

                    def down_piece_rest(d):
                        at = POS["down", 0, d // DOWN_PIECES]
                        c, n = D * (d % DOWN_PIECES), min(D, FF - D * (d % DOWN_PIECES))
                        dve.wait_ge(sem("ffn_hi"), 2 * NF + d + 1)
                        v.tensor_tensor(wf_lo[:, d % 2, 0:n], ring[:, slot_of(at) * SLOTW + c:slot_of(at) * SLOTW + c + n],
                                        wf_hi[:, d % 2, 0:n].bitcast(F32), ALU.subtract).then_inc(sem("ffn_lo"), 1)

                    def hidden(q, j, following):
                        following(0)
                        following(1)
                        dve.wait_ge(sem("silu_up"), q * NSLOT + j + 1)
                        dve.wait_ge(sem("ffn_piece_done"), q * (2 * NSLOT) + (2 * j + 2))
                        dve.wait_ge(sem("a_split"), q * NSLOT + j + 1)
                        v.tensor_tensor(a_up[:, j % 2], banks[2 * (j % 3) + 1][:, 0:T], sig_up[:, j % 2], ALU.mult
                                        ).then_inc(sem("gu_read"), 1)
                        dve.wait_ge(sem("a_rounded"), q * NSLOT + j + 1)
                        at = bass.ds(q * (NSLOT * T) + j * T, T)
                        v.tensor_tensor(aT_lo[:, at], a_up[:, j % 2], aT_hi[:, at].bitcast(F32), ALU.subtract
                                        ).then_inc(sem("a_split"), 1)

                    for u in range(2):
                        up_piece_rest(0, 0, u)
                    for b in range(2):
                        part = slice(b * 4 * T, (b + 1) * 4 * T)
                        dve.wait_ge(sem("h_rounded"), b + 1)
                        v.tensor_tensor(h_lo[:, part], hT[:, part], h_hi[:, part].bitcast(F32), ALU.subtract
                                        ).then_inc(sem("h_split"), 1)
                    with dve.Fori(0, NF // NSLOT) as q:
                        for j in range(NSLOT):
                            hidden(q, j, lambda u: up_piece_rest(q, j + 1, u))
                    q = NF // NSLOT
                    for j in range(NF % NSLOT):
                        hidden(q, j, (lambda u: up_piece_rest(q, j + 1, u)) if j < NF % NSLOT - 1 else down_piece_rest)
                    for d in range(KD * DOWN_PIECES):
                        if d + 2 < KD * DOWN_PIECES:
                            down_piece_rest(d + 2)
                        if d % DOWN_PIECES == DOWN_PIECES - 1:
                            k = d // DOWN_PIECES
                            add_gated(0, ("down", k), k, 40, "ffn_x_ready")
            def r3(a):
                return rt[:, a:a + 24].rearrange("p (g e) -> p g e", g=3)

            logit, chosen, ex, gate, key, order = r3(0), r3(24), r3(48), r3(80), r3(104), r3(248)
            top, total = rt[:, 72:75], rt[:, 75:78]
            nblk, end, start = rt[:, 128:136], rt[:, 136:144], rt[:, 144:152]
            base, eid = rt[:, 152:164], rt[:, 164:176]
            keyi = rt[:, 176:212].rearrange("p (g i) -> p g i", g=3)
            gatei = rt[:, 212:248].rearrange("p (g i) -> p g i", g=3)
            dve.wait_ge(sem("h2_ready"), DEPTH)
            v.memset(ysb[:, :], 0.0).then_inc(sem("y_lo_ready"), 1)
            dve.sem_inc(sem("y_hi_ready"), 1)
            v.memset(gT, 0.0).then_inc(sem("gates_ready"), 1)
            link(v.memset(logit[:, :, :], 0.0))
            take(dve, ("logits",))
            link(v.tensor_copy(rt[:, 0:16], ps(("logits",))[:, 0:16]))
            done(v.tensor_copy(rt[0:32, 16:24], ps(("logits",))[0:32, 16:24]), ("logits",))
            await_done(dve, ("logits",))
            link(v.tensor_reduce(top, logit, AX.X, ALU.max))
            v.tensor_tensor(ex, logit, top.unsqueeze(2).to_broadcast([128, 3, NX]), ALU.subtract
                            ).then_inc(sem("logit_diff"), 1)
            c4 = cmp8.rearrange("p (g e f) -> p g e f", g=3, e=NX)
            d4 = cmp8b.rearrange("p (g e f) -> p g e f", g=3, e=NX)
            lt = cst[:, CLT:CLT + 64].rearrange("p (e f) -> p e f", e=NX)
            for g in range(3):
                other = logit[:, g].unsqueeze(1).to_broadcast([128, NX, NX])
                this = logit[:, g].unsqueeze(2).to_broadcast([128, NX, NX])
                link(v.tensor_tensor(c4[:, g], other, this, ALU.is_gt))
                link(v.tensor_tensor(d4[:, g], other, this, ALU.is_equal))
                link(v.tensor_tensor(d4[:, g], d4[:, g], lt, ALU.mult))
            link(v.tensor_tensor(cmp8, cmp8, cmp8b, ALU.add))
            link(v.tensor_reduce(order, c4, AX.X, ALU.add))
            link(v.tensor_scalar(chosen, order, 1.5, None, ALU.is_lt))
            link(v.memset(chosen[32:64, 2], 0.0))
            link(v.memset(chosen[64:128, 2], 0.0))
            dve.sem_inc(sem("chosen_ready"), 1)
            dve.wait_ge(sem("logit_exp"), 1)
            link(v.tensor_tensor(ex, ex, chosen, ALU.mult))
            link(v.tensor_reduce(total, ex, AX.X, ALU.add))
            link(v.tensor_scalar(total, total, 1e-30, None, ALU.max))
            link(v.reciprocal(total, total))
            link(v.tensor_tensor(gate, ex, total.unsqueeze(2).to_broadcast([128, 3, NX]), ALU.mult))
            take(dve, ("rank",))
            rank = ps(("rank",))[:, 0:24].rearrange("p (g e) -> p g e", g=3)
            count = ps(("rank",))[:, 24:32]
            link(v.tensor_tensor(key, rank, chosen, ALU.mult))
            link(v.tensor_scalar(order, chosen, 1e4, -1e4, ALU.mult, ALU.add))
            link(v.tensor_tensor(key, key, order, ALU.add))
            link(v.tensor_scalar(nblk, count, SLOTS_X + 0.5, None, ALU.is_gt))
            done(v.tensor_scalar(start, count, 2 * SLOTS_X + 0.5, 1.0, ALU.is_gt, ALU.add), ("rank",))
            await_done(dve, ("rank",))
            link(v.tensor_tensor(nblk, nblk, start, ALU.add))
            link(v.tensor_tensor_scan(end, ones[:, 0:NX], nblk, 0.0, ALU.mult, ALU.add))
            link(v.tensor_tensor(start, end, nblk, ALU.subtract))
            oh = cmpi.rearrange("p (i e) -> p i e", e=NX)
            o2 = cmpi2.rearrange("p (i e) -> p i e", e=NX)
            full3 = [128, ITEMS, NX]
            it = cst[:, CIT:CIT + ITEMS].unsqueeze(2).to_broadcast(full3)
            link(v.tensor_tensor(oh, end.unsqueeze(1).to_broadcast(full3), it, ALU.is_gt))
            link(v.tensor_tensor(o2, start.unsqueeze(1).to_broadcast(full3), it, ALU.is_gt))
            link(v.tensor_tensor(oh, oh, o2, ALU.subtract))
            link(v.tensor_tensor(o2, it, start.unsqueeze(1).to_broadcast(full3), ALU.subtract))
            link(v.tensor_tensor(o2, o2, oh, ALU.mult))
            link(v.tensor_reduce(base, o2, AX.X, ALU.add))
            link(v.tensor_scalar(base, base, float(SLOTS_X), None, ALU.mult))
            link(v.tensor_tensor(o2, oh, cst[:, CEX:CEX + NX].unsqueeze(1).to_broadcast(full3), ALU.mult))
            link(v.tensor_reduce(eid, o2, AX.X, ALU.add))
            link(v.tensor_copy(ids[:, 0:ITEMS], eid))
            link(v.tensor_copy(ids[:, ITEMS:ITEMS + 1], end[:, NX - 1:NX]))
            link(v.tensor_scalar(end[:, NX - 1:NX], end[:, NX - 1:NX], -1.0, None, ALU.add))
            link(v.tensor_copy(ids[:, ITEMS + 1:ITEMS + 2], end[:, NX - 1:NX]))
            dve.sem_inc(sem("ids_ready"), 1)
            full4 = [128, 3, ITEMS, NX]
            oh4, o4 = oh.unsqueeze(1).to_broadcast(full4), cmp4.rearrange("p (g i e) -> p g i e", g=3, e=NX)
            link(v.tensor_tensor(o4, oh4, key.unsqueeze(2).to_broadcast(full4), ALU.mult))
            link(v.tensor_reduce(keyi, o4, AX.X, ALU.add))
            link(v.tensor_tensor(keyi, keyi, base.unsqueeze(1).to_broadcast([128, 3, ITEMS]), ALU.subtract))
            dve.sem_inc(sem("scatter_read"), KD)
            dve.sem_inc(sem("at_split"), XSLOT)
            dve.sem_inc(sem("a_ready"), 2)
            last_item = dve.value_load(ids[0:1, ITEMS + 1:ITEMS + 2], min_val=NX - 1, max_val=ITEMS - 1)
            io = cst[:, CIO:CIO + 128].unsqueeze(1).to_broadcast([128, 3, 128])

            def choose(i):
                v.tensor_tensor(pick, io, keyi[:, :, bass.ds(i, 1)].to_broadcast([128, 3, 128]), ALU.is_equal
                                ).then_inc(sem("pick_ready"), 1)

            def split_lo(i, q, j):
                s = j % 4 * SLOTW
                for p in range(3):
                    dve.wait_ge(sem("hi_done"), i * (3 * NFX) + q * (3 * XSLOT) + (3 * j + p + 1))
                    hi, lo = ((w_hi[:, j % 2, D * p:D * p + D], w_lo[:, j % 2, D * p:D * p + D]) if p < 2
                              else (wd_hi[:, j % 4], wd_lo[:, j % 4]))
                    v.tensor_tensor(lo, xring[:, s + D * p:s + D * p + D], hi.bitcast(F32), ALU.subtract
                                    ).then_inc(sem("lo_done"), 1)

            def tokens_lo(i):
                for b in range(2):
                    dve.wait_ge(sem("hg_rounded"), i * 2 + (b + 1))
                    v.tensor_tensor(hg_lo[:, 4 * b:4 * b + 4], banks[6 + b][:, :].rearrange("p (k n) -> p k n", k=4),
                                    hg_hi[:, 4 * b:4 * b + 4].bitcast(F32), ALU.subtract).then_inc(sem("hg_split"), 1)

            def add_scattered(i, some=range(KD)):
                for k in some:
                    dve.wait_ge(sem("scattered"), i * KD + (k + 1))
                    v.tensor_tensor(acc[:, k], acc[:, k], banks[6 + k % 2][:, 0:T], ALU.add
                                    ).then_inc(sem("scatter_read"), 1)

            def gated_to_x(k, src):
                for g, t0, n in GRP:
                    x = xT[:, k * T + t0:k * T + t0 + n]
                    last = v.scalar_tensor_tensor(x, src[:, t0:t0 + n], mods[DEPTH - 1][:, 40 + k, g:g + 1], x,
                                                  ALU.mult, ALU.add)
                last.then_inc(sem("x_summed"), 1)

            def item(i, more):
                dve.wait_ge(sem("pick_ready"), i + 1)
                v.tensor_tensor(pickg, pick, gatei[:, :, bass.ds(i, 1)].to_broadcast([128, 3, 128]), ALU.mult
                                ).then_inc(sem("pickg_ready"), 1)

                def multiply(q, j):
                    dve.wait_ge(sem("silu_x"), i * NFX + q * XSLOT + (j + 1))
                    v.tensor_tensor(aX[:, j % 2], banks[j][:, 128:256], sgX[:, j % 2], ALU.mult
                                    ).then_inc(sem("a_ready"), 1)

                def hidden_lo(q, j):
                    dve.wait_ge(sem("at_rounded"), i * NFX + q * XSLOT + (j + 1))
                    v.tensor_tensor(at_lo[:, j % 4], banks[j % 4][:, 256:384], at_hi[:, j % 4].bitcast(F32),
                                    ALU.subtract).then_inc(sem("at_split"), 1)

                for j in range(4):
                    multiply(0, j)
                    if j:
                        hidden_lo(0, j - 1)
                    add_scattered(i, SCATTER[j])
                    if j == 1 and more:
                        dve.wait_ge(sem("pickg_ready"), i + 1)
                        choose(i + 1)
                    if j == 3:
                        dve.wait_ge(sem("scatter_read"), i * KD + 2 * KD)
                    split_lo(i, 0, j + 2)
                with dve.Fori(1, NFX // XSLOT - 1) as q:
                    for j in range(4):
                        multiply(q, j)
                        hidden_lo(q, j - 1)
                        split_lo(i, q, j + 2)
                q = NFX // XSLOT - 1
                for j in range(4):
                    multiply(q, j)
                    hidden_lo(q, j - 1)
                    if j < 3 and (j < 2 or more):
                        split_lo(i, q, j + 2)
                    if j >= 2 and not more:
                        for k in range(4 * j - 8, 4 * j - 4):
                            gated_to_x(k, acc[:, k])
                if more:
                    tokens_lo(i + 1)
                hidden_lo(q, 3)
                if more:
                    split_lo(i, q, 5)
                dve.wait_ge(sem("down_done"), i * NFX + (NFX + XSLOT))
                v.tensor_copy(ysb[:, 512:1024], banks[5][:, :]).then_inc(sem("y_hi_ready"), 1)

            choose(0)
            link(v.tensor_tensor(o4, oh4, gate.unsqueeze(2).to_broadcast(full4), ALU.mult))
            link(v.tensor_reduce(gatei, o4, AX.X, ALU.add))
            take(dve, ("ht", 2, 1))
            link(v.memset(acc[:, :, :], 0.0))
            split_lo(0, 0, 0)
            tokens_lo(0)
            split_lo(0, 0, 1)
            with dve.Fori(0, last_item) as i:
                item(i, True)
            item(last_item, False)
            dve.wait_ge(sem("x_summed"), KD)
            for k in range(KD):
                dve.wait_ge(sem("scattered"), last_item * KD + (KD + k + 1))
                gated_to_x(k, banks[6 + k % 2])
                dve.wait_ge(sem("x_summed"), KD + k + 1)
                dve.sem_inc(sem("scatter_read"), 1)
                dve.sem_inc(sem("y_final"), 1)
            for g, (t0, n) in enumerate(TB):
                take(dve, ("y", g, 1))
                v.tensor_copy(y_tok[0:n, g, 512:1024], ps(("y", g, 1))[0:n, :]).then_inc(sem("y_right_ready"), 1)

        @block.gpsimd
        def _(pool):
            for l in range(DEPTH):
                if l:
                    take(pool, ("cache", l - 1, 2))
                    pool.wait_ge(sem("state_new"), l)
                    take(pool, ("o", l - 1, 3))
                for k, src in ((0, cache_in[0][l]), (256, cache_in[1][l]), (320, cache_in[1][l])):
                    n = 256 if k == 0 else ROPE
                    pool.dma_start(cache_tok[:, :, k:k + n], src.rearrange("(b p) n -> p b n", p=128)
                                   ).then_inc(sem("cache_loaded"), 16)
                pool.dma_start(s_smp[:, :].rearrange("p (h n) -> p h n", h=HEADS),
                               state_in[l].rearrange("h k v -> k h v")).then_inc(sem("state_loaded"), 16)
                pool.wait_ge(sem("state_ready"), 8 * (l + 1))
                pool.dma_start(s_out[0][l].rearrange("h k v -> k h v"),
                               states[:, 0].rearrange("p (h n) -> p h n", h=HEADS)).then_inc(sem("state_out"), 16)
                pool.wait_ge(sem("state_new"), l + 1)
                pool.dma_start(s_out[1][l].rearrange("h k v -> k h v"),
                               s_new[:, :].rearrange("p (h n) -> p h n", h=HEADS)).then_inc(sem("state_out"), 16)
                for g, (t0, n) in enumerate(TB):
                    pool.wait_ge(sem("kv_tok_ready"), 3 * l + g + 1)
                    src = kv_tok[0:n, (3 * l + g) % 2]
                    out, r0 = (kv_out[0], t0) if g < 2 else (kv_out[1], 0)
                    pool.dma_start(out[0][l][r0:r0 + n, :], src[:, 0:KVL]).then_inc(sem("rows_out%d" % ((l + g) % 2)), 16)
                    pool.dma_start(out[1][l][r0:r0 + n, :], src[:, KVL:KVL + ROPE]).then_inc(sem("rows_out%d" % ((l + g) % 2)), 16)
            pool.wait_ge(sem("h2_ready"), DEPTH)
            pool.dma_start(router, w_router).then_inc(sem("router_loaded"), 16)
            for g, (t0, n) in enumerate(TB):
                pool.wait_ge(sem("y_left_ready"), g + 1)
                pool.wait_ge(sem("y_right_ready"), g + 1)
                out, r0 = (y_out[0], t0) if g < 2 else (y_out[1], 0)
                pool.dma_start(out[r0:r0 + n, :], y_tok[0:n, g]).then_inc(sem("y_stored"), 16)
            pool.wait_ge(sem("y_stored"), 48)
            pool.wait_ge(sem("state_out"), 32 * DEPTH)
            pool.wait_ge(sem("rows_out0"), 96)
            pool.wait_ge(sem("rows_out1"), 96)


def kernel(**x):
    import concourse.bacc as bacc
    from concourse.bass_utils import run_bass_kernel_spmd as run

    def slabs(w, per):
        *lead, k, n = w.shape
        w = w.reshape(*lead, k // 128, 128, n // (128 * per), per, 128)
        a = len(lead)
        return w.transpose(*range(a), a + 2, a + 1, a + 3, a, a + 4).reshape(*lead, n // (128 * per), 128, -1)

    def col(v):
        return v.reshape(v.shape[0], -1, 128).transpose(0, 2, 1)

    x = {k: np.asarray(v) for k, v in x.items()}
    w = x["w_in"]
    H = 512
    kpe = w[:, :, 4 * H + QL + KVL:]
    win = np.concatenate([w[:, :, H:2 * H], w[:, :, 0:H], w[:, :, 3 * H:4 * H], w[:, :, 2 * H:3 * H],
                          w[:, :, 4 * H + QL:4 * H + QL + KVL], kpe, kpe, w[:, :, 4 * H:4 * H + QL]], axis=2)
    q = x["mla_wqb"].reshape(DEPTH, QL, HEADS, 128 + ROPE)
    wqb = np.concatenate([q[..., :128].reshape(DEPTH, QL, -1), q[..., 128:].reshape(DEPTH, QL, -1)], axis=2)
    kv = x["mla_wkvb"].reshape(DEPTH, KVL, HEADS, 256)
    wkvb = np.concatenate([kv[..., :128].reshape(DEPTH, KVL, -1), kv[..., 128:].reshape(DEPTH, KVL, -1)], axis=2)
    g, u = (x[n][0].reshape(KD, 128, NF, 128).transpose(2, 1, 0, 3).reshape(NF, 128, D) for n in ("ffn_w_gate", "ffn_w_up"))
    wup = np.concatenate([g, u], axis=2)
    gu = np.stack([x[n][0].reshape(NX, KD, 128, NFX, 128).transpose(0, 3, 2, 1, 4) for n in ("moe_w_gate", "moe_w_up")],
                  axis=4).reshape(NX * NFX, 128, 2 * D)
    wmoe = np.concatenate([gu, x["moe_w_down"][0].reshape(NX * NFX, 128, D)], axis=2)
    two = lambda v: np.concatenate([v, v], axis=1)
    vecs = np.concatenate([col(x["ada_b"]), col(x["norm1_w"]), col(x["norm2_w"]), col(x["hg_onorm_w"]),
                           col(x["mla_qa_norm_w"]), col(x["mla_kva_norm_w"]), col(x["mla_qn_nope_w"]),
                           col(two(x["mla_qn_rope_w"])), col(x["mla_kn_nope_w"]), col(two(x["mla_kn_rope_w"])),
                           col(x["mla_onorm_w"]), col(x["hg_lower_bounds"])], axis=2)
    vecs = vecs.transpose(1, 0, 2).reshape(128, -1)
    cond = np.stack([x["c_prompt"][0], x["c_sample"][0]], axis=1).reshape(KD, 128, 2).transpose(1, 0, 2).reshape(128, -1)
    arrays = {
        "consts": constants(), "vecs": vecs, "cond": cond,
        "x_in": np.concatenate([x["x_prompt"][0], x["x_sample"][0]], axis=0),
        "state_in": x["state_hgrn"][:, 0], "cache_ckv_in": x["cache_ckv"][:, 0], "cache_kpe_in": x["cache_kpe"][:, 0],
        "w_ada": x["ada_w"].reshape(DEPTH, KD, 128, 16, 384).transpose(0, 3, 2, 1, 4).reshape(DEPTH * ADA, 128, -1), "w_win": slabs(win, 2),
        "w_wqb": wqb.reshape(DEPTH, 3, 128, -1).transpose(0, 2, 1, 3).reshape(DEPTH, 1, 128, -1),
        "w_wkvb": wkvb.reshape(DEPTH, 2, 128, -1).transpose(0, 2, 1, 3).reshape(DEPTH, 1, 128, -1),
        "w_wo": slabs(x["w_o"], 2), "w_up": wup, "w_down": slabs(x["ffn_w_down"][0], 1),
        "w_router": x["moe_router"][0].reshape(KD, 128, NX).transpose(1, 0, 2), "w_moe": wmoe,
    }
    arrays = {k: np.ascontiguousarray(v) for k, v in arrays.items()}
    nc = bacc.Bacc("TRN2", target_bir_lowering=False, num_devices=1)
    a = {k: nc.dram_tensor(k, v.shape, F32, kind="ExternalInput").ap() for k, v in arrays.items()}
    outs = {"y_prompt": (SEQ, D), "y_sample": (DEC, D), "s_prompt": (DEPTH, HEADS, 128, 128),
            "ckv_prompt": (DEPTH, SEQ, KVL), "kpe_prompt": (DEPTH, SEQ, ROPE),
            "s_sample": (DEPTH, HEADS, 128, 128), "ckv_sample": (DEPTH, DEC, KVL), "kpe_sample": (DEPTH, DEC, ROPE)}
    o = {k: nc.dram_tensor(k, s, F32, kind="ExternalOutput").ap() for k, s in outs.items()}
    build(nc, a["consts"], a["vecs"], a["cond"], a["x_in"], a["state_in"], (a["cache_ckv_in"], a["cache_kpe_in"]),
          a["w_ada"], a["w_win"], a["w_wqb"], a["w_wkvb"], a["w_wo"], a["w_up"], a["w_down"], a["w_router"], a["w_moe"],
          (o["y_prompt"], o["y_sample"]), (o["s_prompt"], o["s_sample"]),
          ((o["ckv_prompt"], o["kpe_prompt"]), (o["ckv_sample"], o["kpe_sample"])))
    r = run(nc, [arrays], core_ids=[0]).results[0]
    y_p, y_s = r["y_prompt"][None], r["y_sample"][None]
    return (y_p, y_s, r["s_prompt"][:, None], r["ckv_prompt"][:, None], r["kpe_prompt"][:, None],
            r["s_sample"][:, None], r["ckv_sample"][:, None], r["kpe_sample"][:, None])
```
